# Optimizing a Trainium2 kernel written in Bass

```python
import math
import jax, jax.numpy as jnp
from jax import lax
import numpy as np

D_MODEL = 1024
BATCH = 1
SEQ = 256
DEPTH = 1

CHUNK = 64
N_META = 16
SB_BLOCK = 128
HEAD_DIM = 64
SB_HEADS = D_MODEL // 128
RW_HEADS = D_MODEL // 128
C_SB = SB_HEADS * HEAD_DIM
C_RW = RW_HEADS * HEAD_DIM
W_LORA = 64
A_LORA = 64
V_LORA = 32
G_LORA = 160
RW_COLS = 3 * C_RW + W_LORA + A_LORA + G_LORA
IN_COLS = 3 * C_SB + RW_COLS + 2 * D_MODEL
FFN_HIDDEN = ((8 * D_MODEL // 3 + 255) // 256) * 256
RMS_EPS = 1e-6
GN_EPS = 64e-5


def rms_norm(x, g):
    xf = x.astype(jnp.float32)
    y = xf * lax.rsqrt(jnp.mean(xf * xf, axis=-1, keepdims=True) + RMS_EPS)
    return (y * g.astype(jnp.float32)).astype(x.dtype)

def split_heads(t, n_heads):
    b, l, _ = t.shape
    return t.reshape(b, l, n_heads, HEAD_DIM)

def token_shift(p, mu):
    prev = jnp.pad(p, ((0, 0), (1, 0), (0, 0)))[:, :-1]
    return p + (prev - p) * mu

def stick_breaking_attention(q, k, v):
    b, l, h, dh = q.shape
    n_blocks = l // SB_BLOCK
    q_blocks = q.reshape(b, n_blocks, SB_BLOCK, h, dh).transpose(1, 0, 2, 3, 4)
    k_pos = jnp.arange(l)
    scale = dh ** -0.5

    def one_block(args):
        i, q_blk = args
        z = jnp.einsum("bqhd,bkhd->bhqk", q_blk, k).astype(jnp.float32) * scale
        q_pos = i * SB_BLOCK + jnp.arange(SB_BLOCK)
        mask = k_pos[None, :] < q_pos[:, None]
        neg_log_one_minus_beta = jnp.where(mask, jax.nn.softplus(z), 0.0)
        between = lax.cumsum(neg_log_one_minus_beta, axis=3, reverse=True) - neg_log_one_minus_beta
        log_a = jax.nn.log_sigmoid(z) - between
        a = jnp.where(mask, jnp.exp(log_a), 0.0)
        return jnp.einsum("bhqk,bkhd->bqhd", a.astype(v.dtype), v)

    out = lax.map(one_block, (jnp.arange(n_blocks), q_blocks))
    return out.transpose(1, 0, 2, 3, 4).reshape(b, l, h, dh)

def rwkv7_recurrence(r, decay, k, v, kk, a):
    b, l, h, n = r.shape
    f32 = jnp.float32

    def step(s, inp):
        r_t, w_t, k_t, v_t, kk_t, a_t = inp
        s_kk = jnp.einsum("bhvk,bhk->bhv", s, -kk_t)
        s = (s * w_t[:, :, None, :]
             + s_kk[..., None] * (kk_t * a_t)[:, :, None, :]
             + v_t[..., None] * k_t[:, :, None, :])
        y = jnp.einsum("bhvk,bhk->bhv", s, r_t)
        return s, y

    xs = tuple(jnp.moveaxis(t.astype(f32), 1, 0) for t in (r, decay, k, v, kk, a))
    s0 = jnp.zeros((b, h, n, n), f32)
    _, ys = lax.scan(step, s0, xs)
    return jnp.moveaxis(ys, 0, 1)

def group_norm_heads(y, w, b):
    mean = jnp.mean(y, axis=-1, keepdims=True)
    var = jnp.mean(jnp.square(y - mean), axis=-1, keepdims=True)
    yn = (y - mean) * lax.rsqrt(var + GN_EPS)
    bb, l, h, n = y.shape
    return yn.reshape(bb, l, h * n) * w.astype(jnp.float32) + b.astype(jnp.float32)

def first_inputs(seed: int = 0) -> dict:
    key = jax.random.key(seed)
    ks = jax.random.split(key, 32)
    f32 = jnp.float32
    n_vres = DEPTH - 1

    def nrm(k, shape, scale):
        return jax.random.normal(k, shape, f32) * scale

    def gain(k, shape):
        return 1.0 + 0.05 * jax.random.normal(k, shape, f32)

    return {
        "x": nrm(ks[0], (BATCH, SEQ, D_MODEL), 1.0),
        "meta_tokens": nrm(ks[1], (N_META, D_MODEL), 1.0),
        "norm_mix": gain(ks[2], (DEPTH, D_MODEL)),
        "norm_ffn": gain(ks[3], (DEPTH, D_MODEL)),
        "norm_final": gain(ks[4], (D_MODEL,)),
        "w_in": nrm(ks[5], (DEPTH, D_MODEL, IN_COLS), D_MODEL ** -0.5),
        "mu_rw": jax.random.uniform(ks[6], (DEPTH, RW_COLS), f32, 0.2, 0.8),
        "w0": jax.random.uniform(ks[7], (DEPTH, C_RW), f32, -6.5, -1.5),
        "w_up": nrm(ks[8], (DEPTH, W_LORA, C_RW), W_LORA ** -0.5),
        "a0": nrm(ks[9], (DEPTH, C_RW), 0.1),
        "a_up": nrm(ks[10], (DEPTH, A_LORA, C_RW), A_LORA ** -0.5),
        "g_up": nrm(ks[11], (DEPTH, G_LORA, C_RW), G_LORA ** -0.5),
        "k_k": 0.85 + 0.05 * jax.random.normal(ks[12], (DEPTH, C_RW), f32),
        "k_a": gain(ks[13], (DEPTH, C_RW)),
        "r_k": nrm(ks[14], (DEPTH, RW_HEADS, HEAD_DIM), 0.1),
        "ln_x_w": gain(ks[15], (DEPTH, C_RW)),
        "ln_x_b": nrm(ks[16], (DEPTH, C_RW), 0.02),
        "vres_down": nrm(ks[17], (n_vres, D_MODEL, V_LORA), D_MODEL ** -0.5),
        "vres_mu": jax.random.uniform(ks[18], (n_vres, V_LORA), f32, 0.2, 0.8),
        "vres_up": nrm(ks[19], (n_vres, V_LORA, C_RW), V_LORA ** -0.5),
        "vres0": gain(ks[20], (n_vres, C_RW)),
        "w_sb_out": nrm(ks[21], (DEPTH, C_SB, D_MODEL), C_SB ** -0.5),
        "w_rw_out": nrm(ks[22], (DEPTH, C_RW, D_MODEL), C_RW ** -0.5),
        "w_out": nrm(ks[23], (DEPTH, D_MODEL, D_MODEL), D_MODEL ** -0.5),
        "w_ffn_in": nrm(ks[24], (DEPTH, D_MODEL, 2 * FFN_HIDDEN), D_MODEL ** -0.5),
        "w_ffn_out": nrm(ks[25], (DEPTH, FFN_HIDDEN, D_MODEL), FFN_HIDDEN ** -0.5),
    }

def first_block(x, meta_tokens, norm_mix, norm_ffn, norm_final, w_in, mu_rw, w0, w_up, a0, a_up,
              g_up, k_k, k_a, r_k, ln_x_w, ln_x_b, vres_down, vres_mu, vres_up, vres0,
              w_sb_out, w_rw_out, w_out, w_ffn_in, w_ffn_out):
    b, s, d = x.shape
    l_real = N_META + s
    l_pad = -(-l_real // SB_BLOCK) * SB_BLOCK
    meta = jnp.broadcast_to(meta_tokens.astype(x.dtype)[None], (b, N_META, d))
    h = jnp.concatenate([meta, x], axis=1)
    h = jnp.pad(h, ((0, 0), (0, l_pad - l_real), (0, 0)))

    in_splits = [C_SB, 2 * C_SB, 3 * C_SB, 3 * C_SB + RW_COLS, 3 * C_SB + RW_COLS + D_MODEL]
    rw_splits = [C_RW, 2 * C_RW, 3 * C_RW, 3 * C_RW + W_LORA, 3 * C_RW + W_LORA + A_LORA]
    v_first = None
    for layer in range(DEPTH):
        xn = rms_norm(h, norm_mix[layer])
        proj = xn @ w_in[layer]
        q_sb, k_sb, v_sb, rw, gate_sb, gate_rw = jnp.split(proj, in_splits, axis=-1)

        y_sb = stick_breaking_attention(split_heads(q_sb, SB_HEADS), split_heads(k_sb, SB_HEADS),
                                        split_heads(v_sb, SB_HEADS)).reshape(b, l_pad, C_SB)

        rw = token_shift(rw, mu_rw[layer])
        r, kr, vr, w_lo, a_lo, g_lo = jnp.split(rw, rw_splits, axis=-1)
        w_log = -jax.nn.softplus(-(w0[layer] + jnp.tanh(w_lo) @ w_up[layer])) - 0.5
        decay = jnp.exp(-jnp.exp(w_log.astype(jnp.float32)))
        a = jax.nn.sigmoid(a0[layer] + a_lo @ a_up[layer])
        g = jax.nn.sigmoid(g_lo) @ g_up[layer]
        if layer == 0:
            v_first = vr
        else:
            v_lo = token_shift(xn @ vres_down[layer - 1], vres_mu[layer - 1])
            vr = vr + (v_first - vr) * jax.nn.sigmoid(vres0[layer - 1] + v_lo @ vres_up[layer - 1])
        kk = split_heads((kr * k_k[layer]).astype(jnp.float32), RW_HEADS)
        kk = kk / jnp.maximum(jnp.linalg.norm(kk, axis=-1, keepdims=True), 1e-12)
        kr = kr * (1.0 + (a - 1.0) * k_a[layer])
        r_h, k_h, v_h, a_h = (split_heads(t, RW_HEADS) for t in (r, kr, vr, a))
        y_rw = rwkv7_recurrence(r_h, split_heads(decay, RW_HEADS), k_h, v_h, kk, a_h)
        y_rw = group_norm_heads(y_rw, ln_x_w[layer], ln_x_b[layer])
        bonus = jnp.sum(r_h * k_h * r_k[layer], axis=-1, keepdims=True) * v_h
        y_rw = ((y_rw + bonus.reshape(b, l_pad, C_RW).astype(jnp.float32)).astype(h.dtype)) * g

        merged = (jax.nn.sigmoid(gate_sb) * (y_sb @ w_sb_out[layer])
                  + jax.nn.sigmoid(gate_rw) * (y_rw @ w_rw_out[layer]))
        h = h + merged @ w_out[layer]

        hn = rms_norm(h, norm_ffn[layer])
        gate_ffn, up_ffn = jnp.split(hn @ w_ffn_in[layer], [FFN_HIDDEN], axis=-1)
        h = h + (jax.nn.silu(gate_ffn) * up_ffn) @ w_ffn_out[layer]

    h = rms_norm(h, norm_final)
    return h[:, N_META:N_META + s]


GDN_HEADS = 4
GDN_DK = 128
GDN_DV = 128
HG_HEADS = 4
HG_DK = 128
HG_DV = 128
GDN_QK = GDN_HEADS * GDN_DK
GDN_V = GDN_HEADS * GDN_DV
HG_K = HG_HEADS * HG_DK
HG_V = HG_HEADS * HG_DV
D_MIX = GDN_V + HG_V
D_IN = 2 * GDN_QK + 2 * GDN_V + 2 * GDN_HEADS + 2 * HG_K + 2 * HG_V
CONV_K = 4
N_EXPERTS = 64
N_GROUPS = 8
TOPK_GROUPS = 4
TOP_K = 8
D_EXPERT = 256
D_SHARED = 256
ROUTE_SCALE = 2.5
MOE_BLOCK = 128
EPS = 1e-6


def rms_norm_2(x, w):
    xf = x.astype(jnp.float32)
    y = xf * lax.rsqrt(jnp.mean(xf * xf, axis=-1, keepdims=True) + EPS)
    return (y * w.astype(jnp.float32)).astype(x.dtype)

def l2_normalize(x):
    return x * lax.rsqrt(jnp.sum(x * x, axis=-1, keepdims=True) + EPS)

def causal_short_conv(x, w):
    T = x.shape[1]
    xp = jnp.pad(x, ((0, 0), (CONV_K - 1, 0), (0, 0)))
    y = sum(xp[:, j:j + T, :] * w[j] for j in range(CONV_K))
    return jax.nn.silu(y)

def to_chunks(t):
    B, T, H, D = t.shape
    return t.reshape(B, T // CHUNK, CHUNK, H, D).transpose(0, 3, 1, 2, 4)

def from_chunks(o):
    N, B, H, C, D = o.shape
    return o.transpose(1, 0, 3, 2, 4).reshape(B, N * C, H, D)

def gated_delta_chunked(q, k, v, g, beta):
    B, T, H, DK = q.shape
    DV = v.shape[-1]
    N = T // CHUNK
    qc, kc, vc = to_chunks(q), to_chunks(k), to_chunks(v)
    gc = jnp.cumsum(g.reshape(B, N, CHUNK, H).transpose(0, 3, 1, 2), axis=-1)
    bc = beta.reshape(B, N, CHUNK, H).transpose(0, 3, 1, 2)
    idx = jnp.arange(CHUNK)
    causal = idx[:, None] >= idx[None, :]
    strict = idx[:, None] > idx[None, :]
    decay = jnp.exp(jnp.where(causal, gc[..., :, None] - gc[..., None, :], -jnp.inf))
    kb = kc * bc[..., None]
    L = jnp.where(strict, jnp.einsum('bhncd,bhnsd->bhncs', kb, kc) * decay, 0.0)
    rhs = jnp.concatenate([vc * bc[..., None], kb * jnp.exp(gc)[..., None]], axis=-1)
    sol = lax.linalg.triangular_solve(L + jnp.eye(CHUNK, dtype=L.dtype), rhs,
                                      left_side=True, lower=True, unit_diagonal=True)
    u, w = sol[..., :DV], sol[..., DV:]
    attn = jnp.einsum('bhncd,bhnsd->bhncs', qc, kc) * decay
    q_dec = qc * jnp.exp(gc)[..., None]
    g_last = gc[..., -1]
    k_tail = kc * jnp.exp(g_last[..., None] - gc)[..., None]

    def step(S, xs):
        u_n, w_n, a_n, qd_n, kt_n, gl_n = xs
        v_new = u_n - jnp.einsum('bhcd,bhdv->bhcv', w_n, S)
        o = jnp.einsum('bhcd,bhdv->bhcv', qd_n, S) + jnp.einsum('bhcs,bhsv->bhcv', a_n, v_new)
        S = S * jnp.exp(gl_n)[..., None, None] + jnp.einsum('bhcd,bhcv->bhdv', kt_n, v_new)
        return S, o

    xs = tuple(jnp.moveaxis(t, 2, 0) for t in (u, w, attn, q_dec, k_tail, g_last))
    S0 = jnp.zeros((B, H, DK, DV), q.dtype)
    _, o = lax.scan(step, S0, xs)
    return from_chunks(o)

def hgrn2_chunked(q, k, v, logf):
    B, T, H, DK = q.shape
    DV = v.shape[-1]
    qc, kc, vc = to_chunks(q), to_chunks(k), to_chunks(v)
    bc = jnp.cumsum(to_chunks(logf), axis=3)
    idx = jnp.arange(CHUNK)
    causal = (idx[:, None] >= idx[None, :])[:, :, None]

    def step(S, xs):
        q_n, k_n, v_n, b_n = xs
        decay = jnp.exp(jnp.where(causal, b_n[..., :, None, :] - b_n[..., None, :, :], -jnp.inf))
        A = jnp.einsum('bhtd,bhsd,bhtsd->bhts', q_n, k_n, decay)
        b_last = b_n[..., -1:, :]
        o = jnp.einsum('bhts,bhsv->bhtv', A, v_n) + jnp.einsum('bhtd,bhdv->bhtv', q_n * jnp.exp(b_n), S)
        S = jnp.exp(b_last[..., 0, :])[..., :, None] * S + jnp.einsum('bhsd,bhsv->bhdv', k_n * jnp.exp(b_last - b_n), v_n)
        return S, o

    xs = tuple(jnp.moveaxis(t, 2, 0) for t in (qc, kc, vc, bc))
    S0 = jnp.zeros((B, H, DK, DV), q.dtype)
    _, o = lax.scan(step, S0, xs)
    return from_chunks(o)

def token_mixer(h, w_in, conv_w, a_log, dt_bias, gdn_norm_w, lb, hg_norm_w, w_out):
    B, T, _ = h.shape
    f32 = jnp.float32
    proj = jnp.einsum('btd,de->bte', h, w_in).astype(f32)
    qkv_w = 2 * GDN_QK + GDN_V
    qkv = causal_short_conv(proj[..., :qkv_w], conv_w.astype(f32))
    qA, kA, vA = jnp.split(qkv, [GDN_QK, 2 * GDN_QK], axis=-1)
    sizes = (GDN_V, GDN_HEADS, GDN_HEADS, HG_K, HG_V, HG_K, HG_V)
    cuts = np.cumsum(sizes)[:-1].tolist()
    gateA, beta_raw, a_raw, f_raw, iB, qB, gateB = jnp.split(proj[..., qkv_w:], cuts, axis=-1)

    qA = l2_normalize(qA.reshape(B, T, GDN_HEADS, GDN_DK)) * (GDN_DK ** -0.5)
    kA = l2_normalize(kA.reshape(B, T, GDN_HEADS, GDN_DK))
    vA = vA.reshape(B, T, GDN_HEADS, GDN_DV)
    beta = jax.nn.sigmoid(beta_raw)
    g_log = -jnp.exp(a_log.astype(f32)) * jax.nn.softplus(a_raw + dt_bias.astype(f32))
    oA = gated_delta_chunked(qA, kA, vA, g_log, beta)
    oA = rms_norm_2(oA, gdn_norm_w) * jax.nn.silu(gateA.reshape(B, T, GDN_HEADS, GDN_DV))
    oA = oA.reshape(B, T, GDN_V)

    lb = lb.reshape(HG_HEADS, HG_DK)
    f_raw = f_raw.reshape(B, T, HG_HEADS, HG_DK)
    logf = jnp.log(lb + (1.0 - lb) * jax.nn.sigmoid(f_raw))
    kB = (1.0 - lb) * jax.nn.sigmoid(-f_raw)
    qB = jax.nn.silu(qB.reshape(B, T, HG_HEADS, HG_DK))
    oB = hgrn2_chunked(qB, kB, iB.reshape(B, T, HG_HEADS, HG_DV), logf).reshape(B, T, HG_V)
    oB = rms_norm_2(oB, hg_norm_w) * jax.nn.silu(gateB)

    o = jnp.concatenate([oA, oB], axis=-1).astype(h.dtype)
    return jnp.einsum('bte,ed->btd', o, w_out)

def moe(h, w_router, router_bias, w_gate, w_up, w_down, ws_gate, ws_up, ws_down):
    B, T, D = h.shape
    xt = h.reshape(-1, D)
    M = xt.shape[0]
    scores = jax.nn.sigmoid(xt.astype(jnp.float32) @ w_router.astype(jnp.float32))
    sel = scores + router_bias.astype(jnp.float32)
    group_score = lax.top_k(sel.reshape(M, N_GROUPS, N_EXPERTS // N_GROUPS), 2)[0].sum(-1)
    _, gidx = lax.top_k(group_score, TOPK_GROUPS)
    gmask = jax.nn.one_hot(gidx, N_GROUPS, dtype=jnp.float32).sum(-2) > 0
    emask = jnp.repeat(gmask, N_EXPERTS // N_GROUPS, axis=-1)
    _, eidx = lax.top_k(jnp.where(emask, sel, -jnp.inf), TOP_K)
    wts = jnp.take_along_axis(scores, eidx, axis=-1)
    wts = wts / jnp.sum(wts, axis=-1, keepdims=True) * ROUTE_SCALE
    gates = jnp.einsum('mk,mke->me', wts, jax.nn.one_hot(eidx, N_EXPERTS, dtype=wts.dtype)).astype(h.dtype)

    def expert_block(args):
        x_b, g_b = args
        hg = jnp.einsum('td,edf->tef', x_b, w_gate)
        hu = jnp.einsum('td,edf->tef', x_b, w_up)
        return jnp.einsum('tef,efd->td', jax.nn.silu(hg) * hu * g_b[..., None], w_down)

    routed = lax.map(expert_block, (xt.reshape(-1, MOE_BLOCK, D), gates.reshape(-1, MOE_BLOCK, N_EXPERTS)))
    shared = (jax.nn.silu(xt @ ws_gate) * (xt @ ws_up)) @ ws_down
    return (routed.reshape(M, D) + shared).reshape(B, T, D)

def second_inputs(seed: int = 0) -> dict:
    key = jax.random.key(seed)
    ks = jax.random.split(key, 24)
    f32 = jnp.float32
    nrm = lambda k, s, sc: jax.random.normal(k, s, f32) * sc
    dt = jnp.exp(jax.random.uniform(ks[8], (DEPTH, GDN_HEADS), f32, np.log(1e-3), np.log(1e-1)))
    return {
        "x": nrm(ks[0], (BATCH, SEQ, D_MODEL), 1.0),
        "c": nrm(ks[1], (BATCH, D_MODEL), 1.0),
        "w_ada": nrm(ks[2], (DEPTH, D_MODEL, 6 * D_MODEL), 0.5 * D_MODEL ** -0.5),
        "b_ada": nrm(ks[3], (DEPTH, 6 * D_MODEL), 0.01),
        "norm1_w": 1.0 + nrm(ks[4], (DEPTH, D_MODEL), 0.02),
        "w_in": nrm(ks[5], (DEPTH, D_MODEL, D_IN), D_MODEL ** -0.5),
        "conv_w": nrm(ks[6], (DEPTH, CONV_K, 2 * GDN_QK + GDN_V), CONV_K ** -0.5),
        "gdn_a_log": jnp.log(jax.random.uniform(ks[7], (DEPTH, GDN_HEADS), f32, 1.0, 16.0)),
        "gdn_dt_bias": dt + jnp.log(-jnp.expm1(-dt)),
        "gdn_norm_w": 1.0 + nrm(ks[9], (DEPTH, GDN_DV), 0.02),
        "hg_lb": nrm(ks[10], (DEPTH + 1, HG_K), 0.1),
        "hg_norm_w": 1.0 + nrm(ks[11], (DEPTH, HG_V), 0.02),
        "w_out": nrm(ks[12], (DEPTH, D_MIX, D_MODEL), D_MIX ** -0.5),
        "norm2_w": 1.0 + nrm(ks[13], (DEPTH, D_MODEL), 0.02),
        "w_router": nrm(ks[14], (DEPTH, D_MODEL, N_EXPERTS), D_MODEL ** -0.5),
        "router_bias": nrm(ks[15], (DEPTH, N_EXPERTS), 0.01),
        "w_gate": nrm(ks[16], (DEPTH, N_EXPERTS, D_MODEL, D_EXPERT), D_MODEL ** -0.5),
        "w_up": nrm(ks[17], (DEPTH, N_EXPERTS, D_MODEL, D_EXPERT), D_MODEL ** -0.5),
        "w_down": nrm(ks[18], (DEPTH, N_EXPERTS, D_EXPERT, D_MODEL), D_EXPERT ** -0.5),
        "ws_gate": nrm(ks[19], (DEPTH, D_MODEL, D_SHARED), D_MODEL ** -0.5),
        "ws_up": nrm(ks[20], (DEPTH, D_MODEL, D_SHARED), D_MODEL ** -0.5),
        "ws_down": nrm(ks[21], (DEPTH, D_SHARED, D_MODEL), D_SHARED ** -0.5),
        "final_norm_w": 1.0 + nrm(ks[22], (D_MODEL,), 0.02),
    }

def second_block(x, c, w_ada, b_ada, norm1_w, w_in, conv_w, gdn_a_log, gdn_dt_bias, gdn_norm_w,
              hg_lb, hg_norm_w, w_out, norm2_w, w_router, router_bias, w_gate, w_up, w_down,
              ws_gate, ws_up, ws_down, final_norm_w):
    lb_all = jnp.cumsum(jax.nn.softmax(hg_lb.astype(jnp.float32), axis=0), axis=0)
    c_act = jax.nn.silu(c)
    for l in range(DEPTH):
        mod = jnp.einsum('bd,de->be', c_act, w_ada[l]) + b_ada[l]
        sh1, sc1, g1, sh2, sc2, g2 = jnp.split(mod, 6, axis=-1)
        h = rms_norm_2(x, norm1_w[l]) * (1.0 + sc1[:, None]) + sh1[:, None]
        x = x + g1[:, None] * token_mixer(h, w_in[l], conv_w[l], gdn_a_log[l], gdn_dt_bias[l],
                                          gdn_norm_w[l], lb_all[l], hg_norm_w[l], w_out[l])
        h = rms_norm_2(x, norm2_w[l]) * (1.0 + sc2[:, None]) + sh2[:, None]
        x = x + g2[:, None] * moe(h, w_router[l], router_bias[l], w_gate[l], w_up[l], w_down[l],
                                  ws_gate[l], ws_up[l], ws_down[l])
    return rms_norm_2(x, final_norm_w)


def setup_inputs(seed=0):
    out = dict(first_inputs(seed))
    for name, value in second_inputs(seed + 1).items():
        if name != "x":
            out[name + "_2"] = value
    return out


def reference(
    x, meta_tokens, norm_mix, norm_ffn, norm_final, w_in, mu_rw, w0, w_up, a0, a_up, g_up, k_k,
    k_a, r_k, ln_x_w, ln_x_b, vres_down, vres_mu, vres_up, vres0, w_sb_out, w_rw_out, w_out,
    w_ffn_in, w_ffn_out, c_2, w_ada_2, b_ada_2, norm1_w_2, w_in_2, conv_w_2, gdn_a_log_2,
    gdn_dt_bias_2, gdn_norm_w_2, hg_lb_2, hg_norm_w_2, w_out_2, norm2_w_2, w_router_2,
    router_bias_2, w_gate_2, w_up_2, w_down_2, ws_gate_2, ws_up_2, ws_down_2, final_norm_w_2,
):
    x = first_block(
        x, meta_tokens, norm_mix, norm_ffn, norm_final, w_in, mu_rw, w0, w_up, a0, a_up, g_up,
        k_k, k_a, r_k, ln_x_w, ln_x_b, vres_down, vres_mu, vres_up, vres0, w_sb_out, w_rw_out,
        w_out, w_ffn_in, w_ffn_out,
    )
    return second_block(
        x, c_2, w_ada_2, b_ada_2, norm1_w_2, w_in_2, conv_w_2, gdn_a_log_2, gdn_dt_bias_2,
        gdn_norm_w_2, hg_lb_2, hg_norm_w_2, w_out_2, norm2_w_2, w_router_2, router_bias_2,
        w_gate_2, w_up_2, w_down_2, ws_gate_2, ws_up_2, ws_down_2, final_norm_w_2,
    )


_drawn_inputs = setup_inputs


def setup_inputs(seed=0):
    import zlib

    import numpy as np

    out = dict(_drawn_inputs(seed))
    spreads = {}
    factors = {'ln_x_b': 2.996,
     'norm1_w_2': 4.291,
     'gdn_norm_w_2': 24.953,
     'hg_lb_2': 6.467,
     'hg_norm_w_2': 20.785,
     'final_norm_w_2': 8.74,
     'w_up': 2.712,
     'a0': 3.073,
     'norm2_w_2': 8.0,
     'router_bias_2': 6.68}
    for name, (base, spread) in spreads.items():
        noise = np.random.default_rng([zlib.crc32(name.encode()), seed]).standard_normal(out[name].shape)
        drawn = base * np.exp(spread * noise) if base else spread * noise
        out[name] = __import__('jax').numpy.asarray(drawn.astype(out[name].dtype))
    for name, factor in factors.items():
        out[name] = (out[name] * factor).astype(out[name].dtype)
    return out
```

```python
import numpy as np

import concourse.bass as bass
from concourse import mybir
from contextlib import ExitStack

F32 = mybir.dt.float32
ALU = mybir.AluOpType
ACT = mybir.ActivationFunctionType
AX = mybir.AxisListType

P = 128
D = 1024
KD = D // P
N_META, SEQ = 16, 256
T1 = N_META + SEQ
T1P = 320
HEADS, DH = 8, 64
C = HEADS * DH
CT = C // P
CH = 64
NCH = T1P // CH
NM = NCH * HEADS
FFN = 2816
FT = FFN // P
T2 = SEQ
GH = 4
NE, FE = 64, 256
SLOT = 4096
RING = 3
EXPERT = 6144
ERING = 4
CONSTS = 5200

RMS_EPS = 1e-6
GN_EPS = 64e-5
NEG = -1e30


class Signal:

    def __init__(self, nc, ctx, name):
        self.sem = ctx.enter_context(nc.semaphore(name))
        self.value = 0

    def on(self, instruction, by=1):
        instruction.then_inc(self.sem, by)
        self.value += by
        return self.value


class Memory:

    def __init__(self, tensor, at, end):
        self.tensor, self.at, self.end = tensor, at, end

    def take(self, *shape):
        n = int(np.prod(shape))
        view = self.view(self.at, *shape)
        self.at += n
        assert self.at <= self.end, (self.at, self.end)
        return view

    def view(self, at, *shape):
        n = int(np.prod(shape))
        flat = self.tensor[:, at:at + n]
        if len(shape) == 1:
            return flat
        names = "abcd"[:len(shape)]
        spec = "p (" + " ".join(names) + ") -> p " + " ".join(names)
        return flat.rearrange(spec, **{k: v for k, v in zip(names, shape)})


def param_rows(groups):
    table, row = {}, 0
    for name, size in groups:
        n = -(-size // P)
        table[name] = (row, size)
        row += n
    assert row <= P
    return table


ROWS0 = param_rows([("norm_mix", D), ("norm_ffn", D), ("norm_final", D), ("mu_rw", 3 * C + 288), ("w0", C),
                    ("a0", C), ("k_k", C), ("k_a", C), ("r_k", C), ("ln_x_w", C), ("ln_x_b", C), ("c_2", D),
                    ("gdn_norm_w_2", P), ("hg_lb_2", 2 * C), ("hg_norm_w_2", C), ("norm1_w_2", D),
                    ("norm2_w_2", D), ("final_norm_w_2", D)])
ROWS1 = param_rows([("conv_w_2", 4 * 3 * C), ("b_ada_2", 6 * D)])


def build(nc, a, out):
    ctx = ExitStack()
    with ctx:
        total = 48 * 1024
        sbuf = ctx.enter_context(nc.sbuf_tensor("sbuf", [P, total], F32))
        bank = [ctx.enter_context(nc.psum_tensor(f"bank{i}", [P, 512], F32)) for i in range(8)]
        gates_dram = nc.dram_tensor("gates_scratch", [NE, T2], F32, kind="Internal").ap()

        ring_at = 0
        mem = Memory(sbuf, total - CONSTS, total)
        view = mem.view

        ident = mem.take(P)
        ones = mem.take(P)
        blk64 = mem.take(P)
        tri = mem.take(P)
        ATT = T1 + (T1 - P) + (T1 - 2 * P)
        keep = mem.take(ATT)
        drop = mem.take(ATT)
        rw_mask = mem.take(P)
        upper = [mem.take(P) for _ in range(7)]
        lower = [mem.take(P) for _ in range(7)]
        upper_strict, upper_incl = mem.take(P), mem.take(P)
        reset64 = mem.take(T1P)
        reset128 = mem.take(T2)
        eps_rms, eps_gn, one_col = mem.take(1), mem.take(1), mem.take(1)
        vec0, vec1 = mem.take(P), mem.take(P)
        row_sel = mem.take(GH, P)
        small = mem.take(256)
        base = RING * SLOT

        def param(name, i=0):
            if name in ROWS0:
                r = ROWS0[name][0] + i
                return vec0[:, r:r + 1]
            r = ROWS1[name][0] + i
            return vec1[:, r:r + 1]

        pe_s = Signal(nc, ctx, "tensor_done")
        act_s = Signal(nc, ctx, "scalar_done")
        dve_s = Signal(nc, ctx, "vector_done")
        pool_s = Signal(nc, ctx, "gpsimd_done")
        small_in = Signal(nc, ctx, "small_loads")
        tokens_in = Signal(nc, ctx, "token_loads")
        stored = Signal(nc, ctx, "stored")
        slot_ready = [Signal(nc, ctx, f"slot_ready{i}") for i in range(RING)]
        V, S, G, T = nc.vector, nc.scalar, nc.gpsimd, nc.tensor

        def columns(w, a0, a1):
            return [(w[:, a0:a1].rearrange("(k p) c -> p k c", p=P), 0, a1 - a0)]

        plan = []
        w_in, w_in2 = a["w_in"][0], a["w_in_2"][0]
        edges = [0, 512, 1024, 1536, 2048, 2560, 3072, 3360, 3872, 4384, 4896, 5408]
        for c0, c1 in zip(edges, edges[1:]):
            plan.append((KD, c1 - c0, columns(w_in, c0, c1)))
        SB_OUT = len(plan)
        plan.append((CT, D, columns(a["w_sb_out"][0], 0, D)))
        plan.append((CT, D, columns(a["w_rw_out"][0], 0, D)))
        W_OUT = len(plan)
        for n in range(2):
            plan.append((KD, 512, columns(a["w_out"][0], 512 * n, 512 * n + 512)))
        FFN_IN = len(plan)
        wf = a["w_ffn_in"][0]
        for n in range(FT // 2):
            plan.append((KD, 512, [(wf[:, s + 256 * n:s + 256 * n + 256].rearrange("(k p) c -> p k c", p=P), o, 256)
                                   for s, o in ((0, 0), (FFN, 256))]))
        FFN_OUT = len(plan)
        for n in range(0, FT, 4):
            rows = min(4, FT - n)
            plan.append((rows, D, [(a["w_ffn_out"][0][n * P:(n + rows) * P, :].rearrange("(k p) c -> p k c", p=P), 0, D)]))
        ADA = len(plan)
        for n in range(12):
            plan.append((KD, 512, columns(a["w_ada_2"][0], 512 * n, 512 * n + 512)))
        W_IN2 = len(plan)
        edges2 = [0, 512, 1024, 1536, 2048]
        for c0 in [0, 512, 1024, 1536, 2056, 2568, 3080, 3592]:
            plan.append((KD, 512, columns(w_in2, c0, c0 + 512)))
        W_OUT2 = len(plan)
        for n in range(2):
            plan.append((KD, 512, columns(a["w_out_2"][0], 512 * n, 512 * n + 512)))

        ready_at, counts = [], [0] * RING
        for n, (_, _, parts) in enumerate(plan):
            counts[n % RING] += 16 * len(parts)
            ready_at.append(counts[n % RING])
        slot_freed = {}
        issued = [0]

        def slot(n):
            rows, width, _ = plan[n]
            return view(ring_at + (n % RING) * SLOT, rows, width)

        def load_slots(sp, upto):
            while issued[0] < min(upto, len(plan)):
                n = issued[0]
                if n >= RING:
                    sp.wait_ge(pe_s.sem, slot_freed[n - RING])
                for src, c0, w in plan[n][2]:
                    slot_ready[n % RING].on(sp.dma_start(slot(n)[:, :, c0:c0 + w], src), 16)
                issued[0] += 1

        def await_slot(pe, n):
            pe.wait_ge(slot_ready[n % RING].sem, ready_at[n])

        tok = view(base, 3, D)
        rows0 = view(base + 3 * D, P)
        rows1 = view(base + 3 * D + P, P)
        top = total - CONSTS - KD * T1
        hT = view(top, KD, T1)
        wa_up = view(top - C, C)
        g_up0 = view(top - 2 * C, C)
        g_up1 = view(top - 3 * C, C)
        top -= 3 * C
        NT_TOK = [P, P, T1 - 2 * P]
        with nc.Block() as block:
            @block.vector
            def _(dve):
                cleared = dve_s.on(V.memset(rows0, 0.0))
                cleared = dve_s.on(V.memset(rows1, 0.0))
                tri0 = dve_s.on(V.memset(eps_rms, RMS_EPS))
                dve_s.on(V.memset(eps_gn, GN_EPS))
                dve_s.on(V.memset(one_col, 1.0))

            @block.sync
            def _(sp):
                sp.wait_ge(dve_s.sem, 2)
                for table, rows in ((ROWS0, rows0), (ROWS1, rows1)):
                    for name, (row, size) in table.items():
                        src = a[name]
                        names = "abcd"[:len(src.shape)]
                        flat = src.rearrange(" ".join(names) + " -> (" + " ".join(names) + ")") if len(names) > 1 else src
                        n = size // P
                        small_in.on(sp.dma_start(rows[row:row + n, :], flat[0:n * P].rearrange("(r c) -> r c", c=P)), 16)
                        if size % P:
                            small_in.on(sp.dma_start(rows[row + n:row + n + 1, 0:size % P],
                                                     flat[n * P:size].rearrange("(r c) -> r c", r=1)), 16)
                small_in.on(sp.dma_start(wa_up[0:64, :], a["w_up"][0]), 16)
                small_in.on(sp.dma_start(wa_up[64:128, :], a["a_up"][0]), 16)
                small_in.on(sp.dma_start(g_up0, a["g_up"][0][0:P, :]), 16)
                small_in.on(sp.dma_start(g_up1[0:32, :], a["g_up"][0][P:P + 32, :]), 16)
                wba = w_in2[:, 2048:2056].rearrange("(k p) c -> p k c", p=P)
                small_in.on(sp.dma_start(small[:, 0:64].rearrange("p (k c) -> p k c", c=8), wba), 16)
                small_in.on(sp.dma_start(small[0:GH, 64:65], a["gdn_a_log_2"].rearrange("a h -> h a")), 16)
                small_in.on(sp.dma_start(small[0:GH, 65:66], a["gdn_dt_bias_2"].rearrange("a h -> h a")), 16)
                small_in.on(sp.dma_start(small[:, 128:192], a["router_bias_2"].partition_broadcast(P).rearrange("p a e -> p (a e)")), 16)
                load_slots(sp, RING)

            @block.scalar
            def _(act):
                x = a["x"][0]
                tokens_in.on(act.dma_start(tok[0:N_META, 0, :], a["meta_tokens"]), 16)
                tokens_in.on(act.dma_start(tok[N_META:P, 0, :], x[0:P - N_META, :]), 16)
                tokens_in.on(act.dma_start(tok[:, 1, :], x[P - N_META:2 * P - N_META, :]), 16)
                tokens_in.on(act.dma_start(tok[0:T1 - 2 * P, 2, :], x[2 * P - N_META:SEQ, :]), 16)

            @block.gpsimd
            def _(pool):
                def step(instruction):
                    pool.wait_ge(pool_s.sem, pool_s.on(instruction))

                def fill(ap, value):
                    step(G.memset(ap, value))

                def select(ap, pattern, base_, cm, op, fill_=0.0):
                    step(G.affine_select(out=ap, in_=ap, compare_op=op, fill=fill_, base=base_,
                                         pattern=pattern, channel_multiplier=cm))
                fill(ident, 0.0)
                select(ident, [[-1, P]], 0, 1, ALU.not_equal, 1.0)
                fill(ones, 1.0)
                fill(blk64, 0.0)
                fill(blk64[0:64, 0:64], 1.0)
                fill(blk64[64:128, 64:128], 1.0)
                consts_ready = pool_s.value
                fill(tri, 1.0)
                select(tri, [[-1, P]], 0, 1, ALU.is_ge)
                fill(keep, 1.0)
                fill(drop, 0.0)
                at = 0
                for i in range(3):
                    n = T1 - i * P
                    select(keep[:, at:at + n], [[1, n]], 0, -1, ALU.is_gt)
                    select(drop[:, at:at + n], [[1, n]], 0, -1, ALU.is_gt, NEG)
                    at += n
                fill(rw_mask, 1.0)
                scratch = row_sel[:, 0, :]
                fill(scratch, 1.0)
                select(rw_mask[:, 0:64], [[1, 64]], 0, -1, ALU.is_gt)
                select(rw_mask[:, 64:128], [[1, 64]], 0, -1, ALU.is_ge)
                select(scratch[:, 0:64], [[1, 64]], 64, -1, ALU.is_gt)
                select(scratch[:, 64:128], [[1, 64]], 64, -1, ALU.is_ge)
                select(scratch, [[0, P]], -64, 1, ALU.is_ge)
                step(G.tensor_tensor(rw_mask, rw_mask, scratch, ALU.add))
                for n in range(7):
                    b = 1 << n
                    u = upper[n].rearrange("p (k c) -> p k c", c=2 * b)
                    fill(upper[n], 0.0)
                    fill(u[:, :, b:2 * b], 1.0)
                    select(u, [[-2 * b, P // (2 * b)], [0, 2 * b]], 0, 1, ALU.is_ge)
                    select(u, [[2 * b, P // (2 * b)], [0, 2 * b]], b - 1, -1, ALU.is_ge)
                    w = lower[n].rearrange("p (k c) -> p k c", c=2 * b)
                    fill(lower[n], 0.0)
                    fill(w[:, :, 0:b], 1.0)
                    select(w, [[-2 * b, P // (2 * b)], [0, 2 * b]], -b, 1, ALU.is_ge)
                    select(w, [[2 * b, P // (2 * b)], [0, 2 * b]], 2 * b - 1, -1, ALU.is_ge)
                fill(upper_strict, 1.0)
                select(upper_strict, [[1, P]], 0, -1, ALU.is_gt)
                fill(upper_incl, 1.0)
                select(upper_incl, [[1, P]], 0, -1, ALU.is_ge)
                fill(reset64, 1.0)
                fill(reset64.rearrange("p (k c) -> p k c", c=CH)[:, :, 0:1], 0.0)
                fill(reset128, 1.0)
                fill(reset128.rearrange("p (k c) -> p k c", c=P)[:, :, 0:1], 0.0)
                fill(row_sel, 0.0)
                select(row_sel, [[-1, GH], [0, P]], 0, 1, ALU.not_equal, 1.0)

            @block.tensor
            def _(pe):
                pe.wait_ge(pool_s.sem, 2)
                pe.wait_ge(tokens_in.sem, tokens_in.value)
                for j in range(KD):
                    for i, n in enumerate(NT_TOK):
                        t = T.transpose(bank[j][:, i * P:i * P + n], tok[0:n, i, j * P:j * P + P], ident[0:n, 0:n])
                    pe_s.on(t)
                pe.wait_ge(small_in.sem, small_in.value)
                pe.wait_ge(act_s.sem, 1)
                T.transpose(bank[0][:, 0:P], rows0, ident)
                pe_s.on(T.transpose(bank[0][:, P:2 * P], rows1, ident))

            @block.scalar
            def _(act):
                for j in range(0, KD, 2):
                    act.wait_ge(pe_s.sem, j + 1)
                    act_s.on(S.activation(hT[:, j, :], bank[j][:, 0:T1], ACT.Copy))

            @block.vector
            def _(dve):
                for j in range(1, KD, 2):
                    dve.wait_ge(pe_s.sem, j + 1)
                    dve_s.on(V.tensor_copy(hT[:, j, :], bank[j][:, 0:T1]))
                dve.wait_ge(pe_s.sem, KD + 1)
                dve_s.on(V.tensor_copy(vec0, bank[0][:, 0:P]))
                dve_s.on(V.tensor_copy(vec1, bank[0][:, P:2 * P]))

        def rms_norm(src, dst, gain, shift, n, square, rstd, width=KD, mean=1.0 / D):
            with nc.Block() as block:
                @block.vector
                def _(dve):
                    squared = dve_s.on(V.tensor_tensor(square, src, src, ALU.mult))

                @block.tensor
                def _(pe):
                    pe.wait_ge(dve_s.sem, dve_s.value)
                    for j in range(width):
                        m = T.matmul(bank[0][:, 0:n], ones, square[:, j, :], start=(j == 0), stop=(j == width - 1))
                    pe_s.on(m)

                @block.scalar
                def _(act):
                    act.wait_ge(pe_s.sem, pe_s.value)
                    act_s.on(S.activation(rstd, bank[0][:, 0:n], ACT.Sqrt, bias=eps_rms, scale=mean))

                @block.vector
                def _(dve):
                    dve.wait_ge(act_s.sem, act_s.value)
                    dve.wait_ge(dve_s.sem, dve_s.on(V.reciprocal(rstd, rstd)))
                    for j in range(width):
                        done = dve_s.on(V.scalar_tensor_tensor(out=dst[:, j, :], in0=src[:, j, :], scalar=gain(j),
                                                               in1=rstd, op0=ALU.mult, op1=ALU.mult))
                    if shift is not None:
                        dve.wait_ge(dve_s.sem, done)
                        for j in range(width):
                            dve_s.on(V.tensor_scalar(dst[:, j, :], dst[:, j, :], shift(j), None, ALU.add))

        def project(x, n, tiles, evacuate, first_slot, n_slots, owner=lambda m: ("act", "dve")[m % 2]):
            pe0 = pe_s.value
            emptied, value = [], {"act": act_s.value, "dve": dve_s.value}
            for m in range(len(tiles)):
                value[owner(m)] += 1
                emptied.append((act_s if owner(m) == "act" else dve_s, value[owner(m)]))
            with nc.Block() as block:
                @block.tensor
                def _(pe):
                    seen = None
                    for m, (s, c0, w) in enumerate(tiles):
                        if s != seen:
                            await_slot(pe, s)
                            seen = s
                        if m >= 8:
                            done, by = emptied[m - 8]
                            pe.wait_ge(done.sem, by)
                        weights = slot(s)
                        rows = plan[s][0]
                        for k in range(rows):
                            mm = T.matmul(bank[m % 8][0:w, 0:n], weights[:, k, c0:c0 + w], x[:, k, :],
                                          start=(k == 0), stop=(k == rows - 1))
                        slot_freed[s] = pe_s.on(mm)

                @block.sync
                def _(sp):
                    load_slots(sp, first_slot + n_slots + RING)

                @block.scalar
                def _(act):
                    for m in (m for m in range(len(tiles)) if owner(m) == "act"):
                        act.wait_ge(pe_s.sem, pe0 + m + 1)
                        act_s.on(evacuate(act, m, bank[m % 8][0:tiles[m][2], 0:n]))

                @block.vector
                def _(dve):
                    for m in (m for m in range(len(tiles)) if owner(m) == "dve"):
                        dve.wait_ge(pe_s.sem, pe0 + m + 1)
                        dve_s.on(evacuate(dve, m, bank[m % 8][0:tiles[m][2], 0:n]))

        def copy_out(dst):
            def evacuate(engine, m, psum):
                if engine is S:
                    return S.activation(dst(m), psum, ACT.Copy)
                return V.tensor_copy(dst(m), psum)
            return evacuate

        m1 = Memory(sbuf, base, top)
        xnT = m1.take(KD, T1)
        g_in = m1.take(2, T1)
        y_sb = m1.take(CT, T1)
        y_rw = m1.take(CT, T1)
        after_mixer = m1.at
        qT = m1.take(CT, T1)
        kT = m1.take(CT, 3 * P)
        vT = m1.take(CT, T1)
        raw = view(top - 15 * (1 + T1), 15, 1 + T1)
        att_at = m1.at
        rms_norm(hT, xnT, lambda j: param("norm_mix", j), None, T1, view(att_at, KD, T1), view(att_at + KD * T1, T1))

        tiles = [(m // 4, (m % 4) * P, P) for m in range(24)] + [(6, 0, P), (6, P, P), (6, 2 * P, 32)]

        def put_in(engine, m, psum):
            w = tiles[m][2]
            if m < 4:
                if engine is nc.scalar:
                    return S.activation(qT[:, m, :], psum, ACT.Copy, scale=DH ** -0.5)
                return V.tensor_scalar(qT[:, m, :], psum, DH ** -0.5, None, ALU.mult)
            dst = (kT[:, m - 4, 0:T1] if m < 8 else vT[:, m - 8, :] if m < 12
                   else raw[0:w, m - 12, 1:1 + T1])
            if engine is nc.scalar:
                return S.activation(dst, psum, ACT.Copy)
            return V.tensor_copy(dst, psum)

        with nc.Block() as block:
            @block.gpsimd
            def _(pool):
                for ap in (kT[:, :, T1:3 * P], raw[:, :, 0:1], raw[32:64, 14, :], raw[64:128, 14, :]):
                    pool.wait_ge(pool_s.sem, pool_s.on(G.memset(ap, 0.0)))
        project(xnT, T1, tiles, put_in, 0, 7)

        SEG = [(0, 0, T1), (T1, P, T1 - P), (2 * T1 - P, 2 * P, T1 - 2 * P)]
        ma = Memory(sbuf, att_at, top - 15 * (1 + T1))
        v_tok = ma.take(3, C)
        zs = [ma.take(ATT) for _ in range(2)]
        zm = [ma.take(ATT) for _ in range(2)]
        ab = [ma.take(ATT) for _ in range(2)]
        sp_ = [ma.take(ATT) for _ in range(2)]
        att = [ma.take(ATT) for _ in range(2)]
        with nc.Block() as block:
            @block.gpsimd
            def _(pool):
                pool_s.on(G.memset(v_tok[:, 2, :], 0.0))

            @block.tensor
            def _(pe):
                for i, n in enumerate(NT_TOK):
                    for j in range(CT):
                        t = T.transpose(bank[i][0:n, j * P:j * P + P], vT[:, j, i * P:i * P + n], ident)
                    pe_s.on(t)

            @block.vector
            def _(dve):
                dve.wait_ge(pool_s.sem, pool_s.value)
                for i, n in enumerate(NT_TOK):
                    dve.wait_ge(pe_s.sem, pe_s.value - 2 + i)
                    dve_s.on(V.tensor_copy(v_tok[0:n, i, :], bank[i][0:n, :]))

        s_z = Signal(nc, ctx, "scores_ready")
        s_zs = Signal(nc, ctx, "scores_copied")
        s_abs = Signal(nc, ctx, "abs_scores")
        s_exp = Signal(nc, ctx, "exp_abs")
        s_ln = Signal(nc, ctx, "log_term")
        s_sp = Signal(nc, ctx, "softplus_ready")
        s_c = Signal(nc, ctx, "suffix_sums")
        s_la = Signal(nc, ctx, "log_weights")
        s_att = Signal(nc, ctx, "weights_ready")
        s_y = Signal(nc, ctx, "head_out")
        s_zm = Signal(nc, ctx, "masked_scores")
        s_ycopy = Signal(nc, ctx, "head_out_copied")
        with nc.Block() as block:
            @block.tensor
            def _(pe):
                def scores(h):
                    b = h % 2
                    lo = DH * (h % 2)
                    if h >= 2:
                        pe.wait_ge(s_sp.sem, 2 * (h - 1))
                    for i, (c, q0, n) in enumerate(SEG):
                        m = T.matmul(bank[b][:, c:c + n], kT[lo:lo + DH, h // 2, i * P:i * P + P],
                                     qT[lo:lo + DH, h // 2, q0:q0 + n], start=True, stop=True)
                    s_z.on(m)

                def rest(h):
                    b = h % 2
                    lo = DH * (h % 2)
                    pe.wait_ge(s_sp.sem, 2 * h + 2)
                    if h >= 2:
                        pe.wait_ge(s_la.sem, h - 1)
                    for i in range(3):
                        c, q0, n = SEG[i]
                        T.matmul(bank[2 + b][:, c:c + n], tri, sp_[b][:, c:c + n], start=True, stop=(i == 2))
                        for i2 in range(i + 1, 3):
                            c2, q2, n2 = SEG[i2]
                            o = c + q2 - q0
                            m = T.matmul(bank[2 + b][:, o:o + n2], ones, sp_[b][:, c2:c2 + n2],
                                         start=False, stop=(i2 == 2))
                    s_c.on(T.matmul(bank[6][:, 0:1], ones, one_col, start=True, stop=True))

                def out_(h):
                    b = h % 2
                    lo = DH * (h % 2)
                    pe.wait_ge(s_att.sem, h + 1)
                    if h >= 2:
                        pe.wait_ge(s_ycopy.sem, h - 1)
                    for i, (c, q0, n) in enumerate(SEG):
                        m = T.matmul(bank[4 + b][lo:lo + DH, q0:T1], v_tok[:, i, h * DH:h * DH + DH],
                                     att[b][:, c:c + n], start=(i == 0), stop=(i == 2))
                    s_y.on(m)

                scores(0)
                for h in range(HEADS):
                    if h + 1 < HEADS:
                        scores(h + 1)
                    rest(h)
                    if h >= 1:
                        out_(h - 1)
                out_(HEADS - 1)

            @block.scalar
            def _(act):
                def first(h):
                    b = h % 2
                    act.wait_ge(s_z.sem, h + 1)
                    if h >= 2:
                        act.wait_ge(s_la.sem, h - 1)
                        act.wait_ge(s_sp.sem, 2 * (h - 1))
                    s_zs.on(S.activation(zs[b], bank[b][:, 0:ATT], ACT.Copy))
                    s_abs.on(S.activation(ab[b], bank[b][:, 0:ATT], ACT.Abs))
                    act.wait_ge(s_abs.sem, h + 1)
                    s_exp.on(S.activation(ab[b], ab[b], ACT.Exp, scale=-1.0))
                    act.wait_ge(s_exp.sem, h + 1)
                    s_ln.on(S.activation(ab[b], ab[b], ACT.Ln, bias=one_col))

                def second(h):
                    b = h % 2
                    act.wait_ge(s_la.sem, h + 1)
                    if h >= 2:
                        act.wait_ge(s_y.sem, h - 1)
                    s_att.on(S.activation(att[b], zm[b], ACT.Exp))

                first(0)
                for h in range(HEADS):
                    if h + 1 < HEADS:
                        first(h + 1)
                    second(h)

            @block.gpsimd
            def _(pool):
                for h in range(HEADS):
                    b = h % 2
                    pool.wait_ge(s_zs.sem, h + 1)
                    if h >= 2:
                        pool.wait_ge(s_att.sem, h - 1)
                    s_zm.on(G.tensor_tensor(zm[b], zs[b], drop, ALU.add))

            @block.vector
            def _(dve):
                def first(h):
                    b = h % 2
                    dve.wait_ge(s_ln.sem, h + 1)
                    if h >= 2:
                        dve.wait_ge(s_c.sem, h - 1)
                    s_sp.on(V.scalar_tensor_tensor(out=sp_[b], in0=bank[b][:, 0:ATT], scalar=0.0, in1=ab[b],
                                                   op0=ALU.max, op1=ALU.add))
                    dve.wait_ge(s_sp.sem, 2 * h + 1)
                    s_sp.on(V.tensor_tensor(sp_[b], sp_[b], keep, ALU.mult))

                def second(h):
                    b = h % 2
                    dve.wait_ge(s_c.sem, h + 1)
                    dve.wait_ge(s_zm.sem, h + 1)
                    s_la.on(V.tensor_tensor(zm[b], zm[b], bank[2 + b][:, 0:ATT], ALU.subtract))

                def third(h):
                    lo = DH * (h % 2)
                    dve.wait_ge(s_y.sem, h + 1)
                    s_ycopy.on(V.tensor_copy(y_sb[lo:lo + DH, h // 2, :], bank[4 + h % 2][lo:lo + DH, 0:T1]))

                first(0)
                for h in range(HEADS):
                    if h + 1 < HEADS:
                        first(h + 1)
                    second(h)
                    if h >= 1:
                        third(h - 1)
                third(HEADS - 1)
        A0 = after_mixer
        mr = Memory(sbuf, A0, top - 15 * (1 + T1))
        vS = mr.take(CT, CH + T1P)
        rk = mr.take(CT, T1)
        Q2 = mr.take(CT, NCH, 2, CH)
        at_K2 = mr.at
        K2 = mr.take(CT, NCH, 2, CH)
        at_K2tok = mr.at
        sh = mr.take(9, T1)
        c_sum = mr.take(CT, T1P)
        e_pos = mr.take(CT, T1P)
        e_neg = mr.take(CT, T1P)
        rate = mr.take(CT, T1)
        kk = mr.take(CT, T1)
        work = mr.take(CT, T1)
        ld = view(top - 15 * (1 + T1), CT, T1P)
        grow = view(top - 15 * (1 + T1) + CT * T1P, CT, T1)
        chunks = lambda ap, n: ap[:, :, 0:n * CH].rearrange("p j (c t) -> p j c t", t=CH)

        marks = {}
        with nc.Block() as block:
            @block.gpsimd
            def _(pool):
                for ap in (vS[:, :, 0:CH], vS[:, :, CH + T1:CH + T1P], Q2[:, :, NCH - 1, :, :], K2[:, :, NCH - 1, :, :]):
                    pool.wait_ge(pool_s.sem, pool_s.on(G.memset(ap, 0.0)))

            @block.vector
            def _(dve):
                for first, count, dst in ((0, 4, lambda j: sh[:, j, :]), (4, 4, lambda j: sh[:, 4 + j, :]),
                                          (8, 4, lambda j: vS[:, j, CH:CH + T1]),
                                          (12, 3, lambda j: sh[:, 8, :] if j == 0 else g_in[:, j - 1, :])):
                    diff = work if first % 8 == 0 else kk
                    if first >= 8:
                        dve.wait_ge(dve_s.sem, dve_s.value - 4)
                    cur = raw[:, first:first + count, 1:1 + T1]
                    n = dve_s.on(V.tensor_tensor(diff[:, 0:count, :], raw[:, first:first + count, 0:T1], cur, ALU.subtract))
                    dve.wait_ge(dve_s.sem, n)
                    for j in range(count):
                        dve_s.on(V.scalar_tensor_tensor(out=dst(j), in0=diff[:, j, :], scalar=param("mu_rw", first + j),
                                                        in1=raw[:, first + j, 1:1 + T1], op0=ALU.mult, op1=ALU.add))

            @block.scalar
            def _(act):
                act.wait_ge(dve_s.sem, dve_s.value)
                act_s.on(S.activation(sh[0:64, 8, :], sh[0:64, 8, :], ACT.Tanh))
                n = act_s.on(S.activation(g_in, g_in, ACT.Sigmoid))

            @block.tensor
            def _(pe):
                pe.wait_ge(act_s.sem, act_s.value - 1)
                for m in range(CT):
                    pe_s.on(T.matmul(bank[m][:, 0:T1], wa_up[0:64, m * P:m * P + P], sh[0:64, 8, :], start=True, stop=True))
                for m in range(CT):
                    pe_s.on(T.matmul(bank[4 + m][:, 0:T1], wa_up[64:128, m * P:m * P + P], sh[64:128, 8, :], start=True, stop=True))

            @block.scalar
            def _(act):
                for m in range(CT):
                    act.wait_ge(pe_s.sem, pe_s.value - 7 + m)
                    act_s.on(S.activation(ld[:, m, 0:T1], bank[m][:, 0:T1], ACT.Sigmoid, bias=param("w0", m)))
                for m in range(CT):
                    act.wait_ge(pe_s.sem, pe_s.value - 3 + m)
                    act_s.on(S.activation(rate[:, m, :], bank[4 + m][:, 0:T1], ACT.Sigmoid, bias=param("a0", m)))

            @block.vector
            def _(dve):
                dve.wait_ge(dve_s.sem, dve_s.value)
                for j in range(CT):
                    n = dve_s.on(V.tensor_scalar(kk[:, j, :], sh[:, 4 + j, :], param("k_k", j), None, ALU.mult))
                dve.wait_ge(dve_s.sem, n)
                marks["squares"] = dve_s.on(V.tensor_tensor(work, kk, kk, ALU.mult))
                dve.wait_ge(act_s.sem, act_s.value - 4)
                dve_s.on(V.memset(ld[:, :, T1:T1P], 0.0))
                n = dve_s.on(V.tensor_scalar(ld[:, :, 0:T1], ld[:, :, 0:T1], -float(np.exp(-0.5)), None, ALU.mult))
                dve.wait_ge(dve_s.sem, n)
                for j in range(CT):
                    n = dve_s.on(V.tensor_tensor_scan(c_sum[:, j, :], reset64, ld[:, j, :], 0.0, ALU.mult, ALU.add))
                dve.wait_ge(dve_s.sem, n)
                sums = dve_s.on(V.tensor_tensor(ld, c_sum, ld, ALU.subtract))

            @block.tensor
            def _(pe):
                pe.wait_ge(dve_s.sem, marks["squares"])
                pe.wait_ge(act_s.sem, act_s.value - 4)
                for j in range(CT):
                    pe_s.on(T.matmul(bank[j][:, 0:T1], blk64, work[:, j, :], start=True, stop=True))

            @block.scalar
            def _(act):
                act.wait_ge(dve_s.sem, dve_s.value)
                act_s.on(S.activation(e_pos, c_sum, ACT.Exp))
                act_s.on(S.activation(e_neg, c_sum, ACT.Exp, scale=-1.0))
                act_s.on(S.activation(ld, ld, ACT.Exp))

            @block.vector
            def _(dve):
                exps = act_s.value
                rates = exps - 3
                for j in range(CT):
                    dve.wait_ge(pe_s.sem, pe_s.value - 3 + j)
                    n = dve_s.on(V.tensor_scalar(grow[:, j, :], bank[j][:, 0:T1], 1e-24, None, ALU.max))

            @block.scalar
            def _(act):
                act.wait_ge(dve_s.sem, dve_s.value)
                act_s.on(S.activation(grow, grow, ACT.Sqrt))

            @block.vector
            def _(dve):
                dve.wait_ge(act_s.sem, act_s.value)
                dve.wait_ge(dve_s.sem, dve_s.on(V.reciprocal(grow, grow)))
                dve.wait_ge(dve_s.sem, dve_s.on(V.tensor_tensor(kk, kk, grow, ALU.mult)))
                for j in range(CT):
                    n = dve_s.on(V.tensor_scalar(work[:, j, :], rate[:, j, :], -1.0, param("k_a", j), ALU.add, ALU.mult))
                dve.wait_ge(dve_s.sem, n)
                dve.wait_ge(dve_s.sem, dve_s.on(V.scalar_tensor_tensor(out=work, in0=work, scalar=1.0, in1=sh[:, 4:8, :],
                                                                      op0=ALU.add, op1=ALU.mult)))
                for j in range(CT):
                    dve_s.on(V.scalar_tensor_tensor(out=rk[:, j, :], in0=sh[:, j, :], scalar=param("r_k", j),
                                                    in1=work[:, j, :], op0=ALU.mult, op1=ALU.mult))
                dve.wait_ge(dve_s.sem, dve_s.on(V.tensor_tensor(rate, rate, kk, ALU.mult)))
                tail = T1 - (NCH - 1) * CH
                for dst, i, x, e in ((Q2, 0, kk, ld), (Q2, 1, sh[:, 0:4, :], e_pos), (K2, 0, rate, e_neg), (K2, 1, work, e_neg)):
                    dve_s.on(V.tensor_tensor(dst[:, :, 0:NCH - 1, i, :], chunks(x, NCH - 1), chunks(e, NCH - 1), ALU.mult))
                    dve.wait_ge(pool_s.sem, pool_s.value)
                    dve_s.on(V.tensor_tensor(dst[:, :, NCH - 1, i, 0:tail], x[:, :, T1 - tail:T1], e[:, :, T1 - tail:T1], ALU.mult))

        mi = Memory(sbuf, at_K2tok, top)
        K2tok = mi.take(NCH * CT, P)
        O = mi.take(NM, P)
        at_L = mi.at
        L = mi.take(NM, CH)
        LM = mi.take(2, 8, CH)
        WW = mi.take(2, 8, CH)
        SBD = mi.take(CT, P)
        R = mi.take(C)
        decay_end = mi.take(CT, NCH)
        XT = view(at_K2, NM, CH)
        UV = view(at_L, NCH, C)
        m_of = lambda ch, h: ch * HEADS + (h % 2) * 4 + h // 2
        X = O[0:64, :, 0:CH]
        Tm = XT[0:64]
        bc = lambda ap, n: ap.unsqueeze(1).broadcast_to([ap.shape[0], n, ap.shape[1]])
        with nc.Block() as block:
            dve0, pe0, act0 = dve_s.value, pe_s.value, act_s.value

            @block.tensor
            def _(pe):
                for ch in range(NCH):
                    for par in range(2):
                        n = 2 * ch + par
                        if n >= 4:
                            pe.wait_ge(dve_s.sem, dve0 + n - 3 + 1)
                        lo = par * 64
                        for j in range(CT):
                            mm = T.matmul(bank[n % 4][:, j * P:j * P + P],
                                          K2[lo:lo + 64, j, ch, :, :].rearrange("p a b -> p (a b)"),
                                          Q2[lo:lo + 64, j, ch, :, :].rearrange("p a b -> p (a b)"), start=True, stop=True)
                        pe_s.on(mm)
                for ch in range(NCH):
                    if ch >= 2:
                        pe.wait_ge(act_s.sem, act0 + ch - 1)
                    for j in range(CT):
                        t = T.transpose(bank[4 + ch % 2][:, j * P:j * P + P],
                                        K2[:, j, ch, :, :].rearrange("p a b -> p (a b)"), ident)
                    pe_s.on(t)

            @block.vector
            def _(dve):
                dve_s.on(V.tensor_copy(decay_end, e_pos[:, :, CH - 1:T1P:CH]))
                for n in range(2 * NCH):
                    dve.wait_ge(pe_s.sem, pe0 + n + 1)
                    if n == 0:
                        dve.wait_ge(dve_s.sem, dve_s.value)
                    dve_s.on(V.tensor_tensor(O[:, 4 * n:4 * n + 4, :], bank[n % 4][:, :].rearrange("p (a b) -> p a b", b=P),
                                             bc(rw_mask, 4), ALU.mult))

            @block.scalar
            def _(act):
                for ch in range(NCH):
                    act.wait_ge(pe_s.sem, pe0 + 2 * NCH + ch + 1)
                    act_s.on(S.activation(K2tok[:, ch * CT:ch * CT + CT, :],
                                          bank[4 + ch % 2][:, :].rearrange("p (a b) -> p a b", b=P), ACT.Copy))

        with nc.Block() as block:
            dve0, pe0, act0 = dve_s.value, pe_s.value, act_s.value

            @block.tensor
            def _(pe):
                for g in range(NCH):
                    for i in range(8):
                        t = T.transpose(bank[g][0:64, i * CH:i * CH + CH], O[0:64, 8 * g + i, 0:CH], ident[0:64, 0:64])
                    pe_s.on(t)

            @block.scalar
            def _(act):
                for g in range(NCH):
                    act.wait_ge(pe_s.sem, pe0 + g + 1)
                    act_s.on(S.activation(L[0:64, 8 * g:8 * g + 8, :],
                                          bank[g][0:64, :].rearrange("p (a b) -> p a b", b=CH), ACT.Copy))

            @block.vector
            def _(dve):
                eye = bc(ident[0:64, 0:64], 8)
                for g in range(NCH):
                    s = slice(8 * g, 8 * g + 8)
                    dve.wait_ge(act_s.sem, act0 + g + 1)
                    dve.wait_ge(dve_s.sem, dve_s.on(V.tensor_tensor(X[:, s, :], X[:, s, :], bc(upper[0][0:64, 0:64], 8), ALU.mult)))
                    dve_s.on(V.tensor_tensor(X[:, s, :], eye, X[:, s, :], ALU.subtract))
                    dve.wait_ge(dve_s.sem, dve_s.on(V.tensor_tensor(Tm[:, s, :], L[0:64, s, :], bc(lower[0][0:64, 0:64], 8), ALU.mult)))
                    dve_s.on(V.tensor_tensor(Tm[:, s, :], eye, Tm[:, s, :], ALU.subtract))

        def triangular_inverse(L, X, Tm, LM, WW, width, per, groups, levels):
            s_lm = Signal(nc, ctx, "level_block" + str(width))
            s_w = Signal(nc, ctx, "block_times_inverse" + str(width))
            s_wc = Signal(nc, ctx, "block_times_inverse_copied" + str(width))
            s_xw = Signal(nc, ctx, "correction" + str(width))
            s_x = Signal(nc, ctx, "inverse_updated" + str(width))
            shaped = lambda b: b[0:width, :].rearrange("p (a b) -> p a b", b=width)
            todo = [(n, g) for n in levels for g in range(groups)]
            with nc.Block() as block:
                @block.vector
                def _(dve):
                    def mask(i):
                        n, g = todo[i]
                        if i >= 2:
                            dve.wait_ge(s_w.sem, i - 1)
                        s_lm.on(V.tensor_tensor(LM[0:width, i % 2], L[0:width, per * g:per * g + per, :],
                                                bc(lower[n][0:width, 0:width], per), ALU.mult))

                    def update(i):
                        n, g = todo[i]
                        s = slice(per * g, per * g + per)
                        dve.wait_ge(s_xw.sem, i + 1)
                        s_x.on(V.tensor_tensor(X[:, s, :], X[:, s, :], shaped(bank[2 + i % 2]), ALU.subtract))
                        s_x.on(V.tensor_tensor(Tm[:, s, :], Tm[:, s, :], shaped(bank[4 + i % 2]), ALU.subtract))
                    for i in range(len(todo) + 2):
                        if i < len(todo):
                            mask(i)
                        if i >= 2:
                            update(i - 2)

                @block.tensor
                def _(pe):
                    def block_product(i):
                        n, g = todo[i]
                        pe.wait_ge(s_lm.sem, i + 1)
                        if i >= groups:
                            pe.wait_ge(s_x.sem, 2 * (i - groups + 1))
                        if i >= 2:
                            pe.wait_ge(s_wc.sem, i - 1)
                        for q in range(per):
                            mm = T.matmul(bank[i % 2][0:width, q * width:q * width + width], LM[0:width, i % 2, q, :],
                                          X[:, per * g + q, :], start=True, stop=True)
                        s_w.on(mm)

                    def corrections(i):
                        n, g = todo[i]
                        pe.wait_ge(s_wc.sem, i + 1)
                        if i >= 2:
                            pe.wait_ge(s_x.sem, 2 * (i - 1))
                        for q in range(per):
                            T.matmul(bank[2 + i % 2][0:width, q * width:q * width + width], Tm[:, per * g + q, :],
                                     WW[0:width, i % 2, q, :], start=True, stop=True)
                        for q in range(per):
                            mm = T.matmul(bank[4 + i % 2][0:width, q * width:q * width + width], WW[0:width, i % 2, q, :],
                                          Tm[:, per * g + q, :], start=True, stop=True)
                        s_xw.on(mm)
                    for i in range(len(todo) + 1):
                        if i < len(todo):
                            block_product(i)
                        if i >= 1:
                            corrections(i - 1)

                @block.scalar
                def _(act):
                    for i in range(len(todo)):
                        act.wait_ge(s_w.sem, i + 1)
                        if i >= 2:
                            act.wait_ge(s_xw.sem, i - 1)
                        s_wc.on(S.activation(WW[0:width, i % 2], shaped(bank[i % 2]), ACT.Copy))

        triangular_inverse(L, X, Tm, LM, WW, CH, 8, NCH, range(1, 6))

        with nc.Block() as block:
            dve0, pe0 = dve_s.value, pe_s.value

            @block.tensor
            def _(pe):
                for ch in range(NCH):
                    if ch >= 4:
                        pe.wait_ge(dve_s.sem, dve0 + 2 + ch - 3)
                    for j in range(CT):
                        t = T.transpose(bank[ch % 4][:, j * P:j * P + P], vS[:, j, CH * ch:CH * ch + P], ident)
                    pe_s.on(t)

            @block.vector
            def _(dve):
                dve_s.on(V.memset(UV[0:64, :, :], 0.0))
                dve_s.on(V.memset(SBD, 0.0))
                for ch in range(NCH):
                    dve.wait_ge(pe_s.sem, pe0 + ch + 1)
                    dve_s.on(V.tensor_copy(UV[64:128, ch, :], bank[ch % 4][64:128, :]))

        s_r = Signal(nc, ctx, "rhs_ready")
        s_rc = Signal(nc, ctx, "rhs_copied")
        s_u = Signal(nc, ctx, "u_ready")
        s_uc = Signal(nc, ctx, "u_copied")
        s_ry = Signal(nc, ctx, "chunk_out")
        s_ryc = Signal(nc, ctx, "chunk_out_copied")
        s_st = Signal(nc, ctx, "state_change")
        s_state = Signal(nc, ctx, "state_ready")
        with nc.Block() as block:
            @block.tensor
            def _(pe):
                for ch in range(NCH):
                    if ch:
                        pe.wait_ge(s_state.sem, 4 * ch)
                    for j in range(CT):
                        T.matmul(bank[0][0:64, j * P:j * P + P], Q2[:, j, ch, 0, :], SBD[:, j, :], start=True, stop=False,
                                 skip_group_check=True)
                        for h in (2 * j, 2 * j + 1):
                            mm = T.matmul(bank[0][0:64, h * DH:h * DH + DH], O[:, m_of(ch, h), 0:CH],
                                          UV[:, ch, h * DH:h * DH + DH], start=False, stop=True, skip_group_check=True)
                    s_r.on(mm)
                    pe.wait_ge(s_rc.sem, ch + 1)
                    for h in range(HEADS):
                        mm = T.matmul(bank[1][0:64, h * DH:h * DH + DH], X[:, m_of(ch, h), :], R[0:64, h * DH:h * DH + DH],
                                      start=True, stop=True)
                    s_u.on(mm)
                    pe.wait_ge(s_uc.sem, ch + 1)
                    if ch < NCH - 1:
                        for h in range(HEADS):
                            lo = DH * (h % 2)
                            mm = T.matmul(bank[4][lo:lo + DH, (h // 2) * P + lo:(h // 2) * P + lo + DH],
                                          K2tok[:, ch * CT + h // 2, lo:lo + DH], UV[:, ch, h * DH:h * DH + DH],
                                          start=True, stop=True)
                        s_st.on(mm)
                    if ch >= 2:
                        pe.wait_ge(s_ryc.sem, ch - 1)
                    for j in range(CT):
                        T.matmul(bank[2 + ch % 2][:, j * CH:j * CH + CH], SBD[:, j, :], Q2[:, j, ch, 1, :], start=True,
                                 stop=False, skip_group_check=True)
                        for h in (2 * j, 2 * j + 1):
                            lo = DH * (h % 2)
                            mm = T.matmul(bank[2 + ch % 2][lo:lo + DH, j * CH:j * CH + CH], UV[:, ch, h * DH:h * DH + DH],
                                          O[:, m_of(ch, h), CH:P], start=False, stop=True, skip_group_check=True)
                    s_ry.on(mm)

            @block.scalar
            def _(act):
                for ch in range(NCH):
                    act.wait_ge(s_r.sem, ch + 1)
                    if ch:
                        act.wait_ge(s_u.sem, ch)
                    s_rc.on(S.activation(R[0:64], bank[0][0:64, :], ACT.Copy))
                    act.wait_ge(s_u.sem, ch + 1)
                    s_uc.on(S.activation(UV[0:64, ch, :], bank[1][0:64, :], ACT.Copy, scale=-1.0))

            @block.vector
            def _(dve):
                for ch in range(NCH):
                    if ch < NCH - 1:
                        dve.wait_ge(s_st.sem, ch + 1)
                        dve.wait_ge(s_ry.sem, ch + 1)
                        for lo in (0, DH):
                            s = SBD[lo:lo + DH, :, lo:lo + DH]
                            s_state.on(V.tensor_tensor(s, s, bank[4][lo:lo + DH, :].rearrange("p (a b) -> p a b", b=P)[:, :, lo:lo + DH], ALU.add))
                        dve.wait_ge(s_state.sem, 4 * ch + 2)
                        for lo in (0, DH):
                            s = SBD[lo:lo + DH, :, lo:lo + DH]
                            s_state.on(V.tensor_tensor(s, s, decay_end[lo:lo + DH, :, ch:ch + 1].broadcast_to([DH, CT, DH]), ALU.mult))
                    dve.wait_ge(s_ry.sem, ch + 1)
                    n = min(CH, T1 - ch * CH)
                    s_ryc.on(V.tensor_copy(y_rw[:, :, ch * CH:ch * CH + n],
                                           bank[2 + ch % 2][:, 0:CT * CH].rearrange("p (a b) -> p a b", b=CH)[:, :, 0:n]))

        mg = Memory(sbuf, at_K2, top)
        dev, sq, gnr = mg.take(CT, T1), mg.take(CT, T1), mg.take(CT, T1)
        with nc.Block() as block:
            pe0 = pe_s.value

            @block.tensor
            def _(pe):
                for j in range(CT):
                    pe_s.on(T.matmul(bank[j][:, 0:T1], blk64, y_rw[:, j, :], start=True, stop=True))
                for j in range(CT):
                    pe_s.on(T.matmul(bank[4 + j][:, 0:T1], blk64, rk[:, j, :], start=True, stop=True))

            @block.vector
            def _(dve):
                for j in range(CT):
                    dve.wait_ge(pe_s.sem, pe0 + j + 1)
                    n = dve_s.on(V.scalar_tensor_tensor(out=dev[:, j, :], in0=bank[j][:, 0:T1], scalar=-1.0 / DH,
                                                        in1=y_rw[:, j, :], op0=ALU.mult, op1=ALU.add))
                dve.wait_ge(dve_s.sem, n)
                dve_s.on(V.tensor_tensor(sq, dev, dev, ALU.mult))
                for j in range(CT):
                    dve.wait_ge(pe_s.sem, pe0 + 4 + j + 1)
                    dve_s.on(V.tensor_tensor(rk[:, j, :], bank[4 + j][:, 0:T1], vS[:, j, CH:CH + T1], ALU.mult))

            @block.tensor
            def _(pe):
                pe.wait_ge(dve_s.sem, dve_s.value - 4)
                for j in range(CT):
                    pe_s.on(T.matmul(bank[j][:, 0:T1], blk64, sq[:, j, :], start=True, stop=True))
                pe.wait_ge(dve_s.sem, dve_s.value)
                for j in range(CT):
                    T.matmul(bank[4 + j][:, 0:T1], g_up0[:, j * P:j * P + P], g_in[:, 0, :], start=True, stop=False)
                    pe_s.on(T.matmul(bank[4 + j][:, 0:T1], g_up1[0:32, j * P:j * P + P], g_in[0:32, 1, :], start=False, stop=True))

            @block.scalar
            def _(act):
                for j in range(CT):
                    act.wait_ge(pe_s.sem, pe0 + 8 + j + 1)
                    act_s.on(S.activation(gnr[:, j, :], bank[j][:, 0:T1], ACT.Sqrt, bias=eps_gn, scale=1.0 / DH))

            @block.vector
            def _(dve):
                dve.wait_ge(act_s.sem, act_s.value)
                dve.wait_ge(dve_s.sem, dve_s.on(V.reciprocal(gnr, gnr)))
                dve.wait_ge(dve_s.sem, dve_s.on(V.tensor_tensor(dev, dev, gnr, ALU.mult)))
                for j in range(CT):
                    n = dve_s.on(V.tensor_scalar(dev[:, j, :], dev[:, j, :], param("ln_x_w", j), param("ln_x_b", j), ALU.mult, ALU.add))
                dve.wait_ge(dve_s.sem, n)
                dve.wait_ge(dve_s.sem, dve_s.on(V.tensor_tensor(dev, dev, rk, ALU.add)))
                for j in range(CT):
                    dve.wait_ge(pe_s.sem, pe0 + 12 + j + 1)
                    dve_s.on(V.tensor_tensor(y_rw[:, j, :], dev[:, j, :], bank[4 + j][:, 0:T1], ALU.mult))
        gates = view(A0, 2 * KD, T1)
        part = view(A0 + 2 * KD * T1, KD, T1)
        merged = view(A0 + 3 * KD * T1, KD, T1)

        def gate_out(engine, m, psum):
            return S.activation(gates[:, m, :], psum, ACT.Sigmoid)
        project(xnT, T1, [(7 + m // 4, (m % 4) * P, P) for m in range(2 * KD)], gate_out, 7, 4, owner=lambda m: "act")

        def sb_out(engine, m, psum):
            return V.tensor_tensor(part[:, m, :], psum, gates[:, m, :], ALU.mult)
        project(y_sb, T1, [(SB_OUT, m * P, P) for m in range(KD)], sb_out, SB_OUT, 1, owner=lambda m: "dve")

        def rw_out(engine, m, psum):
            return V.tensor_tensor(merged[:, m, :], psum, gates[:, KD + m, :], ALU.mult)
        project(y_rw, T1, [(SB_OUT + 1, m * P, P) for m in range(KD)], rw_out, SB_OUT + 1, 1, owner=lambda m: "dve")
        with nc.Block() as block:
            @block.vector
            def _(dve):
                dve_s.on(V.tensor_tensor(merged, merged, part, ALU.add))

        def add_to_stream(engine, m, psum):
            return V.tensor_tensor(hT[:, m, :], hT[:, m, :], psum, ALU.add)
        project(merged, T1, [(W_OUT + m // 4, (m % 4) * P, P) for m in range(KD)], add_to_stream, W_OUT, 2,
                owner=lambda m: "dve")

        hnT = view(base, KD, T1)
        ffn = view(base + KD * T1, FT, T1)
        fsig = view(base + (KD + FT) * T1, 2, T1)
        fsq = view(base + (KD + FT + 2) * T1, KD, T1)
        rms_norm(hT, hnT, lambda j: param("norm_ffn", j), None, T1, fsq, fsig[:, 0, :])
        s_gu = Signal(nc, ctx, "gate_up_ready")
        s_sig = Signal(nc, ctx, "gate_sigmoid")
        s_hid = Signal(nc, ctx, "hidden_ready")
        with nc.Block() as block:
            pe0 = pe_s.value

            @block.tensor
            def _(pe):
                for m in range(FT):
                    s, half = FFN_IN + m // 2, m % 2
                    if half == 0:
                        await_slot(pe, s)
                    if m >= 4:
                        pe.wait_ge(s_hid.sem, 2 * (m - 3))
                    for up in range(2):
                        for k in range(KD):
                            c0 = 256 * up + P * half
                            mm = T.matmul(bank[2 * (m % 4) + up][:, 0:T1], slot(s)[:, k, c0:c0 + P], hnT[:, k, :],
                                          start=(k == 0), stop=(k == KD - 1))
                    pe_s.on(mm)
                    slot_freed[s] = pe_s.value

            @block.sync
            def _(sp):
                load_slots(sp, FFN_OUT + RING)

            @block.scalar
            def _(act):
                for m in range(FT):
                    act.wait_ge(pe_s.sem, pe0 + m + 1)
                    if m >= 2:
                        act.wait_ge(s_hid.sem, 2 * (m - 1))
                    s_sig.on(S.activation(fsig[:, m % 2, :], bank[2 * (m % 4)][:, 0:T1], ACT.Sigmoid))

            @block.vector
            def _(dve):
                for m in range(FT):
                    dve.wait_ge(s_sig.sem, m + 1)
                    s_hid.on(V.tensor_tensor(ffn[:, m, :], bank[2 * (m % 4)][:, 0:T1], fsig[:, m % 2, :], ALU.mult))
                    dve.wait_ge(s_hid.sem, 2 * m + 1)
                    s_hid.on(V.tensor_tensor(ffn[:, m, :], ffn[:, m, :], bank[2 * (m % 4) + 1][:, 0:T1], ALU.mult))

        with nc.Block() as block:
            pe0 = pe_s.value

            @block.tensor
            def _(pe):
                for k in range(FT):
                    s, r = FFN_OUT + k // 4, k % 4
                    if r == 0:
                        await_slot(pe, s)
                    for m in range(KD):
                        mm = T.matmul(bank[m][:, 0:T1], slot(s)[:, r, m * P:m * P + P], ffn[:, k, :],
                                      start=(k == 0), stop=(k == FT - 1))
                    slot_freed[s] = pe_s.on(mm)

            @block.sync
            def _(sp):
                load_slots(sp, ADA + RING)

            @block.vector
            def _(dve):
                for m in range(KD):
                    dve.wait_ge(pe_s.sem, pe_s.value)
                    dve_s.on(V.tensor_tensor(hT[:, m, :], hT[:, m, :], bank[m][:, 0:T1], ALU.add))

        end = total - CONSTS
        xT = view(base + 12288, KD, T2)
        at2 = base + 12288 + KD * T2
        m2 = Memory(sbuf, at2, end)
        mod = view(end - 64, 6 * KD)
        csil = view(end - 96, KD, 1)
        gain1 = view(end - 112, KD)
        gain2 = view(end - 128, KD)
        e_hg = view(end - 160, 2 * GH)
        lb = view(end - 168, GH)
        lb1 = view(end - 176, GH)
        rms_norm(hT[:, :, N_META:T1], xT, lambda j: param("norm_final", j), None, T2, view(base, KD, T2), view(base + KD * T2, T2))
        with nc.Block() as block:
            @block.scalar
            def _(act):
                c0 = ROWS0["c_2"][0]
                act_s.on(S.activation(csil[:, :, 0], vec0[:, c0:c0 + KD], ACT.Sigmoid))

            @block.vector
            def _(dve):
                c0 = ROWS0["c_2"][0]
                dve.wait_ge(act_s.sem, act_s.value)
                dve_s.on(V.tensor_tensor(csil[:, :, 0], csil[:, :, 0], vec0[:, c0:c0 + KD], ALU.mult))

        def mod_out(engine, m, psum):
            return V.tensor_tensor(mod[:, m:m + 1], psum, param("b_ada_2", m), ALU.add)
        project(csil, 1, [(ADA + m // 4, (m % 4) * P, P) for m in range(6 * KD)], mod_out, ADA, 12, owner=lambda m: "dve")
        with nc.Block() as block:
            @block.vector
            def _(dve):
                for gain_, name, sc in ((gain1, "norm1_w_2", 1), (gain2, "norm2_w_2", 4)):
                    c0 = ROWS0[name][0]
                    dve_s.on(V.scalar_tensor_tensor(out=gain_, in0=mod[:, sc * KD:sc * KD + KD], scalar=1.0,
                                                    in1=vec0[:, c0:c0 + KD], op0=ALU.add, op1=ALU.mult))
                r0 = ROWS0["hg_lb_2"][0]
                a0_, a1_ = vec0[:, r0:r0 + GH], vec0[:, r0 + GH:r0 + 2 * GH]
                n = dve_s.on(V.tensor_tensor(lb, a0_, a1_, ALU.max))
                dve.wait_ge(dve_s.sem, n)
                dve_s.on(V.tensor_tensor(e_hg[:, 0:GH], a0_, lb, ALU.subtract))
                dve_s.on(V.tensor_tensor(e_hg[:, GH:2 * GH], a1_, lb, ALU.subtract))

            @block.scalar
            def _(act):
                act.wait_ge(dve_s.sem, dve_s.value)
                act_s.on(S.activation(e_hg, e_hg, ACT.Exp))

            @block.vector
            def _(dve):
                dve.wait_ge(act_s.sem, act_s.value)
                dve.wait_ge(dve_s.sem, dve_s.on(V.tensor_tensor(lb1, e_hg[:, 0:GH], e_hg[:, GH:2 * GH], ALU.add)))
                dve.wait_ge(dve_s.sem, dve_s.on(V.reciprocal(lb1, lb1)))
                dve_s.on(V.tensor_tensor(lb, e_hg[:, 0:GH], lb1, ALU.mult))
                dve.wait_ge(dve_s.sem, dve_s.value)
                dve_s.on(V.tensor_scalar(lb1, lb, -1.0, 1.0, ALU.mult, ALU.add))
        low = Memory(sbuf, base, base + 12288)
        hm = low.take(KD, T2)
        raw2 = low.take(12, 3 + T2)
        over_hm = base
        proj_b = low.take(5, GH, T2)
        gate_a, f_b, i_b, q_b, gate_b = (proj_b[:, i] for i in range(5))
        qkv = m2.take(12, T2)
        G_at = m2.at
        gcB = m2.take(GH, T2)
        beB = m2.take(GH, T2)
        Dm = m2.take(2 * GH, P)
        GG = m2.take(2 * GH, 2 * P)
        L2 = m2.take(2 * GH, P)
        Tm2 = m2.take(2 * GH, P)
        LM2 = m2.take(2, 4, P)
        WW2 = m2.take(2, 4, P)
        rows_b, rows_g = m2.take(T2), m2.take(T2)
        cols = m2.take(4, GH)
        tail_f = m2.take(GH)
        ealog = m2.take(1)
        o_all = m2.take(KD, T2)
        assert m2.at <= end - 192, (m2.at, end)
        ba = small[:, 0:64].rearrange("p (k c) -> p k c", c=8)
        alog, dtb = small[0:GH, 64:65], small[0:GH, 65:66]
        rms_norm(xT, hm, lambda j: gain1[:, j:j + 1], lambda j: mod[:, j:j + 1], T2, view(m2.at - KD * T2, KD, T2), view(at2, T2))
        with nc.Block() as block:
            @block.gpsimd
            def _(pool):
                pool_s.on(G.memset(raw2[:, :, 0:3], 0.0))

        def put_in2(engine, m, psum):
            dst = raw2[:, m, 3:3 + T2] if m < 12 else proj_b[:, (m - 12) // 4, m % 4, :]
            if engine is nc.scalar:
                return S.activation(dst, psum, ACT.Copy)
            return V.tensor_copy(dst, psum)
        project(hm, T2, [(W_IN2 + m // 4, (m % 4) * P, P) for m in range(32)], put_in2, W_IN2, 8)

        with nc.Block() as block:
            @block.tensor
            def _(pe):
                for i in range(2):
                    for k in range(KD):
                        mm = T.matmul(bank[i][0:GH, 0:T2], ba[:, k, GH * i:GH * i + GH], hm[:, k, :],
                                      start=(k == 0), stop=(k == KD - 1))
                    pe_s.on(mm)

            @block.scalar
            def _(act):
                act.wait_ge(pe_s.sem, pe_s.value - 1)
                act_s.on(S.activation(rows_b[0:GH, :], bank[0][0:GH, 0:T2], ACT.Sigmoid))
                act.wait_ge(pe_s.sem, pe_s.value)
                act_s.on(S.activation(ealog[0:GH, :], alog, ACT.Exp))
                marks["abs"] = act_s.on(S.activation(rows_g[0:GH, :], bank[1][0:GH, 0:T2], ACT.Abs, bias=dtb))
                act.wait_ge(act_s.sem, act_s.value)
                act.wait_ge(act_s.sem, act_s.on(S.activation(rows_g[0:GH, :], rows_g[0:GH, :], ACT.Exp, scale=-1.0)))
                act_s.on(S.activation(rows_g[0:GH, :], rows_g[0:GH, :], ACT.Ln, bias=one_col[0:GH, :]))

            @block.vector
            def _(dve):
                for j in (3, 2, 1, 0):
                    for m in range(12):
                        w = param("conv_w_2", 12 * j + m)
                        if j == 3:
                            dve_s.on(V.tensor_scalar(qkv[:, m, :], raw2[:, m, 3:3 + T2], w, None, ALU.mult))
                        else:
                            dve.wait_ge(dve_s.sem, dve_s.value - 11)
                            dve_s.on(V.scalar_tensor_tensor(out=qkv[:, m, :], in0=raw2[:, m, j:j + T2], scalar=w,
                                                            in1=qkv[:, m, :], op0=ALU.mult, op1=ALU.add))
                marks["conv"] = dve_s.value

            @block.scalar
            def _(act):
                act.wait_ge(dve_s.sem, dve_s.value)
                marks["log_term"] = act_s.value
                marks["sig"] = act_s.on(S.activation(raw2[:, :, 0:T2], qkv, ACT.Sigmoid))

            @block.vector
            def _(dve):
                dve.wait_ge(act_s.sem, marks["log_term"])
                t = gcB[0:GH, 0, :]
                dve.wait_ge(dve_s.sem, dve_s.on(V.tensor_scalar(t, bank[1][0:GH, 0:T2], dtb, 0.0, ALU.add, ALU.max)))
                dve.wait_ge(dve_s.sem, dve_s.on(V.tensor_tensor(rows_g[0:GH, :], rows_g[0:GH, :], t, ALU.add)))
                dve.wait_ge(dve_s.sem, dve_s.on(V.tensor_scalar(t, rows_g[0:GH, :], ealog[0:GH, :], -1.0, ALU.mult, ALU.mult)))
                marks["rows"] = dve_s.on(V.tensor_tensor_scan(rows_g[0:GH, :], reset128[0:GH, :], t, 0.0, ALU.mult, ALU.add))
                dve.wait_ge(act_s.sem, marks["sig"])
                dve.wait_ge(dve_s.sem, dve_s.on(V.tensor_tensor(qkv, qkv, raw2[:, :, 0:T2], ALU.mult)))
                dve_s.on(V.tensor_tensor(raw2[:, 0:8, 0:T2], qkv[:, 0:8, :], qkv[:, 0:8, :], ALU.mult))

            @block.tensor
            def _(pe):
                pe.wait_ge(dve_s.sem, dve_s.value)
                for m in range(8):
                    mm = T.matmul(bank[2 + m // 2][:, (m % 2) * T2:(m % 2) * T2 + T2], ones, raw2[:, m, 0:T2], start=True, stop=True)
                    if m % 2:
                        pe_s.on(mm)
                for i, rows in enumerate((rows_g, rows_b)):
                    for h in range(GH):
                        b = (6, 7, 0, 1)[2 * i + h // 2]
                        mm = T.matmul(bank[b][:, (h % 2) * T2:(h % 2) * T2 + T2], row_sel[0:GH, h, :], rows[0:GH, :],
                                      start=True, stop=True)
                    pe_s.on(mm)

            @block.scalar
            def _(act):
                for b in range(4):
                    act.wait_ge(pe_s.sem, pe_s.value - 5 + b)
                    act_s.on(S.activation(raw2[:, 2 * b:2 * b + 2, 0:T2], bank[2 + b][:, :].rearrange("p (a b) -> p a b", b=T2),
                                          ACT.Sqrt, bias=eps_rms))

            @block.vector
            def _(dve):
                dve.wait_ge(pe_s.sem, pe_s.value)
                for i, dst in enumerate((gcB, beB)):
                    for q in range(2):
                        dve_s.on(V.tensor_copy(dst[:, 2 * q:2 * q + 2, :], bank[(6, 7, 0, 1)[2 * i + q]][:, :].rearrange("p (a b) -> p a b", b=T2)))
                dve.wait_ge(act_s.sem, act_s.value)
                dve.wait_ge(dve_s.sem, dve_s.on(V.reciprocal(raw2[:, 0:8, 0:T2], raw2[:, 0:8, 0:T2])))
                dve_s.on(V.scalar_tensor_tensor(out=qkv[:, 0:4, :], in0=qkv[:, 0:4, :], scalar=P ** -0.5,
                                                in1=raw2[:, 0:4, 0:T2], op0=ALU.mult, op1=ALU.mult))
                dve_s.on(V.tensor_tensor(qkv[:, 4:8, :], qkv[:, 4:8, :], raw2[:, 4:8, 0:T2], ALU.mult))

            @block.tensor
            def _(pe):
                for i, rows in enumerate((rows_g, rows_b)):
                    for c in range(2):
                        t = T.transpose(bank[2][:, (2 * i + c) * GH:(2 * i + c) * GH + GH], rows[0:GH, c * P:c * P + P],
                                        ident[0:GH, 0:GH]) if not (i == 0 and c == 0) else None
                        if t is None:
                            pe.wait_ge(act_s.sem, act_s.value)
                            t = T.transpose(bank[2][:, 0:GH], rows[0:GH, 0:P], ident[0:GH, 0:GH])
                pe_s.on(t)

            @block.vector
            def _(dve):
                dve.wait_ge(pe_s.sem, pe_s.value)
                dve_s.on(V.tensor_copy(cols, bank[2][:, 0:4 * GH].rearrange("p (a b) -> p a b", b=GH)))

        lowa = Memory(sbuf, over_hm, over_hm + KD * T2 + 12 * (3 + T2))
        kg, qg, ktok, vtok, eg = (lowa.take(2 * GH, P) for _ in range(5))
        q2, k2, v2 = qkv[:, 0:4, :], qkv[:, 4:8, :], qkv[:, 8:12, :]
        mats = lambda ap: ap.rearrange("p h (c t) -> p (h c) t", c=2)
        pair = lambda b: b[:, :].rearrange("p (a b) -> p a b", b=P)
        X2 = GG[:, :, 0:P]
        AT = GG[:, :, P:2 * P]
        with nc.Block() as block:
            pe0, act0, dve0 = pe_s.value, act_s.value, dve_s.value

            @block.tensor
            def _(pe):
                for h in range(GH):
                    for c in range(2):
                        s = slice(c * P, c * P + P)
                        T.matmul(bank[h][:, c * 2 * P:c * 2 * P + P], k2[:, h, s], k2[:, h, s], start=True, stop=True)
                        mm = T.matmul(bank[h][:, c * 2 * P + P:c * 2 * P + 2 * P], k2[:, h, s], q2[:, h, s], start=True, stop=True)
                    pe_s.on(mm)
                for h in range(GH):
                    for c in range(2):
                        t = T.transpose(bank[4 + h // 2][:, (h % 2) * 2 * P + c * P:(h % 2) * 2 * P + c * P + P], v2[:, h, c * P:c * P + P], ident)
                pe_s.on(t)
                for h in range(GH):
                    t = T.transpose(bank[6][:, h * P:h * P + P], k2[:, h, 0:P], ident)
                pe_s.on(t)

            @block.vector
            def _(dve):
                for h in range(GH):
                    for c in range(2):
                        dve_s.on(V.tensor_scalar(Dm[:, 2 * h + c, :], gcB[:, h, c * P:c * P + P], cols[:, c, h:h + 1], 0.0,
                                                 ALU.subtract, ALU.min))
                for h in range(GH):
                    dve_s.on(V.tensor_tensor(tail_f[:, h:h + 1], gcB[:, h, P - 1:P], cols[:, 0, h:h + 1], ALU.subtract))

            @block.scalar
            def _(act):
                act.wait_ge(dve_s.sem, dve_s.value)
                act_s.on(S.activation(Dm, Dm, ACT.Exp))
                act_s.on(S.activation(eg, mats(gcB), ACT.Exp))
                act_s.on(S.activation(tail_f, tail_f, ACT.Exp))
                act.wait_ge(pe_s.sem, pe0 + 5)
                for q in range(2):
                    act_s.on(S.activation(vtok[:, 4 * q:4 * q + 4, :], pair(bank[4 + q]), ACT.Copy))
                act.wait_ge(pe_s.sem, pe0 + 6)
                act.wait_ge(act_s.sem, act_s.value - 2)
                for h in range(GH):
                    act_s.on(S.activation(ktok[:, h, :], bank[6][:, h * P:h * P + P], ACT.Copy, scale=tail_f[:, h:h + 1]))

            @block.vector
            def _(dve):
                dve.wait_ge(act_s.sem, act0 + 1)
                n = dve_s.on(V.tensor_tensor(mats(beB), mats(beB), Dm, ALU.mult))
                dve.wait_ge(dve_s.sem, n)
                for h in range(GH):
                    dve.wait_ge(pe_s.sem, pe0 + h + 1)
                    b3 = bank[h][:, :].rearrange("p (c i t) -> p c i t", c=2, i=2)
                    s = slice(2 * h, 2 * h + 2)
                    dve_s.on(V.tensor_tensor(X2[:, s, :], b3[:, :, 0, :], mats(beB)[:, s, :], ALU.mult))
                    dve_s.on(V.tensor_tensor(AT[:, s, :], b3[:, :, 1, :], Dm[:, s, :], ALU.mult))
                dve.wait_ge(dve_s.sem, dve_s.value)
                dve_s.on(V.tensor_tensor(X2, X2, bc(upper_strict, 2 * GH), ALU.mult))
                marks["n2"] = dve_s.value
                dve_s.on(V.tensor_tensor(AT, AT, bc(upper_incl, 2 * GH), ALU.mult))
                dve.wait_ge(act_s.sem, act0 + 2)
                dve_s.on(V.tensor_tensor(kg, mats(k2), eg, ALU.mult))
                dve_s.on(V.tensor_tensor(qg, mats(q2), eg, ALU.mult))

            @block.tensor
            def _(pe):
                pe.wait_ge(dve_s.sem, marks["n2"])
                for q in range(2):
                    for i in range(4):
                        t = T.transpose(bank[q][:, i * P:i * P + P], X2[:, 4 * q + i, :], ident)
                    pe_s.on(t)

            @block.vector
            def _(dve):
                eye = bc(ident, 4)
                for q in range(2):
                    s = slice(4 * q, 4 * q + 4)
                    dve.wait_ge(pe_s.sem, pe_s.value - 1 + q)
                    dve_s.on(V.tensor_copy(L2[:, s, :], pair(bank[q])))
                    dve.wait_ge(dve_s.sem, dve_s.on(V.tensor_tensor(X2[:, s, :], X2[:, s, :], bc(upper[0], 4), ALU.mult)))
                    dve_s.on(V.tensor_tensor(X2[:, s, :], eye, X2[:, s, :], ALU.subtract))
                    dve.wait_ge(dve_s.sem, dve_s.on(V.tensor_tensor(Tm2[:, s, :], L2[:, s, :], bc(lower[0], 4), ALU.mult)))
                    dve_s.on(V.tensor_tensor(Tm2[:, s, :], eye, Tm2[:, s, :], ALU.subtract))

        triangular_inverse(L2, X2, Tm2, LM2, WW2, P, 4, 2, range(1, 7))

        vn = L2
        RR = Tm2[:, 0:4, :]
        S2 = Tm2[:, 4:8, :]
        oA = LM2[:, :, :, :].rearrange("p a b c -> p (a b) c")
        with nc.Block() as block:
            @block.vector
            def _(dve):
                for h in range(GH):
                    dve_s.on(V.tensor_scalar(RR[:, h, :], vtok[:, 2 * h, :], cols[:, 2, h:h + 1], None, ALU.mult))

            @block.tensor
            def _(pe):
                pe.wait_ge(dve_s.sem, dve_s.value)
                for h in range(GH):
                    mm = T.matmul(bank[0][:, h * P:h * P + P], X2[:, 2 * h, :], RR[:, h, :], start=True, stop=True)
                pe_s.on(mm)

            @block.scalar
            def _(act):
                act.wait_ge(pe_s.sem, pe_s.value)
                act_s.on(S.activation(vn[:, 0:4, :], pair(bank[0]), ACT.Copy))

            @block.tensor
            def _(pe):
                pe.wait_ge(act_s.sem, act_s.value)
                for h in range(GH):
                    mm = T.matmul(bank[1][:, h * P:h * P + P], ktok[:, h, :], vn[:, h, :], start=True, stop=True)
                pe_s.on(mm)
                for h in range(GH):
                    mm = T.matmul(bank[2][:, h * P:h * P + P], vn[:, h, :], AT[:, 2 * h, :], start=True, stop=True)
                pe_s.on(mm)

            @block.scalar
            def _(act):
                act.wait_ge(pe_s.sem, pe_s.value - 1)
                act_s.on(S.activation(S2, pair(bank[1]), ACT.Copy))

            @block.tensor
            def _(pe):
                pe.wait_ge(act_s.sem, act_s.value)
                for h in range(GH):
                    mm = T.matmul(bank[3][:, h * P:h * P + P], kg[:, 2 * h + 1, :], S2[:, h, :], start=True, stop=True)
                pe_s.on(mm)

            @block.vector
            def _(dve):
                dve.wait_ge(pe_s.sem, pe_s.value)
                vt = vtok.rearrange("p (h c) t -> p h c t", c=2)
                dve.wait_ge(dve_s.sem, dve_s.on(V.tensor_tensor(RR, vt[:, :, 1, :], pair(bank[3]), ALU.subtract)))
                for h in range(GH):
                    dve_s.on(V.tensor_scalar(RR[:, h, :], RR[:, h, :], cols[:, 3, h:h + 1], None, ALU.mult))

            @block.tensor
            def _(pe):
                pe.wait_ge(dve_s.sem, dve_s.value)
                for h in range(GH):
                    mm = T.matmul(bank[4][:, h * P:h * P + P], X2[:, 2 * h + 1, :], RR[:, h, :], start=True, stop=True)
                pe_s.on(mm)

            @block.scalar
            def _(act):
                act.wait_ge(pe_s.sem, pe_s.value)
                act_s.on(S.activation(vn[:, 4:8, :], pair(bank[4]), ACT.Copy))

            @block.tensor
            def _(pe):
                pe.wait_ge(act_s.sem, act_s.value)
                for h in range(GH):
                    T.matmul(bank[5][:, h * P:h * P + P], S2[:, h, :], qg[:, 2 * h + 1, :], start=True, stop=False)
                    mm = T.matmul(bank[5][:, h * P:h * P + P], vn[:, 4 + h, :], AT[:, 2 * h + 1, :], start=False, stop=True)
                pe_s.on(mm)

            @block.vector
            def _(dve):
                dve.wait_ge(pe_s.sem, pe_s.value)
                ov = oA.rearrange("p (h c) t -> p h c t", c=2)
                dve_s.on(V.tensor_copy(ov[:, :, 0, :], pair(bank[2])))
                dve_s.on(V.tensor_copy(ov[:, :, 1, :], pair(bank[5])))

        oAh = oA.rearrange("p (h c) t -> p h (c t)", c=2)
        two = lambda b: b[:, :].rearrange("p (a b) -> p a b", b=T2)

        def gated_norm(o, sq, norm, gate, gain, dst, per_head):
            with nc.Block() as block:
                @block.vector
                def _(dve):
                    dve_s.on(V.tensor_tensor(sq, o, o, ALU.mult))

                @block.tensor
                def _(pe):
                    pe.wait_ge(dve_s.sem, dve_s.value)
                    for h in range(GH):
                        if per_head:
                            mm = T.matmul(bank[h // 2][:, (h % 2) * T2:(h % 2) * T2 + T2], ones, sq[:, h, :], start=True, stop=True)
                        else:
                            mm = T.matmul(bank[0][:, 0:T2], ones, sq[:, h, :], start=(h == 0), stop=(h == GH - 1))
                    pe_s.on(mm)

                @block.scalar
                def _(act):
                    act_s.on(S.activation(dst, gate, ACT.Sigmoid))
                    act.wait_ge(pe_s.sem, pe_s.value)
                    if per_head:
                        for q in range(2):
                            act_s.on(S.activation(norm[:, 2 * q:2 * q + 2, :], two(bank[q]), ACT.Sqrt, bias=eps_rms, scale=1.0 / P))
                    else:
                        act_s.on(S.activation(norm[:, 0, :], bank[0][:, 0:T2], ACT.Sqrt, bias=eps_rms, scale=1.0 / C))

                @block.vector
                def _(dve):
                    n = GH if per_head else 1
                    dve.wait_ge(act_s.sem, act_s.value)
                    dve.wait_ge(dve_s.sem, dve_s.on(V.reciprocal(norm[:, 0:n, :], norm[:, 0:n, :])))
                    for h in range(GH):
                        dve_s.on(V.scalar_tensor_tensor(out=sq[:, h, :], in0=o[:, h, :], scalar=gain(h), in1=norm[:, h if per_head else 0, :],
                                                        op0=ALU.mult, op1=ALU.mult))
                    dve.wait_ge(dve_s.sem, dve_s.on(V.tensor_tensor(dst, dst, gate, ALU.mult)))
                    dve_s.on(V.tensor_tensor(dst, dst, sq, ALU.mult))

        gated_norm(oAh, WW2.rearrange("p a b c -> p (a b c)").rearrange("p (h t) -> p h t", h=GH), gcB, gate_a,
                   lambda h: param("gdn_norm_w_2"), o_all[:, 0:GH, :], True)

        mh = Memory(sbuf, at2, m2.at - KD * T2 - 16)
        logf, kB = mh.take(GH, T2), mh.take(GH, T2)
        bcum, sgm = mh.take(GH, T2), mh.take(GH, T2)
        E = [mh.take(GH * T2) for _ in range(2)]
        Qb = [mh.take(GH * T2) for _ in range(2)]
        Kb = [mh.take(GH * T2) for _ in range(2)]
        acc = mh.take(2 * GH, P)
        masked = [mh.take(2 * GH, P) for _ in range(1)]
        low2 = Memory(sbuf, over_hm, over_hm + KD * T2 + 12 * (3 + T2))
        cross = low2.take(GH, P)
        itok = low2.take(2 * GH, P)
        oB = low2.take(GH, T2)
        wsq = low2.take(GH, T2)
        flat = lambda ap: ap.rearrange("p h t -> p (h t)")
        with nc.Block() as block:
            @block.scalar
            def _(act):
                act_s.on(S.activation(sgm, f_b, ACT.Sigmoid))
                act_s.on(S.activation(kB, f_b, ACT.Sigmoid, scale=-1.0))
                act_s.on(S.activation(acc, mats(q_b), ACT.Sigmoid))

            @block.gpsimd
            def _(pool):
                for ap in Qb + Kb:
                    pool.wait_ge(pool_s.sem, pool_s.on(G.memset(ap, 0.0)))

            @block.vector
            def _(dve):
                dve.wait_ge(act_s.sem, act_s.value)
                for h in range(GH):
                    dve_s.on(V.tensor_scalar(sgm[:, h, :], sgm[:, h, :], lb1[:, h:h + 1], lb[:, h:h + 1], ALU.mult, ALU.add))
                marks["f"] = dve_s.value
                for h in range(GH):
                    dve_s.on(V.tensor_scalar(kB[:, h, :], kB[:, h, :], lb1[:, h:h + 1], None, ALU.mult))
                dve_s.on(V.tensor_tensor(mats(q_b), mats(q_b), acc, ALU.mult))

            @block.scalar
            def _(act):
                act.wait_ge(dve_s.sem, marks["f"])
                act_s.on(S.activation(logf, sgm, ACT.Ln))

            @block.vector
            def _(dve):
                dve.wait_ge(act_s.sem, act_s.value)
                for h in range(GH):
                    dve_s.on(V.tensor_tensor_scan(bcum[:, h, :], reset128, logf[:, h, :], 0.0, ALU.mult, ALU.add))

            @block.tensor
            def _(pe):
                for h in range(GH):
                    for c in range(2):
                        t = T.transpose(bank[6 + h // 2][:, (h % 2) * 2 * P + c * P:(h % 2) * 2 * P + c * P + P], i_b[:, h, c * P:c * P + P], ident)
                pe_s.on(t)

            @block.scalar
            def _(act):
                act.wait_ge(pe_s.sem, pe_s.value)
                for q in range(2):
                    act_s.on(S.activation(itok[:, 4 * q:4 * q + 4, :], pair(bank[6 + q]), ACT.Copy))

        s_e = Signal(nc, ctx, "level_exponents")
        s_ee = Signal(nc, ctx, "level_decays")
        s_qk = Signal(nc, ctx, "level_operands")
        s_a = Signal(nc, ctx, "level_products")
        s_m = Signal(nc, ctx, "level_masked")
        s_acc = Signal(nc, ctx, "level_added")
        with nc.Block() as block:
            @block.vector
            def _(dve):
                def exponents(n):
                    b = 1 << n
                    v = flat(bcum).rearrange("p (k i t) -> p k i t", i=2, t=b)
                    e = E[n % 2].rearrange("p (k i t) -> p k i t", i=2, t=b)
                    ref = v[:, :, 0, b - 1:b].broadcast_to([P, GH * T2 // (2 * b), b])
                    if n >= 2:
                        dve.wait_ge(s_qk.sem, 2 * (n - 1))
                    s_e.on(V.tensor_tensor(e[:, :, 1, :], v[:, :, 1, :], ref, ALU.subtract))
                    s_e.on(V.tensor_tensor(e[:, :, 0, :], ref, v[:, :, 0, :], ALU.subtract))

                def operands(n):
                    b = 1 << n
                    sh_ = lambda ap: ap.rearrange("p (k i t) -> p k i t", i=2, t=b)
                    dve.wait_ge(s_ee.sem, n + 1)
                    if n >= 2:
                        dve.wait_ge(s_a.sem, n)
                    s_qk.on(V.tensor_tensor(sh_(Qb[n % 2])[:, :, 1, :], sh_(flat(q_b))[:, :, 1, :], sh_(E[n % 2])[:, :, 1, :], ALU.mult))
                    s_qk.on(V.tensor_tensor(sh_(Kb[n % 2])[:, :, 0, :], sh_(flat(kB))[:, :, 0, :], sh_(E[n % 2])[:, :, 0, :], ALU.mult))

                def mask(i):
                    u = ident if i == 0 else upper[i - 1]
                    dve.wait_ge(s_a.sem, i + 1)
                    b0 = (i % 2) * 2
                    dst = acc if i == 0 else masked[0]
                    if i >= 2:
                        dve.wait_ge(s_acc.sem, i - 1)
                    s_m.on(V.tensor_tensor(dst[:, 0:4, :], pair(bank[b0]), bc(u, 4), ALU.mult))
                    s_m.on(V.tensor_tensor(dst[:, 4:8, :], pair(bank[b0 + 1]), bc(u, 4), ALU.mult))

                exponents(0)
                for n in range(7):
                    if n + 1 < 7:
                        exponents(n + 1)
                    operands(n)
                    mask(n)
                mask(7)
                dve.wait_ge(s_qk.sem, 14)
                last = bcum[:, :, P - 1:P].broadcast_to([P, GH, P])
                ex = E[0][:, 0:GH * P].rearrange("p (h t) -> p h t", h=GH)
                s_e.on(V.tensor_tensor(ex, last, bcum[:, :, 0:P], ALU.subtract))
                dve.wait_ge(s_ee.sem, 9)
                dve.wait_ge(s_a.sem, 8)
                s_qk.on(V.tensor_tensor(Kb[0][:, 0:GH * P].rearrange("p (h t) -> p h t", h=GH), kB[:, :, 0:P], ex, ALU.mult))
                s_qk.on(V.tensor_tensor(Qb[0][:, 0:GH * P].rearrange("p (h t) -> p h t", h=GH), q_b[:, :, P:T2],
                                        E[0][:, GH * P:2 * GH * P].rearrange("p (h t) -> p h t", h=GH), ALU.mult))
                dve.wait_ge(s_a.sem, 9)
                s_m.on(V.tensor_copy(cross, pair(bank[4])))

            @block.scalar
            def _(act):
                for n in range(7):
                    act.wait_ge(s_e.sem, 2 * n + 2)
                    s_ee.on(S.activation(E[n % 2], E[n % 2], ACT.Exp))
                act.wait_ge(s_qk.sem, 14)
                s_ee.on(S.activation(E[0][:, GH * P:2 * GH * P].rearrange("p (h t) -> p h t", h=GH), bcum[:, :, P:T2], ACT.Exp))
                act.wait_ge(s_e.sem, 15)
                s_ee.on(S.activation(E[0][:, 0:GH * P], E[0][:, 0:GH * P], ACT.Exp))

            @block.gpsimd
            def _(pool):
                for i in range(1, 8):
                    pool.wait_ge(s_m.sem, 2 * i + 2)
                    if i >= 2:
                        pool.wait_ge(s_acc.sem, i - 1)
                    s_acc.on(G.tensor_tensor(acc, acc, masked[0], ALU.add))

            @block.tensor
            def _(pe):
                for i in range(8):
                    if i:
                        pe.wait_ge(s_qk.sem, 2 * i)
                    if i >= 2:
                        pe.wait_ge(s_m.sem, 2 * (i - 1))
                    for m in range(2 * GH):
                        k_, q_ = ((flat(kB), flat(q_b)) if i == 0 else (Kb[(i - 1) % 2], Qb[(i - 1) % 2]))
                        mm = T.matmul(bank[(i % 2) * 2 + m // 4][:, (m % 4) * P:(m % 4) * P + P], k_[:, m * P:m * P + P],
                                      q_[:, m * P:m * P + P], start=True, stop=True)
                    s_a.on(mm)
                pe.wait_ge(s_qk.sem, 16)
                for h in range(GH):
                    mm = T.matmul(bank[4][:, h * P:h * P + P], Kb[0][:, h * P:h * P + P], Qb[0][:, h * P:h * P + P],
                                  start=True, stop=True)
                s_a.on(mm)
                pe.wait_ge(s_acc.sem, 7)
                pe.wait_ge(s_m.sem, 17)
                for h in range(GH):
                    o = (h % 2) * T2
                    T.matmul(bank[6 + h // 2][:, o:o + P], itok[:, 2 * h, :], acc[:, 2 * h, :], start=True, stop=True)
                    T.matmul(bank[6 + h // 2][:, o + P:o + T2], itok[:, 2 * h, :], cross[:, h, :], start=True, stop=False)
                    mm = T.matmul(bank[6 + h // 2][:, o + P:o + T2], itok[:, 2 * h + 1, :], acc[:, 2 * h + 1, :], start=False, stop=True)
                s_a.on(mm)

            @block.scalar
            def _(act):
                act.wait_ge(s_a.sem, 10)
                for q in range(2):
                    act_s.on(S.activation(oB[:, 2 * q:2 * q + 2, :], two(bank[6 + q]), ACT.Copy))
        gated_norm(oB, wsq, E[0].rearrange("p (h t) -> p h t", h=GH), gate_b, lambda h: param("hg_norm_w_2", h),
                   o_all[:, GH:2 * GH, :], False)

        def mixer_out(engine, m, psum):
            return V.scalar_tensor_tensor(out=xT[:, m, :], in0=psum, scalar=mod[:, 2 * KD + m:2 * KD + m + 1], in1=xT[:, m, :],
                                          op0=ALU.mult, op1=ALU.add)
        project(o_all, T2, [(W_OUT2 + m // 4, (m % 4) * P, P) for m in range(KD)], mixer_out, W_OUT2, 2, owner=lambda m: "dve")
        expert_ready = [Signal(nc, ctx, f"expert_ready{i}") for i in range(ERING)]
        s_down = Signal(nc, ctx, "expert_done")
        s_gates = Signal(nc, ctx, "gates_stored")
        mm_ = Memory(sbuf, at2, end - 192)
        hB = mm_.take(KD, T2)
        wr = mm_.take(KD, NE)
        scores, sel, rep, tmp64 = (mm_.take(2, NE) for _ in range(4))
        top8 = mm_.take(2, 8, 8)
        gsum, rank = mm_.take(2, 8), mm_.take(2, 8)
        cmp, eqm = mm_.take(2, 8, 8), mm_.take(2, 8, 8)
        total_w = mm_.take(2)
        gatesT = mm_.take(T2)
        gb = mm_.take(ERING, T2)
        esig = mm_.take(2, 2 * T2)
        eprod = mm_.take(2 * T2)
        hid = mm_.take(2, 2, T2)
        sq2, rs2 = mm_.take(KD, T2), mm_.take(T2)
        zero = mm_.take(512)
        y_tok = mm_.take(2, D)
        wg_, wu_, wd_ = a["w_gate_2"][0], a["w_up_2"][0], a["w_down_2"][0]

        def expert_weights(k):
            at = k * EXPERT
            return view(at, KD, FE), view(at + KD * FE, KD, FE), view(at + 2 * KD * FE, FE // P, D)

        def load_expert(sp, k, gate, up, down):
            g_, u_, d_ = expert_weights(k)
            for dst, src in ((g_, gate), (u_, up), (d_, down)):
                sp.dma_start(dst, src.rearrange("(k p) c -> p k c", p=P)).then_inc(expert_ready[k].sem, 16)

        def load_gate_row(sp, k, row):
            sp.dma_start(gb[:, k, :], row.partition_broadcast(P)).then_inc(expert_ready[k].sem, 16)

        with nc.Block() as block:
            @block.sync
            def _(sp):
                small_in.on(sp.dma_start(wr, a["w_router_2"][0].rearrange("(k p) e -> p k e", p=P)), 16)
                load_expert(sp, 0, a["ws_gate_2"][0], a["ws_up_2"][0], a["ws_down_2"][0])
                for n in range(1, ERING):
                    load_expert(sp, n, wg_[n - 1], wu_[n - 1], wd_[n - 1])
        rms_norm(xT, hB, lambda j: gain2[:, j:j + 1], lambda j: mod[:, 3 * KD + j:3 * KD + j + 1], T2, sq2, rs2)
        lt8 = small[:, 192:256].rearrange("p (g j) -> p g j", j=8)
        with nc.Block() as block:
            @block.gpsimd
            def _(pool):
                pool.wait_ge(pool_s.sem, pool_s.on(G.memset(lt8, 1.0)))
                pool_s.on(G.affine_select(out=lt8, in_=lt8, compare_op=ALU.is_gt, fill=0.0, base=0,
                                          pattern=[[1, 8], [-1, 8]], channel_multiplier=0))

            @block.tensor
            def _(pe):
                pe.wait_ge(small_in.sem, small_in.value)
                for c in range(2):
                    for k in range(KD):
                        mm = T.matmul(bank[4][:, c * NE:c * NE + NE], hB[:, k, c * P:c * P + P], wr[:, k, :],
                                      start=(k == 0), stop=(k == KD - 1))
                pe_s.on(mm)

            @block.scalar
            def _(act):
                act.wait_ge(pe_s.sem, pe_s.value)
                act_s.on(S.activation(scores, bank[4][:, 0:2 * NE].rearrange("p (a b) -> p a b", b=NE), ACT.Sigmoid))

            @block.vector
            def _(dve):
                def step(instruction):
                    dve.wait_ge(dve_s.sem, dve_s.on(instruction))
                dve.wait_ge(act_s.sem, act_s.value)
                step(V.tensor_tensor(sel, scores, bc(small[:, 128:192], 2), ALU.add))
                for c in range(2):
                    for g in range(8):
                        last = V.max(top8[:, c, g, :], sel[:, c, 8 * g:8 * g + 8])
                        dve_s.on(last)
                dve.wait_ge(dve_s.sem, dve_s.value)
                step(V.tensor_tensor(gsum, top8[:, :, :, 0], top8[:, :, :, 1], ALU.add))
                for c in range(2):
                    mine = gsum[:, c, :].unsqueeze(2).broadcast_to([P, 8, 8])
                    other = gsum[:, c, :].unsqueeze(1).broadcast_to([P, 8, 8])
                    dve_s.on(V.tensor_tensor(cmp[:, c], other, mine, ALU.is_gt))
                    dve_s.on(V.tensor_tensor(eqm[:, c], other, mine, ALU.is_equal))
                dve.wait_ge(dve_s.sem, dve_s.value)
                dve.wait_ge(pool_s.sem, pool_s.value)
                for c in range(2):
                    dve_s.on(V.tensor_tensor(eqm[:, c], eqm[:, c], lt8, ALU.mult))
                dve.wait_ge(dve_s.sem, dve_s.value)
                step(V.tensor_tensor(cmp, cmp, eqm, ALU.add))
                step(V.tensor_reduce(rank, cmp, AX.X, ALU.add))
                step(V.tensor_scalar(rank, rank, 4.0, None, ALU.is_lt))
                for c in range(2):
                    grp = rank[:, c, :].unsqueeze(2).broadcast_to([P, 8, 8])
                    g8 = lambda ap: ap[:, c, :].rearrange("p (g e) -> p g e", e=8)
                    step(V.tensor_tensor(g8(sel), g8(sel), grp, ALU.mult))
                    step(V.tensor_scalar(g8(tmp64), grp, 1.0, -NEG, ALU.subtract, ALU.mult))
                    step(V.tensor_tensor(g8(sel), g8(sel), g8(tmp64), ALU.add))
                    step(V.max(top8[:, c, 0, :], sel[:, c, :]))
                    step(V.match_replace(out=rep[:, c, :], in_to_replace=top8[:, c, 0, :], in_values=sel[:, c, :], imm_value=-3e38))
                step(V.tensor_tensor(rep, rep, sel, ALU.not_equal))
                step(V.tensor_tensor(scores, scores, rep, ALU.mult))
                step(V.tensor_reduce(total_w, scores, AX.X, ALU.add))
                step(V.reciprocal(total_w, total_w))
                for c in range(2):
                    step(V.tensor_scalar(scores[:, c, :], scores[:, c, :], total_w[:, c:c + 1], 2.5, ALU.mult, ALU.mult))

            @block.tensor
            def _(pe):
                pe.wait_ge(dve_s.sem, dve_s.value)
                for c in range(2):
                    t = T.transpose(bank[5][0:NE, c * P:c * P + P], scores[:, c, :], ident)
                pe_s.on(t)

            @block.vector
            def _(dve):
                dve.wait_ge(pe_s.sem, pe_s.value)
                dve_s.on(V.tensor_copy(gatesT[0:NE, :], bank[5][0:NE, 0:T2]))
                dve_s.on(V.memset(zero, 0.0))

            @block.sync
            def _(sp):
                sp.wait_ge(dve_s.sem, dve_s.value - 1)
                s_gates.on(sp.dma_start(gates_dram, gatesT[0:NE, :]), 16)
                sp.wait_ge(s_gates.sem, 16)
                for n in range(1, ERING):
                    load_gate_row(sp, n, gates_dram[n - 1])

        s_gu2 = Signal(nc, ctx, "expert_gate_up")
        s_esig = Signal(nc, ctx, "expert_sigmoid")
        s_eprod = Signal(nc, ctx, "expert_product")
        s_ehid = Signal(nc, ctx, "expert_hidden")
        with nc.Block() as block:
            @block.sync
            def _(sp):
                def load(k, e, used):
                    sp.wait_ge(s_down.sem, used)
                    load_expert(sp, k, wg_[e], wu_[e], wd_[e])
                    load_gate_row(sp, k, gates_dram[e])
                with sp.Fori(0, NE // 4 - 1) as i:
                    for q in range(4):
                        load(q, i * 4 + (3 + q), i * 4 + (2 + q))
                load(0, NE - 1, NE - 2)

            @block.tensor
            def _(pe):
                def gate_up(k, par, ready, free):
                    g_, u_, _ = expert_weights(k)
                    pe.wait_ge(expert_ready[k].sem, ready)
                    if free is not None:
                        pe.wait_ge(s_ehid.sem, free)
                    for b, w in ((4 + 2 * par, g_), (5 + 2 * par, u_)):
                        for f in range(2):
                            for d in range(KD):
                                mm = T.matmul(bank[b][:, f * T2:f * T2 + T2], w[:, d, f * P:f * P + P], hB[:, d, :],
                                              start=(d == 0), stop=(d == KD - 1))
                    mm.then_inc(s_gu2.sem, 1)

                def down(k, par, hidden):
                    pe.wait_ge(s_ehid.sem, hidden)
                    w = expert_weights(k)[2]
                    for d in range(KD):
                        for f in range(2):
                            mm = T.matmul(bank[d // 2][:, (d % 2) * T2:(d % 2) * T2 + T2], w[:, f, d * P:d * P + P],
                                          hid[:, par, f, :], start=False, stop=False, skip_group_check=True)
                    mm.then_inc(s_down.sem, 1)

                for b in range(4):
                    mm = T.matmul(bank[b][:, :], ident, zero, start=True, stop=False, skip_group_check=True)
                mm.then_inc(s_down.sem, 1)
                gate_up(0, 0, 48, None)
                with pe.Fori(0, NE // 4) as i:
                    for q in range(4):
                        k = (1 + q) % 4
                        gate_up(k, (1 + q) % 2, i * 64 + (64 if k else 112), i * 4 + (1 + q))
                        down(q, q % 2, i * 4 + (2 + q))
                down(0, 0, NE + 2)

            @block.scalar
            def _(act):
                def sigmoid(par, ready, free):
                    act.wait_ge(s_gu2.sem, ready)
                    if free is not None:
                        act.wait_ge(s_ehid.sem, free)
                    S.activation(esig[:, par, :], bank[4 + 2 * par][:, :], ACT.Sigmoid).then_inc(s_esig.sem, 1)
                sigmoid(0, 1, None)
                with act.Fori(0, NE // 4) as i:
                    for q in range(4):
                        sigmoid((1 + q) % 2, i * 4 + (2 + q), i * 4 + (1 + q))

            @block.vector
            def _(dve):
                def product(par, ready, free):
                    dve.wait_ge(s_esig.sem, ready)
                    if free is not None:
                        dve.wait_ge(s_ehid.sem, free)
                    V.tensor_tensor(eprod, bank[4 + 2 * par][:, :], esig[:, par, :], ALU.mult).then_inc(s_eprod.sem, 1)

                def scaled(par, k, first, second, done):
                    dve.wait_ge(s_eprod.sem, first)
                    V.tensor_tensor(eprod, eprod, bank[5 + 2 * par][:, :], ALU.mult).then_inc(s_eprod.sem, 1)
                    dve.wait_ge(s_eprod.sem, second)
                    dve.wait_ge(s_down.sem, done)
                    V.tensor_tensor(hid[:, par], eprod.rearrange("p (f t) -> p f t", f=2),
                                    gb[:, k, :].unsqueeze(1).broadcast_to([P, 2, T2]), ALU.mult).then_inc(s_ehid.sem, 1)
                V.memset(eprod[:, 0:1], 0.0).then_inc(s_ehid.sem, 1)
                dve.wait_ge(s_ehid.sem, 1)
                product(0, 1, None)
                dve.wait_ge(s_eprod.sem, 1)
                V.tensor_tensor(hid[:, 0].rearrange("p f t -> p (f t)"), eprod, bank[5][:, :], ALU.mult).then_inc(s_ehid.sem, 1)
                with dve.Fori(0, NE // 4) as i:
                    for q in range(4):
                        product((1 + q) % 2, i * 4 + (2 + q), i * 4 + (2 + q))
                        scaled((1 + q) % 2, (1 + q) % 4, i * 8 + (2 + 2 * q), i * 8 + (3 + 2 * q), i * 4 + (1 + q))

        with nc.Block() as block:
            @block.vector
            def _(dve):
                for m in range(KD):
                    dve_s.on(V.scalar_tensor_tensor(out=xT[:, m, :], in0=bank[m // 2][:, (m % 2) * T2:(m % 2) * T2 + T2],
                                                    scalar=mod[:, 5 * KD + m:5 * KD + m + 1], in1=xT[:, m, :],
                                                    op0=ALU.mult, op1=ALU.add))
        rms_norm(xT, hB, lambda j: param("final_norm_w_2", j), None, T2, sq2, rs2)
        with nc.Block() as block:
            pe0 = pe_s.value

            @block.tensor
            def _(pe):
                for c in range(2):
                    for half in range(2):
                        for j in range(4):
                            t = T.transpose(bank[2 * c + half][:, j * P:j * P + P], hB[:, 4 * half + j, c * P:c * P + P], ident)
                        pe_s.on(t)

            @block.vector
            def _(dve):
                for i in range(0, 4, 2):
                    dve.wait_ge(pe_s.sem, pe0 + i + 1)
                    dve_s.on(V.tensor_copy(y_tok[:, i // 2, 0:512], bank[i][:, :]))

            @block.scalar
            def _(act):
                for i in range(1, 4, 2):
                    act.wait_ge(pe_s.sem, pe0 + i + 1)
                    act_s.on(S.activation(y_tok[:, i // 2, 512:D], bank[i][:, :], ACT.Copy))

            @block.sync
            def _(sp):
                for c in range(2):
                    sp.wait_ge(dve_s.sem, dve_s.value - 1 + c)
                    sp.wait_ge(act_s.sem, act_s.value - 1 + c)
                    stored.on(sp.dma_start(out[0, c * P:c * P + P, :], y_tok[:, c, :]), 16)
                sp.wait_ge(stored.sem, stored.value)


INPUTS = ["x", "meta_tokens", "norm_mix", "norm_ffn", "norm_final", "w_in", "mu_rw", "w0", "w_up", "a0", "a_up",
          "g_up", "k_k", "k_a", "r_k", "ln_x_w", "ln_x_b", "w_sb_out", "w_rw_out", "w_out", "w_ffn_in",
          "w_ffn_out", "c_2", "w_ada_2", "b_ada_2", "norm1_w_2", "w_in_2", "conv_w_2", "gdn_a_log_2",
          "gdn_dt_bias_2", "gdn_norm_w_2", "hg_lb_2", "hg_norm_w_2", "w_out_2", "norm2_w_2", "w_router_2",
          "router_bias_2", "w_gate_2", "w_up_2", "w_down_2", "ws_gate_2", "ws_up_2", "ws_down_2",
          "final_norm_w_2"]


def kernel(**inputs):
    import concourse.bacc as bacc
    from concourse.bass_utils import run_bass_kernel_spmd

    nc = bacc.Bacc("TRN2", target_bir_lowering=False, num_devices=1)
    arrays, aps = {}, {}
    for name in INPUTS:
        array = np.ascontiguousarray(inputs[name])
        arrays[f"in_{name}"] = array
        aps[name] = nc.dram_tensor(f"in_{name}", array.shape, mybir.dt.from_np(array.dtype), kind="ExternalInput").ap()
    out = nc.dram_tensor("out", (1, SEQ, D), F32, kind="ExternalOutput").ap()
    build(nc, aps, out)
    result = run_bass_kernel_spmd(nc, [arrays], core_ids=[0])
    return result.results[0]["out"]
```

```python
import numpy as np

import concourse.bass as bass
from concourse import mybir
from contextlib import ExitStack

F32 = mybir.dt.float32
F32R = mybir.dt.float32r
ALU = mybir.AluOpType
ACT = mybir.ActivationFunctionType
AX = mybir.AxisListType

P = 128
D = 1024
KD = D // P
N_META, SEQ = 16, 256
T1 = N_META + SEQ
T1P = 320
HEADS, DH = 8, 64
C = HEADS * DH
CT = C // P
CH = 64
NCH = T1P // CH
NM = NCH * HEADS
FFN = 2816
FT = FFN // P
T2 = SEQ
GH = 4
NE, FE = 64, 256
SLOT = 4096
RING = 3
PIECE = 2048
RAW = 6
GROWS = 4
SBUF_FLOATS = 53208
CONSTS = 5600

RMS_EPS = 1e-6
GN_EPS = 64e-5
NEG = -1e30


class Signal:

    def __init__(self, nc, ctx, name):
        self.sem = ctx.enter_context(nc.semaphore(name))
        self.value = 0

    def on(self, instruction, by=1):
        instruction.then_inc(self.sem, by)
        self.value += by
        return self.value


class Memory:

    def __init__(self, tensor, at, end):
        self.tensor, self.at, self.end = tensor, at, end

    def take(self, *shape):
        n = int(np.prod(shape))
        view = self.view(self.at, *shape)
        self.at += n
        assert self.at <= self.end, (self.at, self.end)
        return view

    def view(self, at, *shape):
        assert at + int(np.prod(shape)) <= self.end
        n = int(np.prod(shape))
        flat = self.tensor[:, at:at + n]
        if len(shape) == 1:
            return flat
        names = "abcd"[:len(shape)]
        spec = "p (" + " ".join(names) + ") -> p " + " ".join(names)
        return flat.rearrange(spec, **{k: v for k, v in zip(names, shape)})


def param_rows(groups):
    table, row = {}, 0
    for name, size in groups:
        n = -(-size // P)
        table[name] = (row, size)
        row += n
    assert row <= P
    return table


ROWS0 = param_rows([("norm_mix", D), ("norm_ffn", D), ("norm_final", D), ("mu_rw", 3 * C + 288), ("w0", C),
                    ("a0", C), ("k_k", C), ("k_a", C), ("r_k", C), ("ln_x_w", C), ("ln_x_b", C), ("c_2", D),
                    ("gdn_norm_w_2", P), ("hg_lb_2", 2 * C), ("hg_norm_w_2", C), ("norm1_w_2", D),
                    ("norm2_w_2", D), ("final_norm_w_2", D)])
ROWS1 = param_rows([("conv_w_2", 4 * 3 * C), ("b_ada_2", 6 * D)])


def build(nc, a, out):
    ctx = ExitStack()
    with ctx:
        kept = ctx.enter_context(nc.sbuf_tensor("kept", [P, CONSTS + KD * T1], F32))
        total = SBUF_FLOATS - CONSTS - KD * T1 - RING * SLOT
        ring_stack = ExitStack()
        ring = ring_stack.enter_context(nc.sbuf_tensor("weight_ring", [P, RING, SLOT], F32))
        arena = ExitStack()
        sbuf = arena.enter_context(nc.sbuf_tensor("mixer1_memory", [P, total], F32))
        bank = [ctx.enter_context(nc.psum_tensor(f"bank{i}", [P, 512], F32)) for i in range(8)]
        gates_dram = nc.dram_tensor("gates_scratch", [NE, T2], F32, kind="Internal").ap()

        mem = Memory(kept, 0, CONSTS)
        view = Memory(sbuf, 0, total).view

        ident = mem.take(P)
        ones = mem.take(P)
        blk64 = mem.take(P)
        tri = mem.take(P)
        ATT = T1 + (T1 - P) + (T1 - 2 * P)
        keep = mem.take(ATT)
        drop = mem.take(ATT)
        rw_mask = mem.take(P)
        upper = [mem.take(P) for _ in range(7)]
        lower = [mem.take(P) for _ in range(7)]
        upper_strict, upper_incl = mem.take(P), mem.take(P)
        reset64 = mem.take(T1P)
        reset128 = mem.take(T2)
        eps_rms, eps_gn, one_col = mem.take(1), mem.take(1), mem.take(1)
        vec0, vec1 = mem.take(P), mem.take(P)
        row_sel = mem.take(GH, P)
        small = mem.take(256)
        mod = mem.take(6 * KD)
        csil = mem.take(KD, 1)
        gain1, gain2 = mem.take(KD), mem.take(KD)
        e_hg, lb, lb1 = mem.take(2 * GH), mem.take(GH), mem.take(GH)
        base = 0

        def param(name, i=0):
            if name in ROWS0:
                r = ROWS0[name][0] + i
                return vec0[:, r:r + 1]
            r = ROWS1[name][0] + i
            return vec1[:, r:r + 1]

        pe_s = Signal(nc, ctx, "tensor_done")
        act_s = Signal(nc, ctx, "scalar_done")
        dve_s = Signal(nc, ctx, "vector_done")
        pool_s = Signal(nc, ctx, "gpsimd_done")
        small_in = Signal(nc, ctx, "small_loads")
        tokens_in = Signal(nc, ctx, "token_loads")
        stored = Signal(nc, ctx, "stored")
        slot_ready = [Signal(nc, ctx, f"slot_ready{i}") for i in range(RING)]
        V, S, G, T = nc.vector, nc.scalar, nc.gpsimd, nc.tensor

        def columns(w, a0, a1):
            return [(w[:, a0:a1].rearrange("(k p) c -> p k c", p=P), 0, a1 - a0)]

        plan = []
        w_in, w_in2 = a["w_in"][0], a["w_in_2"][0]
        edges = [0, 512, 1024, 1536, 2048, 2560, 3072, 3360, 3872, 4384, 4896, 5408]
        for c0, c1 in zip(edges, edges[1:]):
            plan.append((KD, c1 - c0, columns(w_in, c0, c1)))
        SB_OUT = len(plan)
        plan.append((CT, D, columns(a["w_sb_out"][0], 0, D)))
        plan.append((CT, D, columns(a["w_rw_out"][0], 0, D)))
        W_OUT = len(plan)
        for n in range(2):
            plan.append((KD, 512, columns(a["w_out"][0], 512 * n, 512 * n + 512)))
        FFN_IN = len(plan)
        wf = a["w_ffn_in"][0]
        for n in range(FT // 2):
            plan.append((KD, 512, [(wf[:, s + 256 * n:s + 256 * n + 256].rearrange("(k p) c -> p k c", p=P), o, 256)
                                   for s, o in ((0, 0), (FFN, 256))]))
        FFN_OUT = len(plan)
        for n in range(0, FT, 4):
            rows = min(4, FT - n)
            plan.append((rows, D, [(a["w_ffn_out"][0][n * P:(n + rows) * P, :].rearrange("(k p) c -> p k c", p=P), 0, D)]))
        W_IN2 = len(plan)
        edges2 = [0, 512, 1024, 1536, 2048]
        for c0 in [0, 512, 1024, 1536, 2056, 2568, 3080, 3592]:
            plan.append((KD, 512, columns(w_in2, c0, c0 + 512)))
        W_OUT2 = len(plan)
        for n in range(2):
            plan.append((KD, 512, columns(a["w_out_2"][0], 512 * n, 512 * n + 512)))

        ready_at, counts = [], [0] * RING
        for n, (_, _, parts) in enumerate(plan):
            counts[n % RING] += 16 * len(parts)
            ready_at.append(counts[n % RING])
        slot_freed = {}
        issued = [0]

        def slot(n):
            rows, width, _ = plan[n]
            return ring[:, n % RING, 0:rows * width].rearrange("p (k c) -> p k c", k=rows)

        def load_slots(sp, upto):
            while issued[0] < min(upto, len(plan)):
                n = issued[0]
                if n >= RING:
                    done, by = slot_freed[n - RING]
                    sp.wait_ge(done.sem, by)
                for src, c0, w in plan[n][2]:
                    slot_ready[n % RING].on(sp.dma_start(slot(n)[:, :, c0:c0 + w], src), 16)
                issued[0] += 1

        def await_slot(pe, n):
            pe.wait_ge(slot_ready[n % RING].sem, ready_at[n])

        tok = view(base, 3, D)
        rows0 = view(base + 3 * D, P)
        rows1 = view(base + 3 * D + P, P)
        top = total
        hT = Memory(kept, CONSTS, CONSTS + KD * T1).take(KD, T1)
        wa_up = view(top - C, C)
        g_up0 = view(top - 2 * C, C)
        g_up1 = view(top - 3 * C, C)
        top -= 3 * C
        NT_TOK = [P, P, T1 - 2 * P]
        with nc.Block() as block:
            @block.vector
            def _(dve):
                cleared = dve_s.on(V.memset(rows0, 0.0))
                cleared = dve_s.on(V.memset(rows1, 0.0))
                tri0 = dve_s.on(V.memset(eps_rms, RMS_EPS))
                dve_s.on(V.memset(eps_gn, GN_EPS))
                dve_s.on(V.memset(one_col, 1.0))

            @block.sync
            def _(sp):
                sp.wait_ge(dve_s.sem, 2)
                for table, rows in ((ROWS0, rows0), (ROWS1, rows1)):
                    for name, (row, size) in table.items():
                        src = a[name]
                        names = "abcd"[:len(src.shape)]
                        flat = src.rearrange(" ".join(names) + " -> (" + " ".join(names) + ")") if len(names) > 1 else src
                        n = size // P
                        small_in.on(sp.dma_start(rows[row:row + n, :], flat[0:n * P].rearrange("(r c) -> r c", c=P)), 16)
                        if size % P:
                            small_in.on(sp.dma_start(rows[row + n:row + n + 1, 0:size % P],
                                                     flat[n * P:size].rearrange("(r c) -> r c", r=1)), 16)
                small_in.on(sp.dma_start(wa_up[0:64, :], a["w_up"][0]), 16)
                small_in.on(sp.dma_start(wa_up[64:128, :], a["a_up"][0]), 16)
                small_in.on(sp.dma_start(g_up0, a["g_up"][0][0:P, :]), 16)
                small_in.on(sp.dma_start(g_up1[0:32, :], a["g_up"][0][P:P + 32, :]), 16)
                wba = w_in2[:, 2048:2056].rearrange("(k p) c -> p k c", p=P)
                small_in.on(sp.dma_start(small[:, 0:64].rearrange("p (k c) -> p k c", c=8), wba), 16)
                small_in.on(sp.dma_start(small[0:GH, 64:65], a["gdn_a_log_2"].rearrange("a h -> h a")), 16)
                small_in.on(sp.dma_start(small[0:GH, 65:66], a["gdn_dt_bias_2"].rearrange("a h -> h a")), 16)
                small_in.on(sp.dma_start(small[:, 128:192], a["router_bias_2"].partition_broadcast(P).rearrange("p a e -> p (a e)")), 16)
                load_slots(sp, RING)

            @block.scalar
            def _(act):
                x = a["x"][0]
                tokens_in.on(act.dma_start(tok[0:N_META, 0, :], a["meta_tokens"]), 16)
                tokens_in.on(act.dma_start(tok[N_META:P, 0, :], x[0:P - N_META, :]), 16)
                tokens_in.on(act.dma_start(tok[:, 1, :], x[P - N_META:2 * P - N_META, :]), 16)
                tokens_in.on(act.dma_start(tok[0:T1 - 2 * P, 2, :], x[2 * P - N_META:SEQ, :]), 16)

            @block.gpsimd
            def _(pool):
                def step(instruction):
                    pool.wait_ge(pool_s.sem, pool_s.on(instruction))

                def fill(ap, value):
                    step(G.memset(ap, value))

                def select(ap, pattern, base_, cm, op, fill_=0.0):
                    step(G.affine_select(out=ap, in_=ap, compare_op=op, fill=fill_, base=base_,
                                         pattern=pattern, channel_multiplier=cm))
                fill(ident, 0.0)
                select(ident, [[-1, P]], 0, 1, ALU.not_equal, 1.0)
                fill(ones, 1.0)
                fill(blk64, 0.0)
                fill(blk64[0:64, 0:64], 1.0)
                fill(blk64[64:128, 64:128], 1.0)
                consts_ready = pool_s.value
                fill(tri, 1.0)
                select(tri, [[-1, P]], 0, 1, ALU.is_ge)
                fill(keep, 1.0)
                fill(drop, 0.0)
                at = 0
                for i in range(3):
                    n = T1 - i * P
                    select(keep[:, at:at + n], [[1, n]], 0, -1, ALU.is_gt)
                    select(drop[:, at:at + n], [[1, n]], 0, -1, ALU.is_gt, NEG)
                    at += n
                fill(rw_mask, 1.0)
                scratch = row_sel[:, 0, :]
                fill(scratch, 1.0)
                select(rw_mask[:, 0:64], [[1, 64]], 0, -1, ALU.is_gt)
                select(rw_mask[:, 64:128], [[1, 64]], 0, -1, ALU.is_ge)
                select(scratch[:, 0:64], [[1, 64]], 64, -1, ALU.is_gt)
                select(scratch[:, 64:128], [[1, 64]], 64, -1, ALU.is_ge)
                select(scratch, [[0, P]], -64, 1, ALU.is_ge)
                step(G.tensor_tensor(rw_mask, rw_mask, scratch, ALU.add))
                for n in range(7):
                    b = 1 << n
                    u = upper[n].rearrange("p (k c) -> p k c", c=2 * b)
                    fill(upper[n], 0.0)
                    fill(u[:, :, b:2 * b], 1.0)
                    select(u, [[-2 * b, P // (2 * b)], [0, 2 * b]], 0, 1, ALU.is_ge)
                    select(u, [[2 * b, P // (2 * b)], [0, 2 * b]], b - 1, -1, ALU.is_ge)
                    w = lower[n].rearrange("p (k c) -> p k c", c=2 * b)
                    fill(lower[n], 0.0)
                    fill(w[:, :, 0:b], 1.0)
                    select(w, [[-2 * b, P // (2 * b)], [0, 2 * b]], -b, 1, ALU.is_ge)
                    select(w, [[2 * b, P // (2 * b)], [0, 2 * b]], 2 * b - 1, -1, ALU.is_ge)
                fill(upper_strict, 1.0)
                select(upper_strict, [[1, P]], 0, -1, ALU.is_gt)
                fill(upper_incl, 1.0)
                select(upper_incl, [[1, P]], 0, -1, ALU.is_ge)
                fill(reset64, 1.0)
                fill(reset64.rearrange("p (k c) -> p k c", c=CH)[:, :, 0:1], 0.0)
                fill(reset128, 1.0)
                fill(reset128.rearrange("p (k c) -> p k c", c=P)[:, :, 0:1], 0.0)
                fill(row_sel, 0.0)
                select(row_sel, [[-1, GH], [0, P]], 0, 1, ALU.not_equal, 1.0)

            @block.tensor
            def _(pe):
                pe.wait_ge(pool_s.sem, 2)
                pe.wait_ge(tokens_in.sem, tokens_in.value)
                for j in range(KD):
                    for i, n in enumerate(NT_TOK):
                        t = T.transpose(bank[j][:, i * P:i * P + n], tok[0:n, i, j * P:j * P + P], ident[0:n, 0:n])
                    pe_s.on(t)
                pe.wait_ge(small_in.sem, small_in.value)
                pe.wait_ge(act_s.sem, 1)
                T.transpose(bank[0][:, 0:P], rows0, ident)
                pe_s.on(T.transpose(bank[0][:, P:2 * P], rows1, ident))

            @block.scalar
            def _(act):
                for j in range(0, KD, 2):
                    act.wait_ge(pe_s.sem, j + 1)
                    act_s.on(S.activation(hT[:, j, :], bank[j][:, 0:T1], ACT.Copy))

            @block.vector
            def _(dve):
                for j in range(1, KD, 2):
                    dve.wait_ge(pe_s.sem, j + 1)
                    dve_s.on(V.tensor_copy(hT[:, j, :], bank[j][:, 0:T1]))
                dve.wait_ge(pe_s.sem, KD + 1)
                dve_s.on(V.tensor_copy(vec0, bank[0][:, 0:P]))
                dve_s.on(V.tensor_copy(vec1, bank[0][:, P:2 * P]))

        def rms_norm(src, dst, gain, shift, n, square, rstd, width=KD, mean=1.0 / D):
            with nc.Block() as block:
                @block.vector
                def _(dve):
                    squared = dve_s.on(V.tensor_tensor(square, src, src, ALU.mult))

                @block.tensor
                def _(pe):
                    pe.wait_ge(dve_s.sem, dve_s.value)
                    for j in range(width):
                        m = T.matmul(bank[0][:, 0:n], ones, square[:, j, :], start=(j == 0), stop=(j == width - 1))
                    pe_s.on(m)

                @block.scalar
                def _(act):
                    act.wait_ge(pe_s.sem, pe_s.value)
                    act_s.on(S.activation(rstd, bank[0][:, 0:n], ACT.Sqrt, bias=eps_rms, scale=mean))

                @block.vector
                def _(dve):
                    dve.wait_ge(act_s.sem, act_s.value)
                    dve.wait_ge(dve_s.sem, dve_s.on(V.reciprocal(rstd, rstd)))
                    for j in range(width):
                        done = dve_s.on(V.scalar_tensor_tensor(out=dst[:, j, :], in0=src[:, j, :], scalar=gain(j),
                                                               in1=rstd, op0=ALU.mult, op1=ALU.mult))
                    if shift is not None:
                        dve.wait_ge(dve_s.sem, done)
                        for j in range(width):
                            dve_s.on(V.tensor_scalar(dst[:, j, :], dst[:, j, :], shift(j), None, ALU.add))

        def project(x, n, tiles, evacuate, first_slot, n_slots, owner=lambda m: ("act", "dve")[m % 2]):
            pe0 = pe_s.value
            emptied, value = [], {"act": act_s.value, "dve": dve_s.value}
            for m in range(len(tiles)):
                value[owner(m)] += 1
                emptied.append((act_s if owner(m) == "act" else dve_s, value[owner(m)]))
            with nc.Block() as block:
                @block.tensor
                def _(pe):
                    seen = None
                    for m, (s, c0, w) in enumerate(tiles):
                        if s != seen:
                            await_slot(pe, s)
                            seen = s
                        if m >= 8:
                            done, by = emptied[m - 8]
                            pe.wait_ge(done.sem, by)
                        weights = slot(s)
                        rows = plan[s][0]
                        for k in range(rows):
                            mm = T.matmul(bank[m % 8][0:w, 0:n], weights[:, k, c0:c0 + w], x[:, k, :],
                                          start=(k == 0), stop=(k == rows - 1))
                        slot_freed[s] = pe_s, pe_s.on(mm)

                @block.sync
                def _(sp):
                    load_slots(sp, first_slot + n_slots + RING)

                @block.scalar
                def _(act):
                    for m in (m for m in range(len(tiles)) if owner(m) == "act"):
                        act.wait_ge(pe_s.sem, pe0 + m + 1)
                        act_s.on(evacuate(act, m, bank[m % 8][0:tiles[m][2], 0:n]))

                @block.vector
                def _(dve):
                    for m in (m for m in range(len(tiles)) if owner(m) == "dve"):
                        dve.wait_ge(pe_s.sem, pe0 + m + 1)
                        dve_s.on(evacuate(dve, m, bank[m % 8][0:tiles[m][2], 0:n]))

        def copy_out(dst):
            def evacuate(engine, m, psum):
                if engine is S:
                    return S.activation(dst(m), psum, ACT.Copy)
                return V.tensor_copy(dst(m), psum)
            return evacuate

        m1 = Memory(sbuf, base, top)
        xnT = m1.take(KD, T1)
        g_in = m1.take(2, T1)
        y_sb = m1.take(CT, T1)
        y_rw = m1.take(CT, T1)
        after_mixer = m1.at
        qT = m1.take(CT, T1)
        kT = m1.take(CT, 3 * P)
        vT = m1.take(CT, T1)
        raw = view(top - 15 * (1 + T1), 15, 1 + T1)
        att_at = m1.at
        rms_norm(hT, xnT, lambda j: param("norm_mix", j), None, T1, view(att_at, KD, T1), view(att_at + KD * T1, T1))

        tiles = [(m // 4, (m % 4) * P, P) for m in range(24)] + [(6, 0, P), (6, P, P), (6, 2 * P, 32)]

        def put_in(engine, m, psum):
            w = tiles[m][2]
            if m < 4:
                if engine is nc.scalar:
                    return S.activation(qT[:, m, :], psum, ACT.Copy, scale=DH ** -0.5)
                return V.tensor_scalar(qT[:, m, :], psum, DH ** -0.5, None, ALU.mult)
            dst = (kT[:, m - 4, 0:T1] if m < 8 else vT[:, m - 8, :] if m < 12
                   else raw[0:w, m - 12, 1:1 + T1])
            if engine is nc.scalar:
                return S.activation(dst, psum, ACT.Copy)
            return V.tensor_copy(dst, psum)

        with nc.Block() as block:
            @block.gpsimd
            def _(pool):
                for ap in (kT[:, :, T1:3 * P], raw[:, :, 0:1], raw[32:64, 14, :], raw[64:128, 14, :]):
                    pool.wait_ge(pool_s.sem, pool_s.on(G.memset(ap, 0.0)))
        project(xnT, T1, tiles, put_in, 0, 7)

        SEG = [(0, 0, T1), (T1, P, T1 - P), (2 * T1 - P, 2 * P, T1 - 2 * P)]
        ma = Memory(sbuf, att_at, top - 15 * (1 + T1))
        v_tok = ma.take(3, C)
        zs = [ma.take(ATT) for _ in range(2)]
        zm = [ma.take(ATT) for _ in range(2)]
        ab = [ma.take(ATT) for _ in range(2)]
        sp_ = [ma.take(ATT) for _ in range(2)]
        att = [ma.take(ATT) for _ in range(2)]
        with nc.Block() as block:
            @block.gpsimd
            def _(pool):
                pool_s.on(G.memset(v_tok[:, 2, :], 0.0))

            @block.tensor
            def _(pe):
                for i, n in enumerate(NT_TOK):
                    for j in range(CT):
                        t = T.transpose(bank[i][0:n, j * P:j * P + P], vT[:, j, i * P:i * P + n], ident)
                    pe_s.on(t)

            @block.vector
            def _(dve):
                dve.wait_ge(pool_s.sem, pool_s.value)
                for i, n in enumerate(NT_TOK):
                    dve.wait_ge(pe_s.sem, pe_s.value - 2 + i)
                    dve_s.on(V.tensor_copy(v_tok[0:n, i, :], bank[i][0:n, :]))

        s_z = Signal(nc, ctx, "scores_ready")
        s_zs = Signal(nc, ctx, "scores_copied")
        s_abs = Signal(nc, ctx, "abs_scores")
        s_exp = Signal(nc, ctx, "exp_abs")
        s_ln = Signal(nc, ctx, "log_term")
        s_sp = Signal(nc, ctx, "softplus_ready")
        s_c = Signal(nc, ctx, "suffix_sums")
        s_la = Signal(nc, ctx, "log_weights")
        s_att = Signal(nc, ctx, "weights_ready")
        s_y = Signal(nc, ctx, "head_out")
        s_zm = Signal(nc, ctx, "masked_scores")
        s_ycopy = Signal(nc, ctx, "head_out_copied")
        with nc.Block() as block:
            @block.tensor
            def _(pe):
                def scores(h):
                    b = h % 2
                    lo = DH * (h % 2)
                    if h >= 2:
                        pe.wait_ge(s_sp.sem, 2 * (h - 1))
                    for i, (c, q0, n) in enumerate(SEG):
                        m = T.matmul(bank[b][:, c:c + n], kT[lo:lo + DH, h // 2, i * P:i * P + P],
                                     qT[lo:lo + DH, h // 2, q0:q0 + n], start=True, stop=True)
                    s_z.on(m)

                def rest(h):
                    b = h % 2
                    lo = DH * (h % 2)
                    pe.wait_ge(s_sp.sem, 2 * h + 2)
                    if h >= 2:
                        pe.wait_ge(s_la.sem, h - 1)
                    for i in range(3):
                        c, q0, n = SEG[i]
                        T.matmul(bank[2 + b][:, c:c + n], tri, sp_[b][:, c:c + n], start=True, stop=(i == 2))
                        for i2 in range(i + 1, 3):
                            c2, q2, n2 = SEG[i2]
                            o = c + q2 - q0
                            m = T.matmul(bank[2 + b][:, o:o + n2], ones, sp_[b][:, c2:c2 + n2],
                                         start=False, stop=(i2 == 2))
                    s_c.on(T.matmul(bank[6][:, 0:1], ones, one_col, start=True, stop=True))

                def out_(h):
                    b = h % 2
                    lo = DH * (h % 2)
                    pe.wait_ge(s_att.sem, h + 1)
                    if h >= 2:
                        pe.wait_ge(s_ycopy.sem, h - 1)
                    for i, (c, q0, n) in enumerate(SEG):
                        m = T.matmul(bank[4 + b][lo:lo + DH, q0:T1], v_tok[:, i, h * DH:h * DH + DH],
                                     att[b][:, c:c + n], start=(i == 0), stop=(i == 2))
                    s_y.on(m)

                scores(0)
                for h in range(HEADS):
                    if h + 1 < HEADS:
                        scores(h + 1)
                    rest(h)
                    if h >= 1:
                        out_(h - 1)
                out_(HEADS - 1)

            @block.scalar
            def _(act):
                def first(h):
                    b = h % 2
                    act.wait_ge(s_z.sem, h + 1)
                    if h >= 2:
                        act.wait_ge(s_la.sem, h - 1)
                        act.wait_ge(s_sp.sem, 2 * (h - 1))
                    s_zs.on(S.activation(zs[b], bank[b][:, 0:ATT], ACT.Copy))
                    s_abs.on(S.activation(ab[b], bank[b][:, 0:ATT], ACT.Abs))
                    act.wait_ge(s_abs.sem, h + 1)
                    s_exp.on(S.activation(ab[b], ab[b], ACT.Exp, scale=-1.0))
                    act.wait_ge(s_exp.sem, h + 1)
                    s_ln.on(S.activation(ab[b], ab[b], ACT.Ln, bias=one_col))

                def second(h):
                    b = h % 2
                    act.wait_ge(s_la.sem, h + 1)
                    if h >= 2:
                        act.wait_ge(s_y.sem, h - 1)
                    s_att.on(S.activation(att[b], zm[b], ACT.Exp))

                first(0)
                for h in range(HEADS):
                    if h + 1 < HEADS:
                        first(h + 1)
                    second(h)

            @block.gpsimd
            def _(pool):
                for h in range(HEADS):
                    b = h % 2
                    pool.wait_ge(s_zs.sem, h + 1)
                    if h >= 2:
                        pool.wait_ge(s_att.sem, h - 1)
                    s_zm.on(G.tensor_tensor(zm[b], zs[b], drop, ALU.add))

            @block.vector
            def _(dve):
                def first(h):
                    b = h % 2
                    dve.wait_ge(s_ln.sem, h + 1)
                    if h >= 2:
                        dve.wait_ge(s_c.sem, h - 1)
                    s_sp.on(V.scalar_tensor_tensor(out=sp_[b], in0=bank[b][:, 0:ATT], scalar=0.0, in1=ab[b],
                                                   op0=ALU.max, op1=ALU.add))
                    dve.wait_ge(s_sp.sem, 2 * h + 1)
                    s_sp.on(V.tensor_tensor(sp_[b], sp_[b], keep, ALU.mult))

                def second(h):
                    b = h % 2
                    dve.wait_ge(s_c.sem, h + 1)
                    dve.wait_ge(s_zm.sem, h + 1)
                    s_la.on(V.tensor_tensor(zm[b], zm[b], bank[2 + b][:, 0:ATT], ALU.subtract))

                def third(h):
                    lo = DH * (h % 2)
                    dve.wait_ge(s_y.sem, h + 1)
                    s_ycopy.on(V.tensor_copy(y_sb[lo:lo + DH, h // 2, :], bank[4 + h % 2][lo:lo + DH, 0:T1]))

                first(0)
                for h in range(HEADS):
                    if h + 1 < HEADS:
                        first(h + 1)
                    second(h)
                    if h >= 1:
                        third(h - 1)
                third(HEADS - 1)
        A0 = after_mixer
        mr = Memory(sbuf, A0, top - 15 * (1 + T1))
        vS = mr.take(CT, CH + T1P)
        rk = mr.take(CT, T1)
        Q2 = mr.take(CT, NCH, 2, CH)
        at_K2 = mr.at
        K2 = mr.take(CT, NCH, 2, CH)
        at_K2tok = mr.at
        sh = mr.take(9, T1)
        c_sum = mr.take(CT, T1P)
        e_pos = mr.take(CT, T1P)
        e_neg = mr.take(CT, T1P)
        rate = mr.take(CT, T1)
        kk = mr.take(CT, T1)
        work = mr.take(CT, T1)
        ld = view(top - 15 * (1 + T1), CT, T1P)
        grow = view(top - 15 * (1 + T1) + CT * T1P, CT, T1)
        chunks = lambda ap, n: ap[:, :, 0:n * CH].rearrange("p j (c t) -> p j c t", t=CH)

        marks = {}
        with nc.Block() as block:
            @block.gpsimd
            def _(pool):
                for ap in (vS[:, :, 0:CH], vS[:, :, CH + T1:CH + T1P], Q2[:, :, NCH - 1, :, :], K2[:, :, NCH - 1, :, :]):
                    pool.wait_ge(pool_s.sem, pool_s.on(G.memset(ap, 0.0)))

            @block.vector
            def _(dve):
                for first, count, dst in ((0, 4, lambda j: sh[:, j, :]), (4, 4, lambda j: sh[:, 4 + j, :]),
                                          (8, 4, lambda j: vS[:, j, CH:CH + T1]),
                                          (12, 3, lambda j: sh[:, 8, :] if j == 0 else g_in[:, j - 1, :])):
                    diff = work if first % 8 == 0 else kk
                    if first >= 8:
                        dve.wait_ge(dve_s.sem, dve_s.value - 4)
                    cur = raw[:, first:first + count, 1:1 + T1]
                    n = dve_s.on(V.tensor_tensor(diff[:, 0:count, :], raw[:, first:first + count, 0:T1], cur, ALU.subtract))
                    dve.wait_ge(dve_s.sem, n)
                    for j in range(count):
                        dve_s.on(V.scalar_tensor_tensor(out=dst(j), in0=diff[:, j, :], scalar=param("mu_rw", first + j),
                                                        in1=raw[:, first + j, 1:1 + T1], op0=ALU.mult, op1=ALU.add))

            @block.scalar
            def _(act):
                act.wait_ge(dve_s.sem, dve_s.value)
                act_s.on(S.activation(sh[0:64, 8, :], sh[0:64, 8, :], ACT.Tanh))
                n = act_s.on(S.activation(g_in, g_in, ACT.Sigmoid))

            @block.tensor
            def _(pe):
                pe.wait_ge(act_s.sem, act_s.value - 1)
                for m in range(CT):
                    pe_s.on(T.matmul(bank[m][:, 0:T1], wa_up[0:64, m * P:m * P + P], sh[0:64, 8, :], start=True, stop=True))
                for m in range(CT):
                    pe_s.on(T.matmul(bank[4 + m][:, 0:T1], wa_up[64:128, m * P:m * P + P], sh[64:128, 8, :], start=True, stop=True))

            @block.scalar
            def _(act):
                for m in range(CT):
                    act.wait_ge(pe_s.sem, pe_s.value - 7 + m)
                    act_s.on(S.activation(ld[:, m, 0:T1], bank[m][:, 0:T1], ACT.Sigmoid, bias=param("w0", m)))
                for m in range(CT):
                    act.wait_ge(pe_s.sem, pe_s.value - 3 + m)
                    act_s.on(S.activation(rate[:, m, :], bank[4 + m][:, 0:T1], ACT.Sigmoid, bias=param("a0", m)))

            @block.vector
            def _(dve):
                dve.wait_ge(dve_s.sem, dve_s.value)
                for j in range(CT):
                    n = dve_s.on(V.tensor_scalar(kk[:, j, :], sh[:, 4 + j, :], param("k_k", j), None, ALU.mult))
                dve.wait_ge(dve_s.sem, n)
                marks["squares"] = dve_s.on(V.tensor_tensor(work, kk, kk, ALU.mult))
                dve.wait_ge(act_s.sem, act_s.value - 4)
                dve_s.on(V.memset(ld[:, :, T1:T1P], 0.0))
                n = dve_s.on(V.tensor_scalar(ld[:, :, 0:T1], ld[:, :, 0:T1], -float(np.exp(-0.5)), None, ALU.mult))
                dve.wait_ge(dve_s.sem, n)
                for j in range(CT):
                    n = dve_s.on(V.tensor_tensor_scan(c_sum[:, j, :], reset64, ld[:, j, :], 0.0, ALU.mult, ALU.add))
                dve.wait_ge(dve_s.sem, n)
                sums = dve_s.on(V.tensor_tensor(ld, c_sum, ld, ALU.subtract))

            @block.tensor
            def _(pe):
                pe.wait_ge(dve_s.sem, marks["squares"])
                pe.wait_ge(act_s.sem, act_s.value - 4)
                for j in range(CT):
                    pe_s.on(T.matmul(bank[j][:, 0:T1], blk64, work[:, j, :], start=True, stop=True))

            @block.scalar
            def _(act):
                act.wait_ge(dve_s.sem, dve_s.value)
                act_s.on(S.activation(e_pos, c_sum, ACT.Exp))
                act_s.on(S.activation(e_neg, c_sum, ACT.Exp, scale=-1.0))
                act_s.on(S.activation(ld, ld, ACT.Exp))

            @block.vector
            def _(dve):
                exps = act_s.value
                rates = exps - 3
                for j in range(CT):
                    dve.wait_ge(pe_s.sem, pe_s.value - 3 + j)
                    n = dve_s.on(V.tensor_scalar(grow[:, j, :], bank[j][:, 0:T1], 1e-24, None, ALU.max))

            @block.scalar
            def _(act):
                act.wait_ge(dve_s.sem, dve_s.value)
                act_s.on(S.activation(grow, grow, ACT.Sqrt))

            @block.vector
            def _(dve):
                dve.wait_ge(act_s.sem, act_s.value)
                dve.wait_ge(dve_s.sem, dve_s.on(V.reciprocal(grow, grow)))
                dve.wait_ge(dve_s.sem, dve_s.on(V.tensor_tensor(kk, kk, grow, ALU.mult)))
                for j in range(CT):
                    n = dve_s.on(V.tensor_scalar(work[:, j, :], rate[:, j, :], -1.0, param("k_a", j), ALU.add, ALU.mult))
                dve.wait_ge(dve_s.sem, n)
                dve.wait_ge(dve_s.sem, dve_s.on(V.scalar_tensor_tensor(out=work, in0=work, scalar=1.0, in1=sh[:, 4:8, :],
                                                                      op0=ALU.add, op1=ALU.mult)))
                for j in range(CT):
                    dve_s.on(V.scalar_tensor_tensor(out=rk[:, j, :], in0=sh[:, j, :], scalar=param("r_k", j),
                                                    in1=work[:, j, :], op0=ALU.mult, op1=ALU.mult))
                dve.wait_ge(dve_s.sem, dve_s.on(V.tensor_tensor(rate, rate, kk, ALU.mult)))
                tail = T1 - (NCH - 1) * CH
                for dst, i, x, e in ((Q2, 0, kk, ld), (Q2, 1, sh[:, 0:4, :], e_pos), (K2, 0, rate, e_neg), (K2, 1, work, e_neg)):
                    dve_s.on(V.tensor_tensor(dst[:, :, 0:NCH - 1, i, :], chunks(x, NCH - 1), chunks(e, NCH - 1), ALU.mult))
                    dve.wait_ge(pool_s.sem, pool_s.value)
                    dve_s.on(V.tensor_tensor(dst[:, :, NCH - 1, i, 0:tail], x[:, :, T1 - tail:T1], e[:, :, T1 - tail:T1], ALU.mult))

        mi = Memory(sbuf, at_K2tok, top)
        K2tok = mi.take(NCH * CT, P)
        O = mi.take(NM, P)
        at_L = mi.at
        L = mi.take(NM, CH)
        LM = mi.take(2, 8, CH)
        WW = mi.take(2, 8, CH)
        SBD = mi.take(CT, P)
        R = mi.take(C)
        decay_end = mi.take(CT, NCH)
        XT = view(at_K2, NM, CH)
        UV = view(at_L, NCH, C)
        m_of = lambda ch, h: ch * HEADS + (h % 2) * 4 + h // 2
        X = O[0:64, :, 0:CH]
        Tm = XT[0:64]
        bc = lambda ap, n: ap.unsqueeze(1).broadcast_to([ap.shape[0], n, ap.shape[1]])
        with nc.Block() as block:
            dve0, pe0, act0 = dve_s.value, pe_s.value, act_s.value

            @block.tensor
            def _(pe):
                for ch in range(NCH):
                    for par in range(2):
                        n = 2 * ch + par
                        if n >= 4:
                            pe.wait_ge(dve_s.sem, dve0 + n - 3 + 1)
                        lo = par * 64
                        for j in range(CT):
                            mm = T.matmul(bank[n % 4][:, j * P:j * P + P],
                                          K2[lo:lo + 64, j, ch, :, :].rearrange("p a b -> p (a b)"),
                                          Q2[lo:lo + 64, j, ch, :, :].rearrange("p a b -> p (a b)"), start=True, stop=True)
                        pe_s.on(mm)
                for ch in range(NCH):
                    if ch >= 2:
                        pe.wait_ge(act_s.sem, act0 + ch - 1)
                    for j in range(CT):
                        t = T.transpose(bank[4 + ch % 2][:, j * P:j * P + P],
                                        K2[:, j, ch, :, :].rearrange("p a b -> p (a b)"), ident)
                    pe_s.on(t)

            @block.vector
            def _(dve):
                dve_s.on(V.tensor_copy(decay_end, e_pos[:, :, CH - 1:T1P:CH]))
                for n in range(2 * NCH):
                    dve.wait_ge(pe_s.sem, pe0 + n + 1)
                    if n == 0:
                        dve.wait_ge(dve_s.sem, dve_s.value)
                    dve_s.on(V.tensor_tensor(O[:, 4 * n:4 * n + 4, :], bank[n % 4][:, :].rearrange("p (a b) -> p a b", b=P),
                                             bc(rw_mask, 4), ALU.mult))

            @block.scalar
            def _(act):
                for ch in range(NCH):
                    act.wait_ge(pe_s.sem, pe0 + 2 * NCH + ch + 1)
                    act_s.on(S.activation(K2tok[:, ch * CT:ch * CT + CT, :],
                                          bank[4 + ch % 2][:, :].rearrange("p (a b) -> p a b", b=P), ACT.Copy))

        with nc.Block() as block:
            dve0, pe0, act0 = dve_s.value, pe_s.value, act_s.value

            @block.tensor
            def _(pe):
                for g in range(NCH):
                    for i in range(8):
                        t = T.transpose(bank[g][0:64, i * CH:i * CH + CH], O[0:64, 8 * g + i, 0:CH], ident[0:64, 0:64])
                    pe_s.on(t)

            @block.scalar
            def _(act):
                for g in range(NCH):
                    act.wait_ge(pe_s.sem, pe0 + g + 1)
                    act_s.on(S.activation(L[0:64, 8 * g:8 * g + 8, :],
                                          bank[g][0:64, :].rearrange("p (a b) -> p a b", b=CH), ACT.Copy))

            @block.vector
            def _(dve):
                eye = bc(ident[0:64, 0:64], 8)
                for g in range(NCH):
                    s = slice(8 * g, 8 * g + 8)
                    dve.wait_ge(act_s.sem, act0 + g + 1)
                    dve.wait_ge(dve_s.sem, dve_s.on(V.tensor_tensor(X[:, s, :], X[:, s, :], bc(upper[0][0:64, 0:64], 8), ALU.mult)))
                    dve_s.on(V.tensor_tensor(X[:, s, :], eye, X[:, s, :], ALU.subtract))
                    dve.wait_ge(dve_s.sem, dve_s.on(V.tensor_tensor(Tm[:, s, :], L[0:64, s, :], bc(lower[0][0:64, 0:64], 8), ALU.mult)))
                    dve_s.on(V.tensor_tensor(Tm[:, s, :], eye, Tm[:, s, :], ALU.subtract))

        def triangular_inverse(L, X, Tm, LM, WW, width, per, groups, levels):
            s_lm = Signal(nc, ctx, "level_block" + str(width))
            s_w = Signal(nc, ctx, "block_times_inverse" + str(width))
            s_wc = Signal(nc, ctx, "block_times_inverse_copied" + str(width))
            s_xw = Signal(nc, ctx, "correction" + str(width))
            s_x = Signal(nc, ctx, "inverse_updated" + str(width))
            shaped = lambda b: b[0:width, :].rearrange("p (a b) -> p a b", b=width)
            todo = [(n, g) for n in levels for g in range(groups)]
            with nc.Block() as block:
                @block.vector
                def _(dve):
                    def mask(i):
                        n, g = todo[i]
                        if i >= 2:
                            dve.wait_ge(s_w.sem, i - 1)
                        s_lm.on(V.tensor_tensor(LM[0:width, i % 2], L[0:width, per * g:per * g + per, :],
                                                bc(lower[n][0:width, 0:width], per), ALU.mult))

                    def update(i):
                        n, g = todo[i]
                        s = slice(per * g, per * g + per)
                        dve.wait_ge(s_xw.sem, i + 1)
                        s_x.on(V.tensor_tensor(X[:, s, :], X[:, s, :], shaped(bank[2 + i % 2]), ALU.subtract))
                        s_x.on(V.tensor_tensor(Tm[:, s, :], Tm[:, s, :], shaped(bank[4 + i % 2]), ALU.subtract))
                    for i in range(len(todo) + 2):
                        if i < len(todo):
                            mask(i)
                        if i >= 2:
                            update(i - 2)

                @block.tensor
                def _(pe):
                    def block_product(i):
                        n, g = todo[i]
                        pe.wait_ge(s_lm.sem, i + 1)
                        if i >= groups:
                            pe.wait_ge(s_x.sem, 2 * (i - groups + 1))
                        if i >= 2:
                            pe.wait_ge(s_wc.sem, i - 1)
                        for q in range(per):
                            mm = T.matmul(bank[i % 2][0:width, q * width:q * width + width], LM[0:width, i % 2, q, :],
                                          X[:, per * g + q, :], start=True, stop=True)
                        s_w.on(mm)

                    def corrections(i):
                        n, g = todo[i]
                        pe.wait_ge(s_wc.sem, i + 1)
                        if i >= 2:
                            pe.wait_ge(s_x.sem, 2 * (i - 1))
                        for q in range(per):
                            T.matmul(bank[2 + i % 2][0:width, q * width:q * width + width], Tm[:, per * g + q, :],
                                     WW[0:width, i % 2, q, :], start=True, stop=True)
                        for q in range(per):
                            mm = T.matmul(bank[4 + i % 2][0:width, q * width:q * width + width], WW[0:width, i % 2, q, :],
                                          Tm[:, per * g + q, :], start=True, stop=True)
                        s_xw.on(mm)
                    for i in range(len(todo) + 1):
                        if i < len(todo):
                            block_product(i)
                        if i >= 1:
                            corrections(i - 1)

                @block.scalar
                def _(act):
                    for i in range(len(todo)):
                        act.wait_ge(s_w.sem, i + 1)
                        if i >= 2:
                            act.wait_ge(s_xw.sem, i - 1)
                        s_wc.on(S.activation(WW[0:width, i % 2], shaped(bank[i % 2]), ACT.Copy))

        triangular_inverse(L, X, Tm, LM, WW, CH, 8, NCH, range(1, 6))

        with nc.Block() as block:
            dve0, pe0 = dve_s.value, pe_s.value

            @block.tensor
            def _(pe):
                for ch in range(NCH):
                    if ch >= 4:
                        pe.wait_ge(dve_s.sem, dve0 + 2 + ch - 3)
                    for j in range(CT):
                        t = T.transpose(bank[ch % 4][:, j * P:j * P + P], vS[:, j, CH * ch:CH * ch + P], ident)
                    pe_s.on(t)

            @block.vector
            def _(dve):
                dve_s.on(V.memset(UV[0:64, :, :], 0.0))
                dve_s.on(V.memset(SBD, 0.0))
                for ch in range(NCH):
                    dve.wait_ge(pe_s.sem, pe0 + ch + 1)
                    dve_s.on(V.tensor_copy(UV[64:128, ch, :], bank[ch % 4][64:128, :]))

        s_r = Signal(nc, ctx, "rhs_ready")
        s_rc = Signal(nc, ctx, "rhs_copied")
        s_u = Signal(nc, ctx, "u_ready")
        s_uc = Signal(nc, ctx, "u_copied")
        s_ry = Signal(nc, ctx, "chunk_out")
        s_ryc = Signal(nc, ctx, "chunk_out_copied")
        s_st = Signal(nc, ctx, "state_change")
        s_state = Signal(nc, ctx, "state_ready")
        with nc.Block() as block:
            @block.tensor
            def _(pe):
                for ch in range(NCH):
                    if ch:
                        pe.wait_ge(s_state.sem, 4 * ch)
                    for j in range(CT):
                        T.matmul(bank[0][0:64, j * P:j * P + P], Q2[:, j, ch, 0, :], SBD[:, j, :], start=True, stop=False,
                                 skip_group_check=True)
                        for h in (2 * j, 2 * j + 1):
                            mm = T.matmul(bank[0][0:64, h * DH:h * DH + DH], O[:, m_of(ch, h), 0:CH],
                                          UV[:, ch, h * DH:h * DH + DH], start=False, stop=True, skip_group_check=True)
                    s_r.on(mm)
                    pe.wait_ge(s_rc.sem, ch + 1)
                    for h in range(HEADS):
                        mm = T.matmul(bank[1][0:64, h * DH:h * DH + DH], X[:, m_of(ch, h), :], R[0:64, h * DH:h * DH + DH],
                                      start=True, stop=True)
                    s_u.on(mm)
                    pe.wait_ge(s_uc.sem, ch + 1)
                    if ch < NCH - 1:
                        for h in range(HEADS):
                            lo = DH * (h % 2)
                            mm = T.matmul(bank[4][lo:lo + DH, (h // 2) * P + lo:(h // 2) * P + lo + DH],
                                          K2tok[:, ch * CT + h // 2, lo:lo + DH], UV[:, ch, h * DH:h * DH + DH],
                                          start=True, stop=True)
                        s_st.on(mm)
                    if ch >= 2:
                        pe.wait_ge(s_ryc.sem, ch - 1)
                    for j in range(CT):
                        T.matmul(bank[2 + ch % 2][:, j * CH:j * CH + CH], SBD[:, j, :], Q2[:, j, ch, 1, :], start=True,
                                 stop=False, skip_group_check=True)
                        for h in (2 * j, 2 * j + 1):
                            lo = DH * (h % 2)
                            mm = T.matmul(bank[2 + ch % 2][lo:lo + DH, j * CH:j * CH + CH], UV[:, ch, h * DH:h * DH + DH],
                                          O[:, m_of(ch, h), CH:P], start=False, stop=True, skip_group_check=True)
                    s_ry.on(mm)

            @block.scalar
            def _(act):
                for ch in range(NCH):
                    act.wait_ge(s_r.sem, ch + 1)
                    if ch:
                        act.wait_ge(s_u.sem, ch)
                    s_rc.on(S.activation(R[0:64], bank[0][0:64, :], ACT.Copy))
                    act.wait_ge(s_u.sem, ch + 1)
                    s_uc.on(S.activation(UV[0:64, ch, :], bank[1][0:64, :], ACT.Copy, scale=-1.0))

            @block.vector
            def _(dve):
                for ch in range(NCH):
                    if ch < NCH - 1:
                        dve.wait_ge(s_st.sem, ch + 1)
                        dve.wait_ge(s_ry.sem, ch + 1)
                        for lo in (0, DH):
                            s = SBD[lo:lo + DH, :, lo:lo + DH]
                            s_state.on(V.tensor_tensor(s, s, bank[4][lo:lo + DH, :].rearrange("p (a b) -> p a b", b=P)[:, :, lo:lo + DH], ALU.add))
                        dve.wait_ge(s_state.sem, 4 * ch + 2)
                        for lo in (0, DH):
                            s = SBD[lo:lo + DH, :, lo:lo + DH]
                            s_state.on(V.tensor_tensor(s, s, decay_end[lo:lo + DH, :, ch:ch + 1].broadcast_to([DH, CT, DH]), ALU.mult))
                    dve.wait_ge(s_ry.sem, ch + 1)
                    n = min(CH, T1 - ch * CH)
                    s_ryc.on(V.tensor_copy(y_rw[:, :, ch * CH:ch * CH + n],
                                           bank[2 + ch % 2][:, 0:CT * CH].rearrange("p (a b) -> p a b", b=CH)[:, :, 0:n]))

        mg = Memory(sbuf, at_K2, top)
        dev, sq, gnr = mg.take(CT, T1), mg.take(CT, T1), mg.take(CT, T1)
        with nc.Block() as block:
            pe0 = pe_s.value

            @block.tensor
            def _(pe):
                for j in range(CT):
                    pe_s.on(T.matmul(bank[j][:, 0:T1], blk64, y_rw[:, j, :], start=True, stop=True))
                for j in range(CT):
                    pe_s.on(T.matmul(bank[4 + j][:, 0:T1], blk64, rk[:, j, :], start=True, stop=True))

            @block.vector
            def _(dve):
                for j in range(CT):
                    dve.wait_ge(pe_s.sem, pe0 + j + 1)
                    n = dve_s.on(V.scalar_tensor_tensor(out=dev[:, j, :], in0=bank[j][:, 0:T1], scalar=-1.0 / DH,
                                                        in1=y_rw[:, j, :], op0=ALU.mult, op1=ALU.add))
                dve.wait_ge(dve_s.sem, n)
                dve_s.on(V.tensor_tensor(sq, dev, dev, ALU.mult))
                for j in range(CT):
                    dve.wait_ge(pe_s.sem, pe0 + 4 + j + 1)
                    dve_s.on(V.tensor_tensor(rk[:, j, :], bank[4 + j][:, 0:T1], vS[:, j, CH:CH + T1], ALU.mult))

            @block.tensor
            def _(pe):
                pe.wait_ge(dve_s.sem, dve_s.value - 4)
                for j in range(CT):
                    pe_s.on(T.matmul(bank[j][:, 0:T1], blk64, sq[:, j, :], start=True, stop=True))
                pe.wait_ge(dve_s.sem, dve_s.value)
                for j in range(CT):
                    T.matmul(bank[4 + j][:, 0:T1], g_up0[:, j * P:j * P + P], g_in[:, 0, :], start=True, stop=False)
                    pe_s.on(T.matmul(bank[4 + j][:, 0:T1], g_up1[0:32, j * P:j * P + P], g_in[0:32, 1, :], start=False, stop=True))

            @block.scalar
            def _(act):
                for j in range(CT):
                    act.wait_ge(pe_s.sem, pe0 + 8 + j + 1)
                    act_s.on(S.activation(gnr[:, j, :], bank[j][:, 0:T1], ACT.Sqrt, bias=eps_gn, scale=1.0 / DH))

            @block.vector
            def _(dve):
                dve.wait_ge(act_s.sem, act_s.value)
                dve.wait_ge(dve_s.sem, dve_s.on(V.reciprocal(gnr, gnr)))
                dve.wait_ge(dve_s.sem, dve_s.on(V.tensor_tensor(dev, dev, gnr, ALU.mult)))
                for j in range(CT):
                    n = dve_s.on(V.tensor_scalar(dev[:, j, :], dev[:, j, :], param("ln_x_w", j), param("ln_x_b", j), ALU.mult, ALU.add))
                dve.wait_ge(dve_s.sem, n)
                dve.wait_ge(dve_s.sem, dve_s.on(V.tensor_tensor(dev, dev, rk, ALU.add)))
                for j in range(CT):
                    dve.wait_ge(pe_s.sem, pe0 + 12 + j + 1)
                    dve_s.on(V.tensor_tensor(y_rw[:, j, :], dev[:, j, :], bank[4 + j][:, 0:T1], ALU.mult))
        gates = view(A0, 2 * KD, T1)
        part = view(A0 + 2 * KD * T1, KD, T1)
        merged = view(A0 + 3 * KD * T1, KD, T1)

        def gate_out(engine, m, psum):
            return S.activation(gates[:, m, :], psum, ACT.Sigmoid)
        project(xnT, T1, [(7 + m // 4, (m % 4) * P, P) for m in range(2 * KD)], gate_out, 7, 4, owner=lambda m: "act")

        def sb_out(engine, m, psum):
            return V.tensor_tensor(part[:, m, :], psum, gates[:, m, :], ALU.mult)
        project(y_sb, T1, [(SB_OUT, m * P, P) for m in range(KD)], sb_out, SB_OUT, 1, owner=lambda m: "dve")

        def rw_out(engine, m, psum):
            return V.tensor_tensor(merged[:, m, :], psum, gates[:, KD + m, :], ALU.mult)
        project(y_rw, T1, [(SB_OUT + 1, m * P, P) for m in range(KD)], rw_out, SB_OUT + 1, 1, owner=lambda m: "dve")
        with nc.Block() as block:
            @block.vector
            def _(dve):
                dve_s.on(V.tensor_tensor(merged, merged, part, ALU.add))

        def add_to_stream(engine, m, psum):
            return V.tensor_tensor(hT[:, m, :], hT[:, m, :], psum, ALU.add)
        project(merged, T1, [(W_OUT + m // 4, (m % 4) * P, P) for m in range(KD)], add_to_stream, W_OUT, 2,
                owner=lambda m: "dve")

        arena.close()
        arena = ExitStack()
        take = lambda name, shape, dt: arena.enter_context(nc.sbuf_tensor(name, shape, dt))
        MODC = 512
        fmem = Memory(take("ffn_memory", [P, 4 * T1 + 2 * MODC], F32), 0, 4 * T1 + 2 * MODC)
        fsig = fmem.take(2, T1)
        fprod = fmem.take(2, T1)
        ada = fmem.take(2, MODC)
        ffn_hi, ffn_lo = take("ffn_hidden_hi", [P, FT, T1], F32R), take("ffn_hidden_lo", [P, FT, T1], F32R)
        fx_hi, fx_lo = take("ffn_x_hi", [P, KD, T1], F32R), take("ffn_x_lo", [P, KD, T1], F32R)
        norm_stack = ExitStack()
        nmem = norm_stack.enter_context(nc.sbuf_tensor("ffn_norm", [P, 2, KD, T1], F32))
        hnT, fsq = nmem[:, 0], nmem[:, 1]
        rms_norm(hT, hnT, lambda j: param("norm_ffn", j), None, T1, fsq, fsig[:, 0, :])
        with nc.Block() as block:
            @block.scalar
            def _(act):
                act_s.on(S.activation(fx_hi[:, :, :], hnT, ACT.Copy))
                c0 = ROWS0["c_2"][0]
                act_s.on(S.activation(csil[:, :, 0], vec0[:, c0:c0 + KD], ACT.Sigmoid))

            @block.vector
            def _(dve):
                dve.wait_ge(act_s.sem, act_s.value - 1)
                dve_s.on(V.tensor_tensor(fx_lo[:, :, :], hnT, fx_hi[:, :, :].bitcast(F32), ALU.subtract))
                dve.wait_ge(act_s.sem, act_s.value)
                dve_s.on(V.tensor_tensor(csil[:, :, 0], csil[:, :, 0], vec0[:, ROWS0["c_2"][0]:ROWS0["c_2"][0] + KD], ALU.mult))
        norm_stack.close()
        CUT = 3
        f_hi = [take(f"ffn_weights_hi{i}", [P, PIECE], F32R) for i in range(CUT)]
        f_lo = [take(f"ffn_weights_lo{i}", [P, PIECE], F32R) for i in range(CUT)]
        n_in, n_out = FT, FT // 2
        s_cut = Signal(nc, ctx, "piece_hi_ready")
        s_rest = Signal(nc, ctx, "piece_lo_ready")
        s_used = Signal(nc, ctx, "piece_used")
        s_sig = Signal(nc, ctx, "gate_sigmoid")
        s_hid = Signal(nc, ctx, "hidden_ready")
        s_fhi = Signal(nc, ctx, "ffn_hidden_hi")
        s_flo = Signal(nc, ctx, "ffn_hidden_lo")
        s_ada = Signal(nc, ctx, "modulation_steps")
        ada_ready = [Signal(nc, ctx, f"modulation_slot{i}") for i in range(2)]
        ada_w = take("modulation_weights", [P, 2, 2, MODC], F32)
        s_ada_sum = Signal(nc, ctx, "modulation_block_summed")
        N_ADA = 48

        sum_bank = []

        def steps_by(m):
            return 4 * (m + 1)

        def piece(r):
            if r < n_in:
                n = FFN_IN + r // 2
                return n, slot(n).rearrange("p k (u c) -> p k u c", u=2)[:, :, :, (r % 2) * P:(r % 2) * P + P]
            r -= n_in
            n = FFN_OUT + r // 2
            return n, slot(n)[:, (r % 2) * 2:(r % 2) * 2 + 2, :]

        def as_piece(ap, r):
            return (ap[:, :].rearrange("p (k u c) -> p k u c", k=KD, u=2) if r < n_in
                    else ap[:, :].rearrange("p (k c) -> p k c", k=2))

        for r in range(n_in + n_out):
            slot_freed[piece(r)[0]] = s_rest, r + 1
        with nc.Block() as block:
            @block.sync
            def _(sp):
                load_slots(sp, W_IN2 + RING)

            @block.gpsimd
            def _(pool):
                w = a["w_ada_2"][0]
                for n in range(N_ADA):
                    if n >= 2:
                        pool.wait_ge(s_ada.sem, 2 * (n - 1))
                    cb, kg = n // 4, n % 4
                    src = w[2 * kg * P:(2 * kg + 2) * P, cb * MODC:(cb + 1) * MODC].rearrange("(k p) c -> p k c", p=P)
                    ada_ready[n % 2].on(pool.dma_start(ada_w[:, n % 2], src), 16)

            @block.tensor
            def _(pe):
                summed = [0]

                def sum_partitions(steps, b):
                    while 8 * (summed[0] + 1) <= steps:
                        cb = summed[0]
                        pe.wait_ge(s_ada.sem, 8 * (cb + 1))
                        for m in range(MODC // P):
                            at = 320 + cb * MODC // P + m
                            mm = T.matmul(bank[b][:, at:at + 1], ada[:, cb % 2, m * P:m * P + P],
                                          one_col, start=True, stop=True)
                        s_ada_sum.on(mm)
                        sum_bank.append(b)
                        summed[0] += 1
                for m in range(n_in):
                    pe.wait_ge(s_rest.sem, m + 1)
                    if m >= 4:
                        pe.wait_ge(s_hid.sem, 2 * (m - 3))
                    sum_partitions(steps_by(m - 3), 2 * (m % 4))
                    hi, lo = as_piece(f_hi[m % CUT], m), as_piece(f_lo[m % CUT], m)
                    for up in range(2):
                        for k in range(KD):
                            for w, x in ((hi, fx_hi), (hi, fx_lo), (lo, fx_hi)):
                                mm = T.matmul(bank[2 * (m % 4) + up][:, 0:T1], w[:, k, up, :], x[:, k, :],
                                              start=(k == 0 and w is hi and x is fx_hi), stop=(k == KD - 1 and w is lo))
                    s_used.on(mm)
                pe.wait_ge(s_hid.sem, 2 * n_in)
                sum_partitions(steps_by(n_in - 1), 7)
                for r in range(n_in, n_in + n_out):
                    pe.wait_ge(s_rest.sem, r + 1)
                    hi, lo = as_piece(f_hi[r % CUT], r), as_piece(f_lo[r % CUT], r)
                    for i in range(2):
                        k = 2 * (r - n_in) + i
                        pe.wait_ge(s_flo.sem, k + 1)
                        for m in range(KD):
                            for w, x in ((hi, ffn_hi), (hi, ffn_lo), (lo, ffn_hi)):
                                mm = T.matmul(bank[m][:, 0:T1], w[:, i, m * P:m * P + P], x[:, k, :],
                                              start=(k == 0 and w is hi and x is ffn_hi), stop=(k == FT - 1 and w is lo))
                    s_used.on(mm)
                sum_partitions(2 * N_ADA, 7)

            @block.scalar
            def _(act):
                def cut(r):
                    n, src = piece(r)
                    await_slot(act, n)
                    if r >= CUT:
                        act.wait_ge(s_used.sem, r - CUT + 1)
                    s_cut.on(S.activation(as_piece(f_hi[r % CUT], r), src, ACT.Copy))
                for r in range(CUT):
                    cut(r)
                for m in range(n_in):
                    act.wait_ge(s_used.sem, m + 1)
                    if m >= 2:
                        act.wait_ge(s_hid.sem, 2 * (m - 1))
                    s_sig.on(S.activation(fsig[:, m % 2, :], bank[2 * (m % 4)][:, 0:T1], ACT.Sigmoid))
                    cut(m + CUT)
                    act.wait_ge(s_hid.sem, 2 * m + 2)
                    s_fhi.on(S.activation(ffn_hi[:, m, :], fprod[:, m % 2, :], ACT.Copy))
                for r in range(n_in + CUT, n_in + n_out):
                    cut(r)

            @block.vector
            def _(dve):
                ada_at = [0]

                def rest_of(r):
                    n, src = piece(r)
                    dve.wait_ge(s_cut.sem, r + 1)
                    s_rest.on(V.tensor_tensor(as_piece(f_lo[r % CUT], r), src, as_piece(f_hi[r % CUT], r).bitcast(F32), ALU.subtract))

                def modulation(upto):
                    while ada_at[0] < min(upto, 2 * N_ADA):
                        step = ada_at[0]
                        n, half = step // 2, step % 2
                        cb, k = n // 4, 2 * (n % 4) + half
                        if half == 0:
                            dve.wait_ge(ada_ready[n % 2].sem, 16 * (n // 2 + 1))
                        if k == 0 and cb >= 2:
                            dve.wait_ge(s_ada_sum.sem, cb - 1)
                        if step:
                            dve.wait_ge(s_ada.sem, step)
                        dst, src = ada[:, cb % 2, :], ada_w[:, n % 2, half, :]
                        if k == 0:
                            s_ada.on(V.tensor_scalar(dst, src, csil[:, 0, :], None, ALU.mult))
                        else:
                            s_ada.on(V.scalar_tensor_tensor(out=dst, in0=src, scalar=csil[:, k, :], in1=dst, op0=ALU.mult, op1=ALU.add))
                        ada_at[0] += 1
                for r in range(CUT):
                    rest_of(r)
                for m in range(n_in):
                    b = 2 * (m % 4)
                    dve.wait_ge(s_sig.sem, m + 1)
                    if m >= 2:
                        dve.wait_ge(s_flo.sem, m - 1)
                    s_hid.on(V.tensor_tensor(fprod[:, m % 2, :], bank[b][:, 0:T1], fsig[:, m % 2, :], ALU.mult))
                    dve.wait_ge(s_hid.sem, 2 * m + 1)
                    s_hid.on(V.tensor_tensor(fprod[:, m % 2, :], fprod[:, m % 2, :], bank[b + 1][:, 0:T1], ALU.mult))
                    rest_of(m + CUT)
                    dve.wait_ge(s_fhi.sem, m + 1)
                    s_flo.on(V.tensor_tensor(ffn_lo[:, m, :], fprod[:, m % 2, :], ffn_hi[:, m, :].bitcast(F32), ALU.subtract))
                    modulation(steps_by(m))
                for r in range(n_in + CUT, n_in + n_out):
                    rest_of(r)
                    modulation(steps_by(n_in - 1) + 2 * (r - n_in - CUT + 1))
                modulation(2 * N_ADA)
                dve.wait_ge(s_ada_sum.sem, 12)
                for m in range(KD):
                    dve_s.on(V.tensor_tensor(hT[:, m, :], hT[:, m, :], bank[m][:, 0:T1], ALU.add))
                c0 = ROWS1["b_ada_2"][0]
                for cb in range(6 * D // MODC):
                    lo, n = cb * MODC // P, MODC // P
                    dve_s.on(V.tensor_tensor(mod[:, lo:lo + n], bank[sum_bank[cb]][:, 320 + lo:320 + lo + n],
                                             vec1[:, c0 + lo:c0 + lo + n], ALU.add))

        arena.close()
        arena = ExitStack()
        sbuf = arena.enter_context(nc.sbuf_tensor("mixer2_memory", [P, total], F32))
        view = Memory(sbuf, 0, total).view
        end = total
        xT = Memory(kept, CONSTS, CONSTS + KD * T1).take(KD, T2)
        at2 = base + 10304
        m2 = Memory(sbuf, at2, end)
        x_new = view(base + 2 * KD * T2, KD, T2)
        rms_norm(hT[:, :, N_META:T1], x_new, lambda j: param("norm_final", j), None, T2, view(base, KD, T2), view(base + KD * T2, T2))
        with nc.Block() as block:
            @block.gpsimd
            def _(pool):
                pool_s.on(G.tensor_copy(xT, x_new))

            @block.vector
            def _(dve):
                for gain_, name, sc in ((gain1, "norm1_w_2", 1), (gain2, "norm2_w_2", 4)):
                    c0 = ROWS0[name][0]
                    dve_s.on(V.scalar_tensor_tensor(out=gain_, in0=mod[:, sc * KD:sc * KD + KD], scalar=1.0,
                                                    in1=vec0[:, c0:c0 + KD], op0=ALU.add, op1=ALU.mult))
                r0 = ROWS0["hg_lb_2"][0]
                a0_, a1_ = vec0[:, r0:r0 + GH], vec0[:, r0 + GH:r0 + 2 * GH]
                n = dve_s.on(V.tensor_tensor(lb, a0_, a1_, ALU.max))
                dve.wait_ge(dve_s.sem, n)
                dve_s.on(V.tensor_tensor(e_hg[:, 0:GH], a0_, lb, ALU.subtract))
                dve_s.on(V.tensor_tensor(e_hg[:, GH:2 * GH], a1_, lb, ALU.subtract))

            @block.scalar
            def _(act):
                act.wait_ge(dve_s.sem, dve_s.value)
                act_s.on(S.activation(e_hg, e_hg, ACT.Exp))

            @block.vector
            def _(dve):
                dve.wait_ge(act_s.sem, act_s.value)
                dve.wait_ge(dve_s.sem, dve_s.on(V.tensor_tensor(lb1, e_hg[:, 0:GH], e_hg[:, GH:2 * GH], ALU.add)))
                dve.wait_ge(dve_s.sem, dve_s.on(V.reciprocal(lb1, lb1)))
                dve_s.on(V.tensor_tensor(lb, e_hg[:, 0:GH], lb1, ALU.mult))
                dve.wait_ge(dve_s.sem, dve_s.value)
                dve_s.on(V.tensor_scalar(lb1, lb, -1.0, 1.0, ALU.mult, ALU.add))
        low = Memory(sbuf, base, base + 10304)
        hm = low.take(KD, T2)
        raw2 = low.take(12, 3 + T2)
        over_hm = base
        proj_b = low.take(5, GH, T2)
        gate_a, f_b, i_b, q_b, gate_b = (proj_b[:, i] for i in range(5))
        qkv = m2.take(12, T2)
        G_at = m2.at
        gcB = m2.take(GH, T2)
        beB = m2.take(GH, T2)
        Dm = m2.take(2 * GH, P)
        GG = m2.take(2 * GH, 2 * P)
        L2 = m2.take(2 * GH, P)
        Tm2 = m2.take(2 * GH, P)
        LM2 = m2.take(2, 4, P)
        WW2 = m2.take(2, 4, P)
        rows_b, rows_g = m2.take(T2), m2.take(T2)
        cols = m2.take(4, GH)
        tail_f = m2.take(GH)
        ealog = m2.take(1)
        o_all = m2.take(KD, T2)
        assert m2.at <= end, (m2.at, end)
        ba = small[:, 0:64].rearrange("p (k c) -> p k c", c=8)
        alog, dtb = small[0:GH, 64:65], small[0:GH, 65:66]
        rms_norm(xT, hm, lambda j: gain1[:, j:j + 1], lambda j: mod[:, j:j + 1], T2, view(m2.at - KD * T2, KD, T2), view(at2, T2))
        with nc.Block() as block:
            @block.gpsimd
            def _(pool):
                pool_s.on(G.memset(raw2[:, :, 0:3], 0.0))

        def put_in2(engine, m, psum):
            dst = raw2[:, m, 3:3 + T2] if m < 12 else proj_b[:, (m - 12) // 4, m % 4, :]
            if engine is nc.scalar:
                return S.activation(dst, psum, ACT.Copy)
            return V.tensor_copy(dst, psum)
        project(hm, T2, [(W_IN2 + m // 4, (m % 4) * P, P) for m in range(32)], put_in2, W_IN2, 8)

        with nc.Block() as block:
            @block.tensor
            def _(pe):
                for i in range(2):
                    for k in range(KD):
                        mm = T.matmul(bank[i][0:GH, 0:T2], ba[:, k, GH * i:GH * i + GH], hm[:, k, :],
                                      start=(k == 0), stop=(k == KD - 1))
                    pe_s.on(mm)

            @block.scalar
            def _(act):
                act.wait_ge(pe_s.sem, pe_s.value - 1)
                act_s.on(S.activation(rows_b[0:GH, :], bank[0][0:GH, 0:T2], ACT.Sigmoid))
                act.wait_ge(pe_s.sem, pe_s.value)
                act_s.on(S.activation(ealog[0:GH, :], alog, ACT.Exp))
                marks["abs"] = act_s.on(S.activation(rows_g[0:GH, :], bank[1][0:GH, 0:T2], ACT.Abs, bias=dtb))
                act.wait_ge(act_s.sem, act_s.value)
                act.wait_ge(act_s.sem, act_s.on(S.activation(rows_g[0:GH, :], rows_g[0:GH, :], ACT.Exp, scale=-1.0)))
                act_s.on(S.activation(rows_g[0:GH, :], rows_g[0:GH, :], ACT.Ln, bias=one_col[0:GH, :]))

            @block.vector
            def _(dve):
                for j in (3, 2, 1, 0):
                    for m in range(12):
                        w = param("conv_w_2", 12 * j + m)
                        if j == 3:
                            dve_s.on(V.tensor_scalar(qkv[:, m, :], raw2[:, m, 3:3 + T2], w, None, ALU.mult))
                        else:
                            dve.wait_ge(dve_s.sem, dve_s.value - 11)
                            dve_s.on(V.scalar_tensor_tensor(out=qkv[:, m, :], in0=raw2[:, m, j:j + T2], scalar=w,
                                                            in1=qkv[:, m, :], op0=ALU.mult, op1=ALU.add))
                marks["conv"] = dve_s.value

            @block.scalar
            def _(act):
                act.wait_ge(dve_s.sem, dve_s.value)
                marks["log_term"] = act_s.value
                marks["sig"] = act_s.on(S.activation(raw2[:, :, 0:T2], qkv, ACT.Sigmoid))

            @block.vector
            def _(dve):
                dve.wait_ge(act_s.sem, marks["log_term"])
                t = gcB[0:GH, 0, :]
                dve.wait_ge(dve_s.sem, dve_s.on(V.tensor_scalar(t, bank[1][0:GH, 0:T2], dtb, 0.0, ALU.add, ALU.max)))
                dve.wait_ge(dve_s.sem, dve_s.on(V.tensor_tensor(rows_g[0:GH, :], rows_g[0:GH, :], t, ALU.add)))
                dve.wait_ge(dve_s.sem, dve_s.on(V.tensor_scalar(t, rows_g[0:GH, :], ealog[0:GH, :], -1.0, ALU.mult, ALU.mult)))
                marks["rows"] = dve_s.on(V.tensor_tensor_scan(rows_g[0:GH, :], reset128[0:GH, :], t, 0.0, ALU.mult, ALU.add))
                dve.wait_ge(act_s.sem, marks["sig"])
                dve.wait_ge(dve_s.sem, dve_s.on(V.tensor_tensor(qkv, qkv, raw2[:, :, 0:T2], ALU.mult)))
                dve_s.on(V.tensor_tensor(raw2[:, 0:8, 0:T2], qkv[:, 0:8, :], qkv[:, 0:8, :], ALU.mult))

            @block.tensor
            def _(pe):
                pe.wait_ge(dve_s.sem, dve_s.value)
                for m in range(8):
                    mm = T.matmul(bank[2 + m // 2][:, (m % 2) * T2:(m % 2) * T2 + T2], ones, raw2[:, m, 0:T2], start=True, stop=True)
                    if m % 2:
                        pe_s.on(mm)
                for i, rows in enumerate((rows_g, rows_b)):
                    for h in range(GH):
                        b = (6, 7, 0, 1)[2 * i + h // 2]
                        mm = T.matmul(bank[b][:, (h % 2) * T2:(h % 2) * T2 + T2], row_sel[0:GH, h, :], rows[0:GH, :],
                                      start=True, stop=True)
                    pe_s.on(mm)

            @block.scalar
            def _(act):
                for b in range(4):
                    act.wait_ge(pe_s.sem, pe_s.value - 5 + b)
                    act_s.on(S.activation(raw2[:, 2 * b:2 * b + 2, 0:T2], bank[2 + b][:, :].rearrange("p (a b) -> p a b", b=T2),
                                          ACT.Sqrt, bias=eps_rms))

            @block.vector
            def _(dve):
                dve.wait_ge(pe_s.sem, pe_s.value)
                for i, dst in enumerate((gcB, beB)):
                    for q in range(2):
                        dve_s.on(V.tensor_copy(dst[:, 2 * q:2 * q + 2, :], bank[(6, 7, 0, 1)[2 * i + q]][:, :].rearrange("p (a b) -> p a b", b=T2)))
                dve.wait_ge(act_s.sem, act_s.value)
                dve.wait_ge(dve_s.sem, dve_s.on(V.reciprocal(raw2[:, 0:8, 0:T2], raw2[:, 0:8, 0:T2])))
                dve_s.on(V.scalar_tensor_tensor(out=qkv[:, 0:4, :], in0=qkv[:, 0:4, :], scalar=P ** -0.5,
                                                in1=raw2[:, 0:4, 0:T2], op0=ALU.mult, op1=ALU.mult))
                dve_s.on(V.tensor_tensor(qkv[:, 4:8, :], qkv[:, 4:8, :], raw2[:, 4:8, 0:T2], ALU.mult))

            @block.tensor
            def _(pe):
                for i, rows in enumerate((rows_g, rows_b)):
                    for c in range(2):
                        t = T.transpose(bank[2][:, (2 * i + c) * GH:(2 * i + c) * GH + GH], rows[0:GH, c * P:c * P + P],
                                        ident[0:GH, 0:GH]) if not (i == 0 and c == 0) else None
                        if t is None:
                            pe.wait_ge(act_s.sem, act_s.value)
                            t = T.transpose(bank[2][:, 0:GH], rows[0:GH, 0:P], ident[0:GH, 0:GH])
                pe_s.on(t)

            @block.vector
            def _(dve):
                dve.wait_ge(pe_s.sem, pe_s.value)
                dve_s.on(V.tensor_copy(cols, bank[2][:, 0:4 * GH].rearrange("p (a b) -> p a b", b=GH)))

        lowa = Memory(sbuf, over_hm, over_hm + KD * T2 + 12 * (3 + T2))
        kg, qg, ktok, vtok, eg = (lowa.take(2 * GH, P) for _ in range(5))
        q2, k2, v2 = qkv[:, 0:4, :], qkv[:, 4:8, :], qkv[:, 8:12, :]
        mats = lambda ap: ap.rearrange("p h (c t) -> p (h c) t", c=2)
        pair = lambda b: b[:, :].rearrange("p (a b) -> p a b", b=P)
        X2 = GG[:, :, 0:P]
        AT = GG[:, :, P:2 * P]
        with nc.Block() as block:
            pe0, act0, dve0 = pe_s.value, act_s.value, dve_s.value

            @block.tensor
            def _(pe):
                for h in range(GH):
                    for c in range(2):
                        s = slice(c * P, c * P + P)
                        T.matmul(bank[h][:, c * 2 * P:c * 2 * P + P], k2[:, h, s], k2[:, h, s], start=True, stop=True)
                        mm = T.matmul(bank[h][:, c * 2 * P + P:c * 2 * P + 2 * P], k2[:, h, s], q2[:, h, s], start=True, stop=True)
                    pe_s.on(mm)
                for h in range(GH):
                    for c in range(2):
                        t = T.transpose(bank[4 + h // 2][:, (h % 2) * 2 * P + c * P:(h % 2) * 2 * P + c * P + P], v2[:, h, c * P:c * P + P], ident)
                pe_s.on(t)
                for h in range(GH):
                    t = T.transpose(bank[6][:, h * P:h * P + P], k2[:, h, 0:P], ident)
                pe_s.on(t)

            @block.vector
            def _(dve):
                for h in range(GH):
                    for c in range(2):
                        dve_s.on(V.tensor_scalar(Dm[:, 2 * h + c, :], gcB[:, h, c * P:c * P + P], cols[:, c, h:h + 1], 0.0,
                                                 ALU.subtract, ALU.min))
                for h in range(GH):
                    dve_s.on(V.tensor_tensor(tail_f[:, h:h + 1], gcB[:, h, P - 1:P], cols[:, 0, h:h + 1], ALU.subtract))

            @block.scalar
            def _(act):
                act.wait_ge(dve_s.sem, dve_s.value)
                act_s.on(S.activation(Dm, Dm, ACT.Exp))
                act_s.on(S.activation(eg, mats(gcB), ACT.Exp))
                act_s.on(S.activation(tail_f, tail_f, ACT.Exp))
                act.wait_ge(pe_s.sem, pe0 + 5)
                for q in range(2):
                    act_s.on(S.activation(vtok[:, 4 * q:4 * q + 4, :], pair(bank[4 + q]), ACT.Copy))
                act.wait_ge(pe_s.sem, pe0 + 6)
                act.wait_ge(act_s.sem, act_s.value - 2)
                for h in range(GH):
                    act_s.on(S.activation(ktok[:, h, :], bank[6][:, h * P:h * P + P], ACT.Copy, scale=tail_f[:, h:h + 1]))

            @block.vector
            def _(dve):
                dve.wait_ge(act_s.sem, act0 + 1)
                n = dve_s.on(V.tensor_tensor(mats(beB), mats(beB), Dm, ALU.mult))
                dve.wait_ge(dve_s.sem, n)
                for h in range(GH):
                    dve.wait_ge(pe_s.sem, pe0 + h + 1)
                    b3 = bank[h][:, :].rearrange("p (c i t) -> p c i t", c=2, i=2)
                    s = slice(2 * h, 2 * h + 2)
                    dve_s.on(V.tensor_tensor(X2[:, s, :], b3[:, :, 0, :], mats(beB)[:, s, :], ALU.mult))
                    dve_s.on(V.tensor_tensor(AT[:, s, :], b3[:, :, 1, :], Dm[:, s, :], ALU.mult))
                dve.wait_ge(dve_s.sem, dve_s.value)
                dve_s.on(V.tensor_tensor(X2, X2, bc(upper_strict, 2 * GH), ALU.mult))
                marks["n2"] = dve_s.value
                dve_s.on(V.tensor_tensor(AT, AT, bc(upper_incl, 2 * GH), ALU.mult))
                dve.wait_ge(act_s.sem, act0 + 2)
                dve_s.on(V.tensor_tensor(kg, mats(k2), eg, ALU.mult))
                dve_s.on(V.tensor_tensor(qg, mats(q2), eg, ALU.mult))

            @block.tensor
            def _(pe):
                pe.wait_ge(dve_s.sem, marks["n2"])
                for q in range(2):
                    for i in range(4):
                        t = T.transpose(bank[q][:, i * P:i * P + P], X2[:, 4 * q + i, :], ident)
                    pe_s.on(t)

            @block.vector
            def _(dve):
                eye = bc(ident, 4)
                for q in range(2):
                    s = slice(4 * q, 4 * q + 4)
                    dve.wait_ge(pe_s.sem, pe_s.value - 1 + q)
                    dve_s.on(V.tensor_copy(L2[:, s, :], pair(bank[q])))
                    dve.wait_ge(dve_s.sem, dve_s.on(V.tensor_tensor(X2[:, s, :], X2[:, s, :], bc(upper[0], 4), ALU.mult)))
                    dve_s.on(V.tensor_tensor(X2[:, s, :], eye, X2[:, s, :], ALU.subtract))
                    dve.wait_ge(dve_s.sem, dve_s.on(V.tensor_tensor(Tm2[:, s, :], L2[:, s, :], bc(lower[0], 4), ALU.mult)))
                    dve_s.on(V.tensor_tensor(Tm2[:, s, :], eye, Tm2[:, s, :], ALU.subtract))

        triangular_inverse(L2, X2, Tm2, LM2, WW2, P, 4, 2, range(1, 7))

        vn = L2
        RR = Tm2[:, 0:4, :]
        S2 = Tm2[:, 4:8, :]
        oA = LM2[:, :, :, :].rearrange("p a b c -> p (a b) c")
        with nc.Block() as block:
            @block.vector
            def _(dve):
                for h in range(GH):
                    dve_s.on(V.tensor_scalar(RR[:, h, :], vtok[:, 2 * h, :], cols[:, 2, h:h + 1], None, ALU.mult))

            @block.tensor
            def _(pe):
                pe.wait_ge(dve_s.sem, dve_s.value)
                for h in range(GH):
                    mm = T.matmul(bank[0][:, h * P:h * P + P], X2[:, 2 * h, :], RR[:, h, :], start=True, stop=True)
                pe_s.on(mm)

            @block.scalar
            def _(act):
                act.wait_ge(pe_s.sem, pe_s.value)
                act_s.on(S.activation(vn[:, 0:4, :], pair(bank[0]), ACT.Copy))

            @block.tensor
            def _(pe):
                pe.wait_ge(act_s.sem, act_s.value)
                for h in range(GH):
                    mm = T.matmul(bank[1][:, h * P:h * P + P], ktok[:, h, :], vn[:, h, :], start=True, stop=True)
                pe_s.on(mm)
                for h in range(GH):
                    mm = T.matmul(bank[2][:, h * P:h * P + P], vn[:, h, :], AT[:, 2 * h, :], start=True, stop=True)
                pe_s.on(mm)

            @block.scalar
            def _(act):
                act.wait_ge(pe_s.sem, pe_s.value - 1)
                act_s.on(S.activation(S2, pair(bank[1]), ACT.Copy))

            @block.tensor
            def _(pe):
                pe.wait_ge(act_s.sem, act_s.value)
                for h in range(GH):
                    mm = T.matmul(bank[3][:, h * P:h * P + P], kg[:, 2 * h + 1, :], S2[:, h, :], start=True, stop=True)
                pe_s.on(mm)

            @block.vector
            def _(dve):
                dve.wait_ge(pe_s.sem, pe_s.value)
                vt = vtok.rearrange("p (h c) t -> p h c t", c=2)
                dve.wait_ge(dve_s.sem, dve_s.on(V.tensor_tensor(RR, vt[:, :, 1, :], pair(bank[3]), ALU.subtract)))
                for h in range(GH):
                    dve_s.on(V.tensor_scalar(RR[:, h, :], RR[:, h, :], cols[:, 3, h:h + 1], None, ALU.mult))

            @block.tensor
            def _(pe):
                pe.wait_ge(dve_s.sem, dve_s.value)
                for h in range(GH):
                    mm = T.matmul(bank[4][:, h * P:h * P + P], X2[:, 2 * h + 1, :], RR[:, h, :], start=True, stop=True)
                pe_s.on(mm)

            @block.scalar
            def _(act):
                act.wait_ge(pe_s.sem, pe_s.value)
                act_s.on(S.activation(vn[:, 4:8, :], pair(bank[4]), ACT.Copy))

            @block.tensor
            def _(pe):
                pe.wait_ge(act_s.sem, act_s.value)
                for h in range(GH):
                    T.matmul(bank[5][:, h * P:h * P + P], S2[:, h, :], qg[:, 2 * h + 1, :], start=True, stop=False)
                    mm = T.matmul(bank[5][:, h * P:h * P + P], vn[:, 4 + h, :], AT[:, 2 * h + 1, :], start=False, stop=True)
                pe_s.on(mm)

            @block.vector
            def _(dve):
                dve.wait_ge(pe_s.sem, pe_s.value)
                ov = oA.rearrange("p (h c) t -> p h c t", c=2)
                dve_s.on(V.tensor_copy(ov[:, :, 0, :], pair(bank[2])))
                dve_s.on(V.tensor_copy(ov[:, :, 1, :], pair(bank[5])))

        oAh = oA.rearrange("p (h c) t -> p h (c t)", c=2)
        two = lambda b: b[:, :].rearrange("p (a b) -> p a b", b=T2)

        def gated_norm(o, sq, norm, gate, gain, dst, per_head):
            with nc.Block() as block:
                @block.vector
                def _(dve):
                    dve_s.on(V.tensor_tensor(sq, o, o, ALU.mult))

                @block.tensor
                def _(pe):
                    pe.wait_ge(dve_s.sem, dve_s.value)
                    for h in range(GH):
                        if per_head:
                            mm = T.matmul(bank[h // 2][:, (h % 2) * T2:(h % 2) * T2 + T2], ones, sq[:, h, :], start=True, stop=True)
                        else:
                            mm = T.matmul(bank[0][:, 0:T2], ones, sq[:, h, :], start=(h == 0), stop=(h == GH - 1))
                    pe_s.on(mm)

                @block.scalar
                def _(act):
                    act_s.on(S.activation(dst, gate, ACT.Sigmoid))
                    act.wait_ge(pe_s.sem, pe_s.value)
                    if per_head:
                        for q in range(2):
                            act_s.on(S.activation(norm[:, 2 * q:2 * q + 2, :], two(bank[q]), ACT.Sqrt, bias=eps_rms, scale=1.0 / P))
                    else:
                        act_s.on(S.activation(norm[:, 0, :], bank[0][:, 0:T2], ACT.Sqrt, bias=eps_rms, scale=1.0 / C))

                @block.vector
                def _(dve):
                    n = GH if per_head else 1
                    dve.wait_ge(act_s.sem, act_s.value)
                    dve.wait_ge(dve_s.sem, dve_s.on(V.reciprocal(norm[:, 0:n, :], norm[:, 0:n, :])))
                    for h in range(GH):
                        dve_s.on(V.scalar_tensor_tensor(out=sq[:, h, :], in0=o[:, h, :], scalar=gain(h), in1=norm[:, h if per_head else 0, :],
                                                        op0=ALU.mult, op1=ALU.mult))
                    dve.wait_ge(dve_s.sem, dve_s.on(V.tensor_tensor(dst, dst, gate, ALU.mult)))
                    dve_s.on(V.tensor_tensor(dst, dst, sq, ALU.mult))

        gated_norm(oAh, WW2.rearrange("p a b c -> p (a b c)").rearrange("p (h t) -> p h t", h=GH), gcB, gate_a,
                   lambda h: param("gdn_norm_w_2"), o_all[:, 0:GH, :], True)

        mh = Memory(sbuf, at2, m2.at - KD * T2 - 16)
        logf, kB = mh.take(GH, T2), mh.take(GH, T2)
        bcum, sgm = mh.take(GH, T2), mh.take(GH, T2)
        E = [mh.take(GH * T2) for _ in range(2)]
        Qb = [mh.take(GH * T2) for _ in range(2)]
        Kb = [mh.take(GH * T2) for _ in range(2)]
        acc = mh.take(2 * GH, P)
        masked = [mh.take(2 * GH, P) for _ in range(1)]
        low2 = Memory(sbuf, over_hm, over_hm + KD * T2 + 12 * (3 + T2))
        cross = low2.take(GH, P)
        itok = low2.take(2 * GH, P)
        oB = low2.take(GH, T2)
        wsq = low2.take(GH, T2)
        flat = lambda ap: ap.rearrange("p h t -> p (h t)")
        with nc.Block() as block:
            @block.scalar
            def _(act):
                act_s.on(S.activation(sgm, f_b, ACT.Sigmoid))
                act_s.on(S.activation(kB, f_b, ACT.Sigmoid, scale=-1.0))
                act_s.on(S.activation(acc, mats(q_b), ACT.Sigmoid))

            @block.gpsimd
            def _(pool):
                for ap in Qb + Kb:
                    pool.wait_ge(pool_s.sem, pool_s.on(G.memset(ap, 0.0)))

            @block.vector
            def _(dve):
                dve.wait_ge(act_s.sem, act_s.value)
                for h in range(GH):
                    dve_s.on(V.tensor_scalar(sgm[:, h, :], sgm[:, h, :], lb1[:, h:h + 1], lb[:, h:h + 1], ALU.mult, ALU.add))
                marks["f"] = dve_s.value
                for h in range(GH):
                    dve_s.on(V.tensor_scalar(kB[:, h, :], kB[:, h, :], lb1[:, h:h + 1], None, ALU.mult))
                dve_s.on(V.tensor_tensor(mats(q_b), mats(q_b), acc, ALU.mult))

            @block.scalar
            def _(act):
                act.wait_ge(dve_s.sem, marks["f"])
                act_s.on(S.activation(logf, sgm, ACT.Ln))

            @block.vector
            def _(dve):
                dve.wait_ge(act_s.sem, act_s.value)
                for h in range(GH):
                    dve_s.on(V.tensor_tensor_scan(bcum[:, h, :], reset128, logf[:, h, :], 0.0, ALU.mult, ALU.add))

            @block.tensor
            def _(pe):
                for h in range(GH):
                    for c in range(2):
                        t = T.transpose(bank[6 + h // 2][:, (h % 2) * 2 * P + c * P:(h % 2) * 2 * P + c * P + P], i_b[:, h, c * P:c * P + P], ident)
                pe_s.on(t)

            @block.scalar
            def _(act):
                act.wait_ge(pe_s.sem, pe_s.value)
                for q in range(2):
                    act_s.on(S.activation(itok[:, 4 * q:4 * q + 4, :], pair(bank[6 + q]), ACT.Copy))

        s_e = Signal(nc, ctx, "level_exponents")
        s_ee = Signal(nc, ctx, "level_decays")
        s_qk = Signal(nc, ctx, "level_operands")
        s_a = Signal(nc, ctx, "level_products")
        s_m = Signal(nc, ctx, "level_masked")
        s_acc = Signal(nc, ctx, "level_added")
        with nc.Block() as block:
            @block.vector
            def _(dve):
                def exponents(n):
                    b = 1 << n
                    v = flat(bcum).rearrange("p (k i t) -> p k i t", i=2, t=b)
                    e = E[n % 2].rearrange("p (k i t) -> p k i t", i=2, t=b)
                    ref = v[:, :, 0, b - 1:b].broadcast_to([P, GH * T2 // (2 * b), b])
                    if n >= 2:
                        dve.wait_ge(s_qk.sem, 2 * (n - 1))
                    s_e.on(V.tensor_tensor(e[:, :, 1, :], v[:, :, 1, :], ref, ALU.subtract))
                    s_e.on(V.tensor_tensor(e[:, :, 0, :], ref, v[:, :, 0, :], ALU.subtract))

                def operands(n):
                    b = 1 << n
                    sh_ = lambda ap: ap.rearrange("p (k i t) -> p k i t", i=2, t=b)
                    dve.wait_ge(s_ee.sem, n + 1)
                    if n >= 2:
                        dve.wait_ge(s_a.sem, n)
                    s_qk.on(V.tensor_tensor(sh_(Qb[n % 2])[:, :, 1, :], sh_(flat(q_b))[:, :, 1, :], sh_(E[n % 2])[:, :, 1, :], ALU.mult))
                    s_qk.on(V.tensor_tensor(sh_(Kb[n % 2])[:, :, 0, :], sh_(flat(kB))[:, :, 0, :], sh_(E[n % 2])[:, :, 0, :], ALU.mult))

                def mask(i):
                    u = ident if i == 0 else upper[i - 1]
                    dve.wait_ge(s_a.sem, i + 1)
                    b0 = (i % 2) * 2
                    dst = acc if i == 0 else masked[0]
                    if i >= 2:
                        dve.wait_ge(s_acc.sem, i - 1)
                    s_m.on(V.tensor_tensor(dst[:, 0:4, :], pair(bank[b0]), bc(u, 4), ALU.mult))
                    s_m.on(V.tensor_tensor(dst[:, 4:8, :], pair(bank[b0 + 1]), bc(u, 4), ALU.mult))

                exponents(0)
                for n in range(7):
                    if n + 1 < 7:
                        exponents(n + 1)
                    operands(n)
                    mask(n)
                mask(7)
                dve.wait_ge(s_qk.sem, 14)
                last = bcum[:, :, P - 1:P].broadcast_to([P, GH, P])
                ex = E[0][:, 0:GH * P].rearrange("p (h t) -> p h t", h=GH)
                s_e.on(V.tensor_tensor(ex, last, bcum[:, :, 0:P], ALU.subtract))
                dve.wait_ge(s_ee.sem, 9)
                dve.wait_ge(s_a.sem, 8)
                s_qk.on(V.tensor_tensor(Kb[0][:, 0:GH * P].rearrange("p (h t) -> p h t", h=GH), kB[:, :, 0:P], ex, ALU.mult))
                s_qk.on(V.tensor_tensor(Qb[0][:, 0:GH * P].rearrange("p (h t) -> p h t", h=GH), q_b[:, :, P:T2],
                                        E[0][:, GH * P:2 * GH * P].rearrange("p (h t) -> p h t", h=GH), ALU.mult))
                dve.wait_ge(s_a.sem, 9)
                s_m.on(V.tensor_copy(cross, pair(bank[4])))

            @block.scalar
            def _(act):
                for n in range(7):
                    act.wait_ge(s_e.sem, 2 * n + 2)
                    s_ee.on(S.activation(E[n % 2], E[n % 2], ACT.Exp))
                act.wait_ge(s_qk.sem, 14)
                s_ee.on(S.activation(E[0][:, GH * P:2 * GH * P].rearrange("p (h t) -> p h t", h=GH), bcum[:, :, P:T2], ACT.Exp))
                act.wait_ge(s_e.sem, 15)
                s_ee.on(S.activation(E[0][:, 0:GH * P], E[0][:, 0:GH * P], ACT.Exp))

            @block.gpsimd
            def _(pool):
                for i in range(1, 8):
                    pool.wait_ge(s_m.sem, 2 * i + 2)
                    if i >= 2:
                        pool.wait_ge(s_acc.sem, i - 1)
                    s_acc.on(G.tensor_tensor(acc, acc, masked[0], ALU.add))

            @block.tensor
            def _(pe):
                for i in range(8):
                    if i:
                        pe.wait_ge(s_qk.sem, 2 * i)
                    if i >= 2:
                        pe.wait_ge(s_m.sem, 2 * (i - 1))
                    for m in range(2 * GH):
                        k_, q_ = ((flat(kB), flat(q_b)) if i == 0 else (Kb[(i - 1) % 2], Qb[(i - 1) % 2]))
                        mm = T.matmul(bank[(i % 2) * 2 + m // 4][:, (m % 4) * P:(m % 4) * P + P], k_[:, m * P:m * P + P],
                                      q_[:, m * P:m * P + P], start=True, stop=True)
                    s_a.on(mm)
                pe.wait_ge(s_qk.sem, 16)
                for h in range(GH):
                    mm = T.matmul(bank[4][:, h * P:h * P + P], Kb[0][:, h * P:h * P + P], Qb[0][:, h * P:h * P + P],
                                  start=True, stop=True)
                s_a.on(mm)
                pe.wait_ge(s_acc.sem, 7)
                pe.wait_ge(s_m.sem, 17)
                for h in range(GH):
                    o = (h % 2) * T2
                    T.matmul(bank[6 + h // 2][:, o:o + P], itok[:, 2 * h, :], acc[:, 2 * h, :], start=True, stop=True)
                    T.matmul(bank[6 + h // 2][:, o + P:o + T2], itok[:, 2 * h, :], cross[:, h, :], start=True, stop=False)
                    mm = T.matmul(bank[6 + h // 2][:, o + P:o + T2], itok[:, 2 * h + 1, :], acc[:, 2 * h + 1, :], start=False, stop=True)
                s_a.on(mm)

            @block.scalar
            def _(act):
                act.wait_ge(s_a.sem, 10)
                for q in range(2):
                    act_s.on(S.activation(oB[:, 2 * q:2 * q + 2, :], two(bank[6 + q]), ACT.Copy))
        gated_norm(oB, wsq, E[0].rearrange("p (h t) -> p h t", h=GH), gate_b, lambda h: param("hg_norm_w_2", h),
                   o_all[:, GH:2 * GH, :], False)

        def mixer_out(engine, m, psum):
            return V.scalar_tensor_tensor(out=xT[:, m, :], in0=psum, scalar=mod[:, 2 * KD + m:2 * KD + m + 1], in1=xT[:, m, :],
                                          op0=ALU.mult, op1=ALU.add)
        project(o_all, T2, [(W_OUT2 + m // 4, (m % 4) * P, P) for m in range(KD)], mixer_out, W_OUT2, 2, owner=lambda m: "dve")
        arena.close()
        ring_stack.close()
        raw_w = ctx.enter_context(nc.sbuf_tensor("raw_weights", [P, RAW, PIECE], F32))
        w_hi = [ctx.enter_context(nc.sbuf_tensor(f"weights_hi{t}", [P, PIECE], F32R)) for t in range(3)]
        w_lo = [ctx.enter_context(nc.sbuf_tensor(f"weights_lo{t}", [P, PIECE], F32R)) for t in range(3)]
        x_hi = ctx.enter_context(nc.sbuf_tensor("x_hi", [P, KD, T2], F32R))
        x_lo = ctx.enter_context(nc.sbuf_tensor("x_lo", [P, KD, T2], F32R))
        hid_hi = ctx.enter_context(nc.sbuf_tensor("hidden_hi", [P, 2, T2], F32R))
        hid_lo = ctx.enter_context(nc.sbuf_tensor("hidden_lo", [P, 2, T2], F32R))
        rest = ctx.enter_context(nc.sbuf_tensor("moe_memory", [P, 10752], F32))
        raw_ready = [Signal(nc, ctx, f"piece_ready{i}") for i in range(RAW)]
        row_ready = [Signal(nc, ctx, f"router_row_ready{i}") for i in range(GROWS)]
        s_gates = Signal(nc, ctx, "gates_stored")
        mm_ = Memory(rest, 0, 10752)
        hB = mm_.take(KD, T2)
        wr = mm_.take(KD, NE)
        scores, sel, rep, tmp64 = (mm_.take(2, NE) for _ in range(4))
        top8 = mm_.take(2, 8, 8)
        gsum, rank = mm_.take(2, 8), mm_.take(2, 8)
        cmp, eqm = mm_.take(2, 8, 8), mm_.take(2, 8, 8)
        total_w = mm_.take(2)
        gatesT = mm_.take(T2)
        gb = mm_.take(GROWS, T2)
        esig = mm_.take(2, 2 * T2)
        eprod = mm_.take(2 * T2)
        hid = mm_.take(2 * T2)
        rs2 = mm_.take(T2)
        zero = mm_.take(512)
        y_tok = mm_.take(2, D)
        sq2 = y_tok.rearrange("p c (j t) -> p (c j) t", t=T2)
        routed = (a["w_gate_2"][0], a["w_up_2"][0], a["w_down_2"][0])
        shared = (a["ws_gate_2"][0], a["ws_up_2"][0], a["ws_down_2"][0])

        def piece_view(ap, t):
            return ap.rearrange("p (k c) -> p k c", c=(FE, FE, D)[t])

        def load_piece(sp, r, t, source):
            sp.dma_start(piece_view(raw_w[:, r, :], t), source.rearrange("(k p) c -> p k c", p=P)).then_inc(raw_ready[r].sem, 16)

        def load_row(sp, q, row):
            sp.dma_start(gb[:, q, :], row.partition_broadcast(P)).then_inc(row_ready[q].sem, 16)

        with nc.Block() as block:
            @block.sync
            def _(sp):
                small_in.on(sp.dma_start(wr, a["w_router_2"][0].rearrange("(k p) e -> p k e", p=P)), 16)
                for t in range(3):
                    load_piece(sp, t, t, shared[t])
                for t in range(3):
                    load_piece(sp, 3 + t, t, routed[t][0])
        rms_norm(xT, hB, lambda j: gain2[:, j:j + 1], lambda j: mod[:, 3 * KD + j:3 * KD + j + 1], T2, sq2, rs2)
        lt8 = small[:, 192:256].rearrange("p (g j) -> p g j", j=8)
        with nc.Block() as block:
            @block.gpsimd
            def _(pool):
                pool.wait_ge(pool_s.sem, pool_s.on(G.memset(lt8, 1.0)))
                pool_s.on(G.affine_select(out=lt8, in_=lt8, compare_op=ALU.is_gt, fill=0.0, base=0,
                                          pattern=[[1, 8], [-1, 8]], channel_multiplier=0))

            @block.tensor
            def _(pe):
                pe.wait_ge(small_in.sem, small_in.value)
                for c in range(2):
                    for k in range(KD):
                        mm = T.matmul(bank[4][:, c * NE:c * NE + NE], hB[:, k, c * P:c * P + P], wr[:, k, :],
                                      start=(k == 0), stop=(k == KD - 1))
                pe_s.on(mm)

            @block.scalar
            def _(act):
                act.wait_ge(pe_s.sem, pe_s.value)
                act_s.on(S.activation(scores, bank[4][:, 0:2 * NE].rearrange("p (a b) -> p a b", b=NE), ACT.Sigmoid))

            @block.vector
            def _(dve):
                def step(instruction):
                    dve.wait_ge(dve_s.sem, dve_s.on(instruction))
                dve.wait_ge(act_s.sem, act_s.value)
                step(V.tensor_tensor(sel, scores, bc(small[:, 128:192], 2), ALU.add))
                for c in range(2):
                    for g in range(8):
                        last = V.max(top8[:, c, g, :], sel[:, c, 8 * g:8 * g + 8])
                        dve_s.on(last)
                dve.wait_ge(dve_s.sem, dve_s.value)
                step(V.tensor_tensor(gsum, top8[:, :, :, 0], top8[:, :, :, 1], ALU.add))
                for c in range(2):
                    mine = gsum[:, c, :].unsqueeze(2).broadcast_to([P, 8, 8])
                    other = gsum[:, c, :].unsqueeze(1).broadcast_to([P, 8, 8])
                    dve_s.on(V.tensor_tensor(cmp[:, c], other, mine, ALU.is_gt))
                    dve_s.on(V.tensor_tensor(eqm[:, c], other, mine, ALU.is_equal))
                dve.wait_ge(dve_s.sem, dve_s.value)
                dve.wait_ge(pool_s.sem, pool_s.value)
                for c in range(2):
                    dve_s.on(V.tensor_tensor(eqm[:, c], eqm[:, c], lt8, ALU.mult))
                dve.wait_ge(dve_s.sem, dve_s.value)
                step(V.tensor_tensor(cmp, cmp, eqm, ALU.add))
                step(V.tensor_reduce(rank, cmp, AX.X, ALU.add))
                step(V.tensor_scalar(rank, rank, 4.0, None, ALU.is_lt))
                for c in range(2):
                    grp = rank[:, c, :].unsqueeze(2).broadcast_to([P, 8, 8])
                    g8 = lambda ap: ap[:, c, :].rearrange("p (g e) -> p g e", e=8)
                    step(V.tensor_tensor(g8(sel), g8(sel), grp, ALU.mult))
                    step(V.tensor_scalar(g8(tmp64), grp, 1.0, -NEG, ALU.subtract, ALU.mult))
                    step(V.tensor_tensor(g8(sel), g8(sel), g8(tmp64), ALU.add))
                    step(V.max(top8[:, c, 0, :], sel[:, c, :]))
                    step(V.match_replace(out=rep[:, c, :], in_to_replace=top8[:, c, 0, :], in_values=sel[:, c, :], imm_value=-3e38))
                step(V.tensor_tensor(rep, rep, sel, ALU.not_equal))
                step(V.tensor_tensor(scores, scores, rep, ALU.mult))
                step(V.tensor_reduce(total_w, scores, AX.X, ALU.add))
                step(V.reciprocal(total_w, total_w))
                for c in range(2):
                    step(V.tensor_scalar(scores[:, c, :], scores[:, c, :], total_w[:, c:c + 1], 2.5, ALU.mult, ALU.mult))

            @block.tensor
            def _(pe):
                pe.wait_ge(dve_s.sem, dve_s.value)
                for c in range(2):
                    t = T.transpose(bank[5][0:NE, c * P:c * P + P], scores[:, c, :], ident)
                pe_s.on(t)

            @block.gpsimd
            def _(pool):
                G.memset(gb[:, 0, :], 1.0).then_inc(row_ready[0].sem, 16)

            @block.scalar
            def _(act):
                act_s.on(S.activation(x_hi[:, :, :], hB, ACT.Copy))

            @block.vector
            def _(dve):
                dve.wait_ge(act_s.sem, act_s.value)
                dve_s.on(V.tensor_tensor(x_lo[:, :, :], hB, x_hi[:, :, :].bitcast(F32), ALU.subtract))
                dve.wait_ge(pe_s.sem, pe_s.value)
                dve_s.on(V.tensor_copy(gatesT[0:NE, :], bank[5][0:NE, 0:T2]))
                dve_s.on(V.memset(zero, 0.0))

            @block.sync
            def _(sp):
                sp.wait_ge(dve_s.sem, dve_s.value - 1)
                s_gates.on(sp.dma_start(gates_dram, gatesT[0:NE, :]), 16)
                sp.wait_ge(s_gates.sem, 16)
                for n in range(1, GROWS):
                    load_row(sp, n, gates_dram[n - 1])

        s_hi = [Signal(nc, ctx, f"hi_ready{t}") for t in range(3)]
        s_lo = [Signal(nc, ctx, f"lo_ready{t}") for t in range(3)]
        s_gate = Signal(nc, ctx, "expert_gate")
        s_up = Signal(nc, ctx, "expert_up")
        s_down = Signal(nc, ctx, "expert_down")
        s_esig = Signal(nc, ctx, "expert_sigmoid")
        s_mul = Signal(nc, ctx, "expert_first_product")
        s_read = Signal(nc, ctx, "expert_banks_read")
        s_ehid = Signal(nc, ctx, "expert_hidden")
        s_hhi = Signal(nc, ctx, "hidden_hi_ready")
        s_hlo = Signal(nc, ctx, "hidden_lo_ready")
        LAST = NE
        with nc.Block() as block:
            @block.sync
            def _(sp):
                def load(n, q, row=True):
                    for t in range(3):
                        sp.wait_ge(s_lo[t].sem, n - 1)
                        load_piece(sp, (3 * q + t) % RAW, t, routed[t][n - 1])
                    if row:
                        sp.wait_ge(s_ehid.sem, n - 1)
                        load_row(sp, (q + 2) % GROWS, gates_dram[n + 1])
                with sp.Fori(0, 15) as i:
                    for q in range(2, 6):
                        load(i * 4 + q, q)
                load(62, 62)
                load(63, 63, False)
                load(64, 64, False)

            @block.tensor
            def _(pe):
                def halves(t):
                    return piece_view(w_hi[t][:, :], t), piece_view(w_lo[t][:, :], t)

                def product(t, par, n):
                    pe.wait_ge(s_lo[t].sem, n + 1)
                    if t == 0:
                        pe.wait_ge(s_read.sem, n + 1)
                    hi, lo = halves(t)
                    for f in range(2):
                        out_ = bank[4 + 2 * par + t][:, f * T2:f * T2 + T2]
                        cut = slice(f * P, f * P + P)
                        for d in range(KD):
                            T.matmul(out_, hi[:, d, cut], x_hi[:, d, :], start=(d == 0), stop=False)
                            T.matmul(out_, hi[:, d, cut], x_lo[:, d, :], start=False, stop=False)
                            mm = T.matmul(out_, lo[:, d, cut], x_hi[:, d, :], start=False, stop=(d == KD - 1))
                    mm.then_inc((s_gate, s_up)[t].sem, 1)

                def down(n):
                    pe.wait_ge(s_lo[2].sem, n + 1)
                    pe.wait_ge(s_hlo.sem, n + 1)
                    hi, lo = halves(2)
                    for d in range(KD):
                        out_ = bank[d // 2][:, (d % 2) * T2:(d % 2) * T2 + T2]
                        cut = slice(d * P, d * P + P)
                        for f in range(2):
                            for w, h in ((hi, hid_hi), (hi, hid_lo), (lo, hid_hi)):
                                mm = T.matmul(out_, w[:, f, cut], h[:, f, :], start=False, stop=False, skip_group_check=True)
                    mm.then_inc(s_down.sem, 1)

                for b in range(4):
                    mm = T.matmul(bank[b][:, :], ident, zero, start=True, stop=False, skip_group_check=True)
                mm.then_inc(s_down.sem, 1)
                product(0, 0, 0)
                product(1, 0, 0)
                with pe.Fori(0, NE // 4) as i:
                    for q in range(4):
                        product(0, (q + 1) % 2, i * 4 + (q + 1))
                        product(1, (q + 1) % 2, i * 4 + (q + 1))
                        down(i * 4 + q)
                down(LAST)

            @block.scalar
            def _(act):
                def cut(t, q, n, arrived):
                    r = (3 * q + t) % RAW
                    act.wait_ge(raw_ready[r].sem, arrived)
                    S.activation(w_hi[t][:, :], raw_w[:, r, :], ACT.Copy).then_inc(s_hi[t].sem, 1)

                def sigmoid(par, n):
                    act.wait_ge(s_gate.sem, n + 1)
                    act.wait_ge(s_read.sem, n + 1)
                    S.activation(esig[:, par, :], bank[4 + 2 * par][:, :], ACT.Sigmoid).then_inc(s_esig.sem, 1)

                def hidden_hi(n):
                    act.wait_ge(s_ehid.sem, n + 1)
                    act.wait_ge(s_down.sem, n + 1)
                    S.activation(hid_hi[:, :, :].rearrange("p f t -> p (f t)"), hid, ACT.Copy).then_inc(s_hhi.sem, 1)

                def expert(q, n, arrived, next_arrived):
                    sigmoid(q % 2, n)
                    cut(0, q + 1, n + 1, next_arrived)
                    act.wait_ge(s_up.sem, n + 1)
                    cut(1, q + 1, n + 1, next_arrived)
                    hidden_hi(n)
                    cut(2, q, n, arrived)
                cut(0, 0, 0, 16)
                cut(1, 0, 0, 16)
                with act.Fori(0, NE // 4) as i:
                    for q in range(4):
                        expert(q, i * 4 + q, i * 32 + 16 * (q // 2 + 1), i * 32 + 16 * ((q + 1) // 2 + 1))
                sigmoid(0, LAST)
                hidden_hi(LAST)
                cut(2, 0, LAST, 16 * (LAST // 2 + 1))

            @block.vector
            def _(dve):
                def rest_of(t, q, n):
                    dve.wait_ge(s_hi[t].sem, n + 1)
                    V.tensor_tensor(w_lo[t][:, :], raw_w[:, (3 * q + t) % RAW, :], w_hi[t][:, :].bitcast(F32),
                                    ALU.subtract).then_inc(s_lo[t].sem, 1)

                def hidden(par, n, q, row):
                    dve.wait_ge(s_esig.sem, n + 1)
                    V.tensor_tensor(eprod, bank[4 + 2 * par][:, :], esig[:, par, :], ALU.mult).then_inc(s_mul.sem, 1)
                    dve.wait_ge(s_mul.sem, n + 1)
                    dve.wait_ge(s_up.sem, n + 1)
                    V.tensor_tensor(eprod, eprod, bank[5 + 2 * par][:, :], ALU.mult).then_inc(s_read.sem, 1)
                    dve.wait_ge(s_read.sem, n + 3)
                    dve.wait_ge(row_ready[q % GROWS].sem, row)
                    V.tensor_tensor(hid.rearrange("p (f t) -> p f t", f=2), eprod.rearrange("p (f t) -> p f t", f=2),
                                    gb[:, q % GROWS, :].unsqueeze(1).broadcast_to([P, 2, T2]), ALU.mult).then_inc(s_ehid.sem, 1)

                def hidden_lo(n):
                    dve.wait_ge(s_hhi.sem, n + 1)
                    V.tensor_tensor(hid_lo[:, :, :].rearrange("p f t -> p (f t)"), hid,
                                    hid_hi[:, :, :].rearrange("p f t -> p (f t)").bitcast(F32), ALU.subtract).then_inc(s_hlo.sem, 1)
                V.memset(eprod[:, 0:1], 0.0).then_inc(s_read.sem, 2)
                dve.wait_ge(s_read.sem, 2)
                rest_of(0, 0, 0)
                rest_of(1, 0, 0)
                with dve.Fori(0, NE // 4) as i:
                    for q in range(4):
                        n = i * 4 + q
                        rest_of(0, q + 1, n + 1)
                        hidden(q % 2, n, q, i * 16 + 16)
                        rest_of(1, q + 1, n + 1)
                        hidden_lo(n)
                        rest_of(2, q, n)
                hidden(0, LAST, 0, 16 * (LAST // 4 + 1))
                hidden_lo(LAST)
                rest_of(2, 0, LAST)

        with nc.Block() as block:
            @block.vector
            def _(dve):
                for m in range(KD):
                    dve_s.on(V.scalar_tensor_tensor(out=xT[:, m, :], in0=bank[m // 2][:, (m % 2) * T2:(m % 2) * T2 + T2],
                                                    scalar=mod[:, 5 * KD + m:5 * KD + m + 1], in1=xT[:, m, :],
                                                    op0=ALU.mult, op1=ALU.add))
        rms_norm(xT, hB, lambda j: param("final_norm_w_2", j), None, T2, sq2, rs2)
        with nc.Block() as block:
            pe0 = pe_s.value

            @block.tensor
            def _(pe):
                for c in range(2):
                    for half in range(2):
                        for j in range(4):
                            t = T.transpose(bank[2 * c + half][:, j * P:j * P + P], hB[:, 4 * half + j, c * P:c * P + P], ident)
                        pe_s.on(t)

            @block.vector
            def _(dve):
                for i in range(0, 4, 2):
                    dve.wait_ge(pe_s.sem, pe0 + i + 1)
                    dve_s.on(V.tensor_copy(y_tok[:, i // 2, 0:512], bank[i][:, :]))

            @block.scalar
            def _(act):
                for i in range(1, 4, 2):
                    act.wait_ge(pe_s.sem, pe0 + i + 1)
                    act_s.on(S.activation(y_tok[:, i // 2, 512:D], bank[i][:, :], ACT.Copy))

            @block.sync
            def _(sp):
                for c in range(2):
                    sp.wait_ge(dve_s.sem, dve_s.value - 1 + c)
                    sp.wait_ge(act_s.sem, act_s.value - 1 + c)
                    stored.on(sp.dma_start(out[0, c * P:c * P + P, :], y_tok[:, c, :]), 16)
                sp.wait_ge(stored.sem, stored.value)


INPUTS = ["x", "meta_tokens", "norm_mix", "norm_ffn", "norm_final", "w_in", "mu_rw", "w0", "w_up", "a0", "a_up",
          "g_up", "k_k", "k_a", "r_k", "ln_x_w", "ln_x_b", "w_sb_out", "w_rw_out", "w_out", "w_ffn_in",
          "w_ffn_out", "c_2", "w_ada_2", "b_ada_2", "norm1_w_2", "w_in_2", "conv_w_2", "gdn_a_log_2",
          "gdn_dt_bias_2", "gdn_norm_w_2", "hg_lb_2", "hg_norm_w_2", "w_out_2", "norm2_w_2", "w_router_2",
          "router_bias_2", "w_gate_2", "w_up_2", "w_down_2", "ws_gate_2", "ws_up_2", "ws_down_2",
          "final_norm_w_2"]


def kernel(**inputs):
    import concourse.bacc as bacc
    from concourse.bass_utils import run_bass_kernel_spmd

    nc = bacc.Bacc("TRN2", target_bir_lowering=False, num_devices=1)
    arrays, aps = {}, {}
    for name in INPUTS:
        array = np.ascontiguousarray(inputs[name])
        arrays[f"in_{name}"] = array
        aps[name] = nc.dram_tensor(f"in_{name}", array.shape, mybir.dt.from_np(array.dtype), kind="ExternalInput").ap()
    out = nc.dram_tensor("out", (1, SEQ, D), F32, kind="ExternalOutput").ap()
    build(nc, aps, out)
    result = run_bass_kernel_spmd(nc, [arrays], core_ids=[0])
    return result.results[0]["out"]
```

```python
import numpy as np

import concourse.bass as bass
from concourse import mybir
from contextlib import ExitStack

F32 = mybir.dt.float32
F32R = mybir.dt.float32r
ALU = mybir.AluOpType
ACT = mybir.ActivationFunctionType
AX = mybir.AxisListType

P = 128
D = 1024
KD = D // P
N_META, SEQ = 16, 256
T1 = N_META + SEQ
T1P = 320
HEADS, DH = 8, 64
C = HEADS * DH
CT = C // P
CH = 64
NCH = T1P // CH
NM = NCH * HEADS
FFN = 2816
FT = FFN // P
T2 = SEQ
GH = 4
NE, FE = 64, 256
SLOT = 4096
RING = 3
PIECE = 2048
RAW = 6
GROWS = 4
SBUF_FLOATS = 53208
CONSTS = 5600

RMS_EPS = 1e-6
GN_EPS = 64e-5
NEG = -1e30


class Signal:

    def __init__(self, nc, ctx, name):
        self.sem = ctx.enter_context(nc.semaphore(name))
        self.value = 0

    def on(self, instruction, by=1):
        instruction.then_inc(self.sem, by)
        self.value += by
        return self.value


class Memory:

    def __init__(self, tensor, at, end):
        self.tensor, self.at, self.end = tensor, at, end

    def take(self, *shape):
        n = int(np.prod(shape))
        view = self.view(self.at, *shape)
        self.at += n
        assert self.at <= self.end, (self.at, self.end)
        return view

    def view(self, at, *shape):
        assert at + int(np.prod(shape)) <= self.end
        n = int(np.prod(shape))
        flat = self.tensor[:, at:at + n]
        if len(shape) == 1:
            return flat
        names = "abcd"[:len(shape)]
        spec = "p (" + " ".join(names) + ") -> p " + " ".join(names)
        return flat.rearrange(spec, **{k: v for k, v in zip(names, shape)})


def param_rows(groups):
    table, row = {}, 0
    for name, size in groups:
        n = -(-size // P)
        table[name] = (row, size)
        row += n
    assert row <= P
    return table


ROWS0 = param_rows([("norm_mix", D), ("norm_ffn", D), ("norm_final", D), ("mu_rw", 3 * C + 288), ("w0", C),
                    ("a0", C), ("k_k", C), ("k_a", C), ("r_k", C), ("ln_x_w", C), ("ln_x_b", C), ("c_2", D),
                    ("gdn_norm_w_2", P), ("hg_lb_2", 2 * C), ("hg_norm_w_2", C), ("norm1_w_2", D),
                    ("norm2_w_2", D), ("final_norm_w_2", D)])
ROWS1 = param_rows([("conv_w_2", 4 * 3 * C), ("b_ada_2", 6 * D)])


def build(nc, a, out):
    ctx = ExitStack()
    with ctx:
        kept = ctx.enter_context(nc.sbuf_tensor("kept", [P, CONSTS + KD * T1], F32))
        total = SBUF_FLOATS - CONSTS - KD * T1 - RING * SLOT
        ring_stack = ExitStack()
        ring = ring_stack.enter_context(nc.sbuf_tensor("weight_ring", [P, RING, SLOT], F32))
        arena = ExitStack()
        FIRST = (KD + 2 + 4 * CT) * T1 + CT * 3 * P + 3 * C + 15 * (1 + T1)
        first_kept = arena.enter_context(nc.sbuf_tensor("mixer1_kept", [P, FIRST], F32))
        bank = [ctx.enter_context(nc.psum_tensor(f"bank{i}", [P, 512], F32)) for i in range(8)]
        gates_dram = nc.dram_tensor("gates_scratch", [NE, T2], F32, kind="Internal").ap()

        mem = Memory(kept, 0, CONSTS)
        view = Memory(first_kept, 0, FIRST).view

        ident = mem.take(P)
        ones = mem.take(P)
        blk64 = mem.take(P)
        tri = mem.take(P)
        ATT = T1 + (T1 - P) + (T1 - 2 * P)
        eye2 = mem.take(CH)
        drop = mem.take(ATT)
        rw_mask = mem.take(P)
        upper = [mem.take(P) for _ in range(7)]
        lower = [mem.take(P) for _ in range(7)]
        upper_strict, upper_incl = mem.take(P), mem.take(P)
        reset64 = mem.take(T1P)
        reset128 = mem.take(T2)
        eps_rms, eps_gn, one_col = mem.take(1), mem.take(1), mem.take(1)
        vec0, vec1 = mem.take(P), mem.take(P)
        row_sel = mem.take(GH, P)
        small = mem.take(256)
        mod = mem.take(6 * KD)
        csil = mem.take(KD, 1)
        gain1, gain2 = mem.take(KD), mem.take(KD)
        e_hg, lb, lb1 = mem.take(2 * GH), mem.take(GH), mem.take(GH)

        def param(name, i=0):
            if name in ROWS0:
                r = ROWS0[name][0] + i
                return vec0[:, r:r + 1]
            r = ROWS1[name][0] + i
            return vec1[:, r:r + 1]

        pe_s = Signal(nc, ctx, "tensor_done")
        act_s = Signal(nc, ctx, "scalar_done")
        dve_s = Signal(nc, ctx, "vector_done")
        pool_s = Signal(nc, ctx, "gpsimd_done")
        small_in = Signal(nc, ctx, "small_loads")
        tokens_in = Signal(nc, ctx, "token_loads")
        stored = Signal(nc, ctx, "stored")
        slot_ready = [Signal(nc, ctx, f"slot_ready{i}") for i in range(RING)]
        V, S, G, T = nc.vector, nc.scalar, nc.gpsimd, nc.tensor

        def columns(w, a0, a1):
            return [(w[:, a0:a1].rearrange("(k p) c -> p k c", p=P), 0, a1 - a0)]

        plan = []
        w_in, w_in2 = a["w_in"][0], a["w_in_2"][0]
        edges = [0, 512, 1024, 1536, 2048, 2560, 3072, 3360, 3872, 4384, 4896, 5408]
        for c0, c1 in zip(edges, edges[1:]):
            plan.append((KD, c1 - c0, columns(w_in, c0, c1)))
        SB_OUT = len(plan)
        plan.append((CT, D, columns(a["w_sb_out"][0], 0, D)))
        plan.append((CT, D, columns(a["w_rw_out"][0], 0, D)))
        W_OUT = len(plan)
        for n in range(2):
            plan.append((KD, 512, columns(a["w_out"][0], 512 * n, 512 * n + 512)))
        FFN_IN = len(plan)
        wf = a["w_ffn_in"][0]
        for n in range(FT // 2):
            plan.append((KD, 512, [(wf[:, s + 256 * n:s + 256 * n + 256].rearrange("(k p) c -> p k c", p=P), o, 256)
                                   for s, o in ((0, 0), (FFN, 256))]))
        FFN_OUT = len(plan)
        for n in range(0, FT, 4):
            rows = min(4, FT - n)
            plan.append((rows, D, [(a["w_ffn_out"][0][n * P:(n + rows) * P, :].rearrange("(k p) c -> p k c", p=P), 0, D)]))
        W_IN2 = len(plan)
        for c0 in [0, 512, 1024, 1536, 2056, 2568, 3080, 3592]:
            plan.append((KD, 512, columns(w_in2, c0, c0 + 512)))
        W_OUT2 = len(plan)
        for n in range(2):
            plan.append((KD, 512, columns(a["w_out_2"][0], 512 * n, 512 * n + 512)))

        ready_at, counts = [], [0] * RING
        for n, (_, _, parts) in enumerate(plan):
            counts[n % RING] += 16 * len(parts)
            ready_at.append(counts[n % RING])
        slot_freed = {}
        issued = [0]

        def slot(n):
            rows, width, _ = plan[n]
            return ring[:, n % RING, 0:rows * width].rearrange("p (k c) -> p k c", k=rows)

        def load_slots(sp, upto):
            while issued[0] < min(upto, len(plan)):
                n = issued[0]
                if n >= RING:
                    done, by = slot_freed[n - RING]
                    sp.wait_ge(done.sem, by)
                for src, c0, w in plan[n][2]:
                    slot_ready[n % RING].on(sp.dma_start(slot(n)[:, :, c0:c0 + w], src), 16)
                issued[0] += 1

        def await_slot(pe, n):
            pe.wait_ge(slot_ready[n % RING].sem, ready_at[n])

        tok = view(0, 3, D)
        rows0 = view(3 * D, P)
        rows1 = view(3 * D + P, P)
        top = FIRST
        hT = Memory(kept, CONSTS, CONSTS + KD * T1).take(KD, T1)
        wa_up = view(top - C, C)
        g_up0 = view(top - 2 * C, C)
        g_up1 = view(top - 3 * C, C)
        top -= 3 * C
        NT_TOK = [P, P, T1 - 2 * P]
        with nc.Block() as block:
            @block.vector
            def _(dve):
                dve_s.on(V.memset(rows0, 0.0))
                dve_s.on(V.memset(rows1, 0.0))
                dve_s.on(V.memset(eps_rms, RMS_EPS))
                dve_s.on(V.memset(eps_gn, GN_EPS))
                dve_s.on(V.memset(one_col, 1.0))

            @block.sync
            def _(sp):
                sp.wait_ge(dve_s.sem, 2)
                for table, rows in ((ROWS0, rows0), (ROWS1, rows1)):
                    for name, (row, size) in table.items():
                        src = a[name]
                        names = "abcd"[:len(src.shape)]
                        flat = src.rearrange(" ".join(names) + " -> (" + " ".join(names) + ")") if len(names) > 1 else src
                        n = size // P
                        small_in.on(sp.dma_start(rows[row:row + n, :], flat[0:n * P].rearrange("(r c) -> r c", c=P)), 16)
                        if size % P:
                            small_in.on(sp.dma_start(rows[row + n:row + n + 1, 0:size % P],
                                                     flat[n * P:size].rearrange("(r c) -> r c", r=1)), 16)
                small_in.on(sp.dma_start(wa_up[0:64, :], a["w_up"][0]), 16)
                small_in.on(sp.dma_start(wa_up[64:128, :], a["a_up"][0]), 16)
                small_in.on(sp.dma_start(g_up0, a["g_up"][0][0:P, :]), 16)
                small_in.on(sp.dma_start(g_up1[0:32, :], a["g_up"][0][P:P + 32, :]), 16)
                wba = w_in2[:, 2048:2056].rearrange("(k p) c -> p k c", p=P)
                small_in.on(sp.dma_start(small[:, 0:64].rearrange("p (k c) -> p k c", c=8), wba), 16)
                small_in.on(sp.dma_start(small[0:GH, 64:65], a["gdn_a_log_2"].rearrange("a h -> h a")), 16)
                small_in.on(sp.dma_start(small[0:GH, 65:66], a["gdn_dt_bias_2"].rearrange("a h -> h a")), 16)
                small_in.on(sp.dma_start(small[:, 128:192], a["router_bias_2"].partition_broadcast(P).rearrange("p a e -> p (a e)")), 16)
                load_slots(sp, RING)

            @block.scalar
            def _(act):
                x = a["x"][0]
                tokens_in.on(act.dma_start(tok[0:N_META, 0, :], a["meta_tokens"]), 16)
                tokens_in.on(act.dma_start(tok[N_META:P, 0, :], x[0:P - N_META, :]), 16)
                tokens_in.on(act.dma_start(tok[:, 1, :], x[P - N_META:2 * P - N_META, :]), 16)
                tokens_in.on(act.dma_start(tok[0:T1 - 2 * P, 2, :], x[2 * P - N_META:SEQ, :]), 16)

            @block.gpsimd
            def _(pool):
                def step(instruction):
                    pool.wait_ge(pool_s.sem, pool_s.on(instruction))

                def fill(ap, value):
                    step(G.memset(ap, value))

                def select(ap, pattern, base_, cm, op, fill_=0.0):
                    step(G.affine_select(out=ap, in_=ap, compare_op=op, fill=fill_, base=base_,
                                         pattern=pattern, channel_multiplier=cm))
                fill(ident, 0.0)
                select(ident, [[-1, P]], 0, 1, ALU.not_equal, 1.0)
                fill(ones, 1.0)
                fill(eye2, 0.0)
                select(eye2, [[-1, CH]], 0, 1, ALU.not_equal, 1.0)
                select(eye2, [[-1, CH]], -CH, 1, ALU.not_equal, 1.0)
                fill(blk64, 0.0)
                fill(blk64[0:64, 0:64], 1.0)
                fill(blk64[64:128, 64:128], 1.0)
                fill(tri, 1.0)
                select(tri, [[-1, P]], 0, 1, ALU.is_ge)
                fill(drop, 0.0)
                at = 0
                for i in range(3):
                    n = T1 - i * P
                    select(drop[:, at:at + n], [[1, n]], 0, -1, ALU.is_gt, NEG)
                    at += n
                fill(rw_mask, 1.0)
                scratch = row_sel[:, 0, :]
                fill(scratch, 1.0)
                select(rw_mask[:, 0:64], [[1, 64]], 0, -1, ALU.is_gt)
                select(rw_mask[:, 64:128], [[1, 64]], 0, -1, ALU.is_ge)
                select(scratch[:, 0:64], [[1, 64]], 64, -1, ALU.is_gt)
                select(scratch[:, 64:128], [[1, 64]], 64, -1, ALU.is_ge)
                select(scratch, [[0, P]], -64, 1, ALU.is_ge)
                step(G.tensor_tensor(rw_mask, rw_mask, scratch, ALU.add))
                for n in range(7):
                    b = 1 << n
                    u = upper[n].rearrange("p (k c) -> p k c", c=2 * b)
                    fill(upper[n], 0.0)
                    fill(u[:, :, b:2 * b], 1.0)
                    select(u, [[-2 * b, P // (2 * b)], [0, 2 * b]], 0, 1, ALU.is_ge)
                    select(u, [[2 * b, P // (2 * b)], [0, 2 * b]], b - 1, -1, ALU.is_ge)
                    w = lower[n].rearrange("p (k c) -> p k c", c=2 * b)
                    fill(lower[n], 0.0)
                    fill(w[:, :, 0:b], 1.0)
                    select(w, [[-2 * b, P // (2 * b)], [0, 2 * b]], -b, 1, ALU.is_ge)
                    select(w, [[2 * b, P // (2 * b)], [0, 2 * b]], 2 * b - 1, -1, ALU.is_ge)
                fill(upper_strict, 1.0)
                select(upper_strict, [[1, P]], 0, -1, ALU.is_gt)
                fill(upper_incl, 1.0)
                select(upper_incl, [[1, P]], 0, -1, ALU.is_ge)
                fill(reset64, 1.0)
                fill(reset64.rearrange("p (k c) -> p k c", c=CH)[:, :, 0:1], 0.0)
                fill(reset128, 1.0)
                fill(reset128.rearrange("p (k c) -> p k c", c=P)[:, :, 0:1], 0.0)
                fill(row_sel, 0.0)
                select(row_sel, [[-1, GH], [0, P]], 0, 1, ALU.not_equal, 1.0)

            @block.tensor
            def _(pe):
                pe.wait_ge(pool_s.sem, 2)
                pe.wait_ge(tokens_in.sem, tokens_in.value)
                for j in range(KD):
                    for i, n in enumerate(NT_TOK):
                        t = T.transpose(bank[j][:, i * P:i * P + n], tok[0:n, i, j * P:j * P + P], ident[0:n, 0:n])
                    pe_s.on(t)
                pe.wait_ge(small_in.sem, small_in.value)
                pe.wait_ge(act_s.sem, 1)
                T.transpose(bank[0][:, 0:P], rows0, ident)
                pe_s.on(T.transpose(bank[0][:, P:2 * P], rows1, ident))

            @block.scalar
            def _(act):
                for j in range(0, KD, 2):
                    act.wait_ge(pe_s.sem, j + 1)
                    act_s.on(S.activation(hT[:, j, :], bank[j][:, 0:T1], ACT.Copy))

            @block.vector
            def _(dve):
                for j in range(1, KD, 2):
                    dve.wait_ge(pe_s.sem, j + 1)
                    dve_s.on(V.tensor_copy(hT[:, j, :], bank[j][:, 0:T1]))
                dve.wait_ge(pe_s.sem, KD + 1)
                dve_s.on(V.tensor_copy(vec0, bank[0][:, 0:P]))
                dve_s.on(V.tensor_copy(vec1, bank[0][:, P:2 * P]))

        def rms_norm(src, dst, gain, shift, n, square, rstd):
            with nc.Block() as block:
                pe0, act0, dve0 = pe_s.value, act_s.value, dve_s.value

                @block.vector
                def _(dve):
                    for j in range(0, KD, 2):
                        dve_s.on(V.tensor_tensor(square[:, j, :], src[:, j, :], src[:, j, :], ALU.mult))

                @block.scalar
                def _(act):
                    for j in range(1, KD, 2):
                        act_s.on(S.activation(square[:, j, :], src[:, j, :], ACT.Square))

                @block.tensor
                def _(pe):
                    for j in range(KD):
                        done, before = ((dve_s, dve0), (act_s, act0))[j % 2]
                        pe.wait_ge(done.sem, before + j // 2 + 1)
                        m = T.matmul(bank[0][:, 0:n], ones, square[:, j, :], start=(j == 0), stop=(j == KD - 1))
                    pe_s.on(m)

                @block.scalar
                def _(act):
                    act.wait_ge(pe_s.sem, pe0 + 1)
                    act_s.on(S.activation(rstd, bank[0][:, 0:n], ACT.Sqrt, bias=eps_rms, scale=1.0 / D))

                @block.vector
                def _(dve):
                    dve.wait_ge(act_s.sem, act_s.value)
                    dve.wait_ge(dve_s.sem, dve_s.on(V.reciprocal(rstd, rstd)))
                    for j in range(KD):
                        dve_s.on(V.scalar_tensor_tensor(out=dst[:, j, :], in0=src[:, j, :], scalar=gain(j),
                                                        in1=rstd, op0=ALU.mult, op1=ALU.mult))

                if shift is not None:
                    @block.scalar
                    def _(act):
                        for j in range(KD):
                            act.wait_ge(dve_s.sem, dve_s.value - KD + 1 + j)
                            act_s.on(S.activation(dst[:, j, :], dst[:, j, :], ACT.Identity, bias=shift(j)))

        CUT = 3
        s_thi = Signal(nc, ctx, "tile_hi_ready")
        s_tlo = Signal(nc, ctx, "tile_lo_ready")

        def split_memory(stack, phase, rows, n):
            take = lambda name, shape: stack.enter_context(nc.sbuf_tensor(phase + name, shape, F32R))
            return (take("x_hi", [P, rows, n]), take("x_lo", [P, rows, n]),
                    [take(f"w_hi{i}", [P, KD, P]) for i in range(CUT)], [take(f"w_lo{i}", [P, KD, P]) for i in range(CUT)])

        def project(sources, n, tiles, evacuate, first_slot, n_slots, parts, owner=lambda m: ("act", "dve")[m % 2]):
            x_hi, x_lo, w_hi, w_lo = parts
            pe0, lo0 = pe_s.value, s_tlo.value
            emptied, value = [], {"act": act_s.value, "dve": dve_s.value}
            for m in range(len(tiles)):
                value[owner(m)] += 1
                emptied.append((act_s if owner(m) == "act" else dve_s, value[owner(m)]))
            order = [("x", 0)] + [("w", m) for m in range(CUT)] + [("x", i) for i in range(1, len(sources))]
            ahead = len(order)
            order += [("w", m) for m in range(CUT, len(tiles))]
            split_at = {part: lo0 + i + 1 for i, part in enumerate(order)}
            for m, (s, _, _, _) in enumerate(tiles):
                slot_freed[s] = s_tlo, split_at["w", m]
            first_row = [sum(ap.shape[1] for ap in sources[:i]) for i in range(len(sources))]

            def operands(part):
                kind, i = part
                if kind == "x":
                    rows = slice(first_row[i], first_row[i] + sources[i].shape[1])
                    return sources[i], x_hi[:, rows, :], x_lo[:, rows, :]
                s, c0, w, _ = tiles[i]
                rows = plan[s][0]
                return slot(s)[:, :, c0:c0 + w], w_hi[i % CUT][:, 0:rows, 0:w], w_lo[i % CUT][:, 0:rows, 0:w]

            with nc.Block() as block:
                @block.sync
                def _(sp):
                    load_slots(sp, first_slot + n_slots + RING)

                @block.scalar
                def _(act):
                    def cut(part):
                        if part[0] == "w":
                            await_slot(act, tiles[part[1]][0])
                            if part[1] >= CUT:
                                act.wait_ge(pe_s.sem, pe0 + part[1] - CUT + 1)
                        src, hi, _ = operands(part)
                        s_thi.on(S.activation(hi, src, ACT.Copy))
                    for part in order[:ahead]:
                        cut(part)
                    for m in range(len(tiles)):
                        if owner(m) == "act":
                            act.wait_ge(pe_s.sem, pe0 + m + 1)
                            act_s.on(evacuate(act, m, bank[m % 8][0:tiles[m][2], 0:n]))
                        if m + CUT < len(tiles):
                            cut(("w", m + CUT))

                @block.vector
                def _(dve):
                    def rest_of(part):
                        dve.wait_ge(s_thi.sem, split_at[part])
                        src, hi, lo = operands(part)
                        s_tlo.on(V.tensor_tensor(lo, src, hi.bitcast(F32), ALU.subtract))
                    for part in order[:ahead]:
                        rest_of(part)
                    for m in range(len(tiles)):
                        if owner(m) == "dve":
                            dve.wait_ge(pe_s.sem, pe0 + m + 1)
                            dve_s.on(evacuate(dve, m, bank[m % 8][0:tiles[m][2], 0:n]))
                        if m + CUT < len(tiles):
                            rest_of(("w", m + CUT))

                @block.tensor
                def _(pe):
                    for m, (s, c0, w, source) in enumerate(tiles):
                        pe.wait_ge(s_tlo.sem, max(split_at["w", m], split_at["x", source]))
                        if m >= 8:
                            done, by = emptied[m - 8]
                            pe.wait_ge(done.sem, by)
                        _, hi, lo = operands(("w", m))
                        rows, r0 = plan[s][0], first_row[source]
                        for k in range(rows):
                            for weights, x in ((hi, x_hi), (hi, x_lo), (lo, x_hi)):
                                mm = T.matmul(bank[m % 8][0:w, 0:n], weights[:, k, :], x[:, r0 + k, :],
                                              start=(k == 0 and weights is hi and x is x_hi), stop=(k == rows - 1 and weights is lo))
                        pe_s.on(mm)

        m1 = Memory(first_kept, 0, top - 15 * (1 + T1))
        xnT = m1.take(KD, T1)
        g_in = m1.take(2, T1)
        y_sb = m1.take(CT, T1)
        y_rw = m1.take(CT, T1)
        after_mixer = m1.at
        qT = m1.take(CT, T1)
        kT = m1.take(CT, 3 * P)
        vT = m1.take(CT, T1)
        raw = view(top - 15 * (1 + T1), 15, 1 + T1)
        over_qkv = Memory(first_kept, after_mixer, FIRST)
        rms_norm(hT, xnT, lambda j: param("norm_mix", j), None, T1, over_qkv.take(KD, T1), over_qkv.take(T1))

        tiles = [(m // 4, (m % 4) * P, P, 0) for m in range(24)] + [(6, 0, P, 0), (6, P, P, 0), (6, 2 * P, 32, 0)]

        def put_in(engine, m, psum):
            w = tiles[m][2]
            if m < 4:
                if engine is nc.scalar:
                    return S.activation(qT[:, m, :], psum, ACT.Copy, scale=DH ** -0.5)
                return V.tensor_scalar(qT[:, m, :], psum, DH ** -0.5, None, ALU.mult)
            dst = (kT[:, m - 4, 0:T1] if m < 8 else vT[:, m - 8, :] if m < 12
                   else raw[0:w, m - 12, 1:1 + T1])
            if engine is nc.scalar:
                return S.activation(dst, psum, ACT.Copy)
            return V.tensor_copy(dst, psum)

        with nc.Block() as block:
            @block.gpsimd
            def _(pool):
                for ap in (kT[:, :, T1:3 * P], raw[:, :, 0:1], raw[32:64, 14, :], raw[64:128, 14, :]):
                    pool.wait_ge(pool_s.sem, pool_s.on(G.memset(ap, 0.0)))
        with ExitStack() as stack:
            project([xnT], T1, tiles, put_in, 0, 7, split_memory(stack, "in_", KD, T1))

        SEG = [(0, 0, T1), (T1, P, T1 - P), (2 * T1 - P, 2 * P, T1 - 2 * P)]
        MIX = total - FIRST - 16
        mixer_stack = ExitStack()
        mixer = mixer_stack.enter_context(nc.sbuf_tensor("mixer1_memory", [P, MIX], F32))
        ma = Memory(mixer, 0, MIX)
        v_tok = ma.take(3, C)
        zm = [ma.take(ATT) for _ in range(HEADS)]
        sp_ = [ma.take(ATT) for _ in range(HEADS)]
        with nc.Block() as block:
            @block.gpsimd
            def _(pool):
                pool_s.on(G.memset(v_tok[:, 2, :], 0.0))

            @block.tensor
            def _(pe):
                for i, n in enumerate(NT_TOK):
                    for j in range(CT):
                        t = T.transpose(bank[i][0:n, j * P:j * P + P], vT[:, j, i * P:i * P + n], ident)
                    pe_s.on(t)

            @block.vector
            def _(dve):
                dve.wait_ge(pool_s.sem, pool_s.value)
                for i, n in enumerate(NT_TOK):
                    dve.wait_ge(pe_s.sem, pe_s.value - 2 + i)
                    dve_s.on(V.tensor_copy(v_tok[0:n, i, :], bank[i][0:n, :]))

        s_z = Signal(nc, ctx, "scores_ready")
        s_zm = Signal(nc, ctx, "masked_scores")
        s_abs = Signal(nc, ctx, "abs_scores")
        s_exp = Signal(nc, ctx, "exp_abs")
        s_ln = Signal(nc, ctx, "log_term")
        s_sp = Signal(nc, ctx, "softplus_ready")
        s_c = Signal(nc, ctx, "suffix_sums")
        s_la = Signal(nc, ctx, "log_weights")
        s_att = Signal(nc, ctx, "weights_ready")
        s_y = Signal(nc, ctx, "head_out")
        s_ycopy = Signal(nc, ctx, "head_out_copied")
        with nc.Block() as block:
            @block.tensor
            def _(pe):
                for h in range(HEADS):
                    lo = DH * (h % 2)
                    if h >= 4:
                        pe.wait_ge(s_zm.sem, h - 3)
                    for i, (c, q0, n) in enumerate(SEG):
                        m = T.matmul(bank[h % 4][:, c:c + n], kT[lo:lo + DH, h // 2, i * P:i * P + P],
                                     qT[lo:lo + DH, h // 2, q0:q0 + n], start=True, stop=True)
                    s_z.on(m)

                def sums(h):
                    b = 4 + h % 2
                    pe.wait_ge(s_sp.sem, h + 1)
                    if h >= 2:
                        pe.wait_ge(s_la.sem, h - 1)
                    for i in range(3):
                        c, q0, n = SEG[i]
                        m = T.matmul(bank[b][:, c:c + n], tri, sp_[h][:, c:c + n], start=True, stop=(i == 2))
                        for i2 in range(i + 1, 3):
                            c2, q2, n2 = SEG[i2]
                            o = c + q2 - q0
                            T.matmul(bank[b][:, o:o + n2], ones, sp_[h][:, c2:c2 + n2], start=False, stop=(i2 == 2))
                    s_c.on(m)

                def out_(h):
                    lo = DH * (h % 2)
                    pe.wait_ge(s_att.sem, h + 1)
                    if h >= 2:
                        pe.wait_ge(s_ycopy.sem, h - 1)
                    for i, (c, q0, n) in enumerate(SEG):
                        m = T.matmul(bank[6 + h % 2][lo:lo + DH, q0:T1], v_tok[:, i, h * DH:h * DH + DH],
                                     zm[h][:, c:c + n], start=(i == 0), stop=(i == 2))
                    s_y.on(m)

                for h in range(HEADS):
                    sums(h)
                    if h >= 2:
                        out_(h - 2)
                out_(HEADS - 2)
                out_(HEADS - 1)

            @block.scalar
            def _(act):
                for h in range(HEADS):
                    act.wait_ge(s_abs.sem, h + 1)
                    s_exp.on(S.activation(sp_[h], sp_[h], ACT.Exp))
                for h in range(HEADS):
                    act.wait_ge(s_exp.sem, h + 1)
                    s_ln.on(S.activation(sp_[h], sp_[h], ACT.Ln, bias=one_col))
                for h in range(HEADS):
                    act.wait_ge(s_la.sem, h + 1)
                    s_att.on(S.activation(zm[h], zm[h], ACT.Exp))

            @block.vector
            def _(dve):
                for h in range(HEADS):
                    dve.wait_ge(s_z.sem, h + 1)
                    s_zm.on(V.tensor_tensor(zm[h], bank[h % 4][:, 0:ATT], drop, ALU.add))
                    dve.wait_ge(s_zm.sem, h + 1)
                    s_abs.on(V.scalar_tensor_tensor(out=sp_[h], in0=zm[h], scalar=-1.0, in1=zm[h], op0=ALU.mult, op1=ALU.min))

                def softplus(h):
                    dve.wait_ge(s_ln.sem, h + 1)
                    s_sp.on(V.scalar_tensor_tensor(out=sp_[h], in0=zm[h], scalar=0.0, in1=sp_[h], op0=ALU.max, op1=ALU.add))

                def log_weights(h):
                    dve.wait_ge(s_c.sem, h + 1)
                    s_la.on(V.tensor_tensor(zm[h], zm[h], bank[4 + h % 2][:, 0:ATT], ALU.subtract))

                def copy_out(h):
                    lo = DH * (h % 2)
                    dve.wait_ge(s_y.sem, h + 1)
                    s_ycopy.on(V.tensor_copy(y_sb[lo:lo + DH, h // 2, :], bank[6 + h % 2][lo:lo + DH, 0:T1]))

                softplus(0)
                softplus(1)
                for h in range(HEADS):
                    if h + 2 < HEADS:
                        softplus(h + 2)
                    log_weights(h)
                    if h >= 3:
                        copy_out(h - 3)
                for h in range(HEADS - 3, HEADS):
                    copy_out(h)
        mr = Memory(mixer, 0, MIX)
        vS = mr.take(CT, CH + T1P)
        rk = mr.take(CT, T1)
        Q2 = mr.take(CT, NCH, 2, CH)
        at_K2 = mr.at
        K2 = mr.take(CT, NCH, 2, CH)
        at_K2tok = mr.at
        sh = mr.take(9, T1)
        c_sum = mr.take(CT, T1P)
        e_pos = mr.take(CT, T1P)
        e_neg = mr.take(CT, T1P)
        rate = mr.take(CT, T1)
        kk = mr.take(CT, T1)
        work = mr.take(CT, T1)
        ld = view(top - 15 * (1 + T1), CT, T1P)
        grow = view(top - 15 * (1 + T1) + CT * T1P, CT, T1)
        chunks = lambda ap, n: ap[:, :, 0:n * CH].rearrange("p j (c t) -> p j c t", t=CH)

        marks = {}
        with nc.Block() as block:
            @block.gpsimd
            def _(pool):
                for ap in (vS[:, :, 0:CH], vS[:, :, CH + T1:CH + T1P], Q2[:, :, NCH - 1, :, :], K2[:, :, NCH - 1, :, :]):
                    pool.wait_ge(pool_s.sem, pool_s.on(G.memset(ap, 0.0)))

            @block.vector
            def _(dve):
                for first, count, dst in ((0, 4, lambda j: sh[:, j, :]), (4, 4, lambda j: sh[:, 4 + j, :]),
                                          (8, 4, lambda j: vS[:, j, CH:CH + T1]),
                                          (12, 3, lambda j: sh[:, 8, :] if j == 0 else g_in[:, j - 1, :])):
                    diff = work if first % 8 == 0 else kk
                    if first >= 8:
                        dve.wait_ge(dve_s.sem, dve_s.value - 4)
                    cur = raw[:, first:first + count, 1:1 + T1]
                    n = dve_s.on(V.tensor_tensor(diff[:, 0:count, :], raw[:, first:first + count, 0:T1], cur, ALU.subtract))
                    dve.wait_ge(dve_s.sem, n)
                    for j in range(count):
                        dve_s.on(V.scalar_tensor_tensor(out=dst(j), in0=diff[:, j, :], scalar=param("mu_rw", first + j),
                                                        in1=raw[:, first + j, 1:1 + T1], op0=ALU.mult, op1=ALU.add))

            @block.scalar
            def _(act):
                act.wait_ge(dve_s.sem, dve_s.value)
                act_s.on(S.activation(sh[0:64, 8, :], sh[0:64, 8, :], ACT.Tanh))
                n = act_s.on(S.activation(g_in, g_in, ACT.Sigmoid))

            @block.tensor
            def _(pe):
                pe.wait_ge(act_s.sem, act_s.value - 1)
                for m in range(CT):
                    pe_s.on(T.matmul(bank[m][:, 0:T1], wa_up[0:64, m * P:m * P + P], sh[0:64, 8, :], start=True, stop=True))
                for m in range(CT):
                    pe_s.on(T.matmul(bank[4 + m][:, 0:T1], wa_up[64:128, m * P:m * P + P], sh[64:128, 8, :], start=True, stop=True))

            @block.scalar
            def _(act):
                for m in range(CT):
                    act.wait_ge(pe_s.sem, pe_s.value - 7 + m)
                    act_s.on(S.activation(ld[:, m, 0:T1], bank[m][:, 0:T1], ACT.Sigmoid, bias=param("w0", m)))
                for m in range(CT):
                    act.wait_ge(pe_s.sem, pe_s.value - 3 + m)
                    act_s.on(S.activation(rate[:, m, :], bank[4 + m][:, 0:T1], ACT.Sigmoid, bias=param("a0", m)))

            @block.vector
            def _(dve):
                dve.wait_ge(dve_s.sem, dve_s.value)
                for j in range(CT):
                    n = dve_s.on(V.tensor_scalar(kk[:, j, :], sh[:, 4 + j, :], param("k_k", j), None, ALU.mult))
                dve.wait_ge(dve_s.sem, n)
                marks["squares"] = dve_s.on(V.tensor_tensor(work, kk, kk, ALU.mult))
                dve.wait_ge(act_s.sem, act_s.value - 4)
                dve_s.on(V.memset(ld[:, :, T1:T1P], 0.0))
                n = dve_s.on(V.tensor_scalar(ld[:, :, 0:T1], ld[:, :, 0:T1], -float(np.exp(-0.5)), None, ALU.mult))
                dve.wait_ge(dve_s.sem, n)
                for j in range(CT):
                    n = dve_s.on(V.tensor_tensor_scan(c_sum[:, j, :], reset64, ld[:, j, :], 0.0, ALU.mult, ALU.add))
                dve.wait_ge(dve_s.sem, n)
                sums = dve_s.on(V.tensor_tensor(ld, c_sum, ld, ALU.subtract))

            @block.tensor
            def _(pe):
                pe.wait_ge(dve_s.sem, marks["squares"])
                pe.wait_ge(act_s.sem, act_s.value - 4)
                for j in range(CT):
                    pe_s.on(T.matmul(bank[j][:, 0:T1], blk64, work[:, j, :], start=True, stop=True))

            @block.scalar
            def _(act):
                act.wait_ge(dve_s.sem, dve_s.value)
                act_s.on(S.activation(e_pos, c_sum, ACT.Exp))
                act_s.on(S.activation(e_neg, c_sum, ACT.Exp, scale=-1.0))
                act_s.on(S.activation(ld, ld, ACT.Exp))

            @block.vector
            def _(dve):
                for j in range(CT):
                    dve.wait_ge(pe_s.sem, pe_s.value - 3 + j)
                    n = dve_s.on(V.tensor_scalar(grow[:, j, :], bank[j][:, 0:T1], 1e-24, None, ALU.max))

            @block.scalar
            def _(act):
                act.wait_ge(dve_s.sem, dve_s.value)
                act_s.on(S.activation(grow, grow, ACT.Sqrt))

            @block.vector
            def _(dve):
                dve.wait_ge(act_s.sem, act_s.value)
                dve.wait_ge(dve_s.sem, dve_s.on(V.reciprocal(grow, grow)))
                dve.wait_ge(dve_s.sem, dve_s.on(V.tensor_tensor(kk, kk, grow, ALU.mult)))
                for j in range(CT):
                    n = dve_s.on(V.tensor_scalar(work[:, j, :], rate[:, j, :], -1.0, param("k_a", j), ALU.add, ALU.mult))
                dve.wait_ge(dve_s.sem, n)
                dve.wait_ge(dve_s.sem, dve_s.on(V.scalar_tensor_tensor(out=work, in0=work, scalar=1.0, in1=sh[:, 4:8, :],
                                                                      op0=ALU.add, op1=ALU.mult)))
                for j in range(CT):
                    dve_s.on(V.scalar_tensor_tensor(out=rk[:, j, :], in0=sh[:, j, :], scalar=param("r_k", j),
                                                    in1=work[:, j, :], op0=ALU.mult, op1=ALU.mult))
                dve.wait_ge(dve_s.sem, dve_s.on(V.tensor_tensor(rate, rate, kk, ALU.mult)))
                tail = T1 - (NCH - 1) * CH
                for dst, i, x, e in ((Q2, 0, kk, ld), (Q2, 1, sh[:, 0:4, :], e_pos), (K2, 0, rate, e_neg), (K2, 1, work, e_neg)):
                    dve_s.on(V.tensor_tensor(dst[:, :, 0:NCH - 1, i, :], chunks(x, NCH - 1), chunks(e, NCH - 1), ALU.mult))
                    dve.wait_ge(pool_s.sem, pool_s.value)
                    dve_s.on(V.tensor_tensor(dst[:, :, NCH - 1, i, 0:tail], x[:, :, T1 - tail:T1], e[:, :, T1 - tail:T1], ALU.mult))

        mi = Memory(mixer, at_K2tok, MIX)
        K2tok = view(after_mixer, NCH * CT, P)
        O = mi.take(NM, P)
        UV = mi.view(mi.at, NCH, C)
        NP = NCH * CT
        L = mi.take(NP, CH)
        Ts = mi.take(NP, CH)
        Xs = mi.take(NP, CH)
        N = mi.view(mi.at - 2 * NP * CH, NM, CH)
        SBD = mi.take(CT, P)
        R = mi.take(C)
        decay_end = mi.take(CT, NCH)
        Tb = mi.view(at_K2, NP, P)
        over_raw = Memory(first_kept, top - 15 * (1 + T1), top)
        LMb = over_raw.take(2, CT, P)
        WWb = over_raw.take(2, CT, P)
        WWs = over_raw.take(2, CT, CH)
        XO = over_raw.take(NP, CH)
        m_of = lambda ch, h: ch * HEADS + h
        inverse = lambda ch, h: (XO if h % 2 else Xs)[0:64, ch * CT + h // 2, :]
        bc = lambda ap, n: ap.unsqueeze(1).broadcast_to([ap.shape[0], n, ap.shape[1]])
        HALF = (slice(0, 64), slice(64, P))
        with nc.Block() as block:
            dve0, pe0, act0 = dve_s.value, pe_s.value, act_s.value

            @block.tensor
            def _(pe):
                for ch in range(NCH):
                    for par in range(2):
                        n = 2 * ch + par
                        if n >= 4:
                            pe.wait_ge(dve_s.sem, dve0 + n - 3 + 1)
                        lo = par * 64
                        for j in range(CT):
                            mm = T.matmul(bank[n % 4][:, j * P:j * P + P],
                                          K2[lo:lo + 64, j, ch, :, :].rearrange("p a b -> p (a b)"),
                                          Q2[lo:lo + 64, j, ch, :, :].rearrange("p a b -> p (a b)"), start=True, stop=True)
                        pe_s.on(mm)
                for ch in range(NCH):
                    if ch >= 2:
                        pe.wait_ge(act_s.sem, act0 + ch - 1)
                    for j in range(CT):
                        t = T.transpose(bank[4 + ch % 2][:, j * P:j * P + P],
                                        K2[:, j, ch, :, :].rearrange("p a b -> p (a b)"), ident)
                    pe_s.on(t)

            @block.vector
            def _(dve):
                dve_s.on(V.tensor_copy(decay_end, e_pos[:, :, CH - 1:T1P:CH]))
                for n in range(2 * NCH):
                    dve.wait_ge(pe_s.sem, pe0 + n + 1)
                    if n == 0:
                        dve.wait_ge(dve_s.sem, dve_s.value)
                    m0 = HEADS * (n // 2)
                    dve_s.on(V.tensor_tensor(O[:, m0 + n % 2:m0 + HEADS:2, :], bank[n % 4][:, :].rearrange("p (a b) -> p a b", b=P),
                                             bc(rw_mask, 4), ALU.mult))

            @block.scalar
            def _(act):
                for ch in range(NCH):
                    act.wait_ge(pe_s.sem, pe0 + 2 * NCH + ch + 1)
                    act_s.on(S.activation(K2tok[:, ch * CT:ch * CT + CT, :],
                                          bank[4 + ch % 2][:, :].rearrange("p (a b) -> p a b", b=P), ACT.Copy))

        four = lambda b: b[:, 0:CT * CH].rearrange("p (a b) -> p a b", b=CH)
        group = lambda g: slice(CT * g, CT * g + CT)
        with nc.Block() as block:
            dve0, pe0, act0 = dve_s.value, pe_s.value, act_s.value

            @block.gpsimd
            def _(pool):
                for ap in (LMb, WWb, Tb):
                    pool_s.on(G.memset(ap, 0.0))

            @block.tensor
            def _(pe):
                for g in range(NCH):
                    pe.wait_ge(act_s.sem, act0 + g + 1)
                    for i in range(CT):
                        m = HEADS * g + 2 * i
                        t = T.transpose(bank[g][:, i * CH:i * CH + CH], N[0:64, m:m + 2, :].rearrange("p a b -> p (a b)"),
                                        ident[0:64, 0:64])
                    pe_s.on(t)

            @block.scalar
            def _(act):
                for g in range(NCH):
                    m = HEADS * g
                    act_s.on(S.activation(N[0:64, m:m + HEADS, :], O[0:64, m:m + HEADS, 0:CH], ACT.Copy))
                for g in range(NCH):
                    act.wait_ge(pe_s.sem, pe0 + g + 1)
                    act_s.on(S.activation(L[:, group(g), :], four(bank[g]), ACT.Copy))

            @block.vector
            def _(dve):
                dve.wait_ge(act_s.sem, act_s.value)
                for half in HALF:
                    n = dve_s.on(V.tensor_tensor(Ts[half], L[half], bc(lower[0][half, half], NP), ALU.mult))
                dve.wait_ge(dve_s.sem, n)
                n = dve_s.on(V.tensor_tensor(Ts, bc(eye2, NP), Ts, ALU.subtract))
                dve.wait_ge(pool_s.sem, pool_s.value)
                dve.wait_ge(dve_s.sem, n)
                dve_s.on(V.tensor_copy(Tb[HALF[1], :, HALF[1]], Ts[HALF[1]]))

            @block.scalar
            def _(act):
                act.wait_ge(pool_s.sem, pool_s.value)
                act.wait_ge(dve_s.sem, dve_s.value - 1)
                act_s.on(S.activation(Tb[HALF[0], :, HALF[0]], Ts[HALF[0]], ACT.Copy))

            @block.tensor
            def _(pe):
                pe.wait_ge(act_s.sem, act_s.value)
                pe.wait_ge(dve_s.sem, dve_s.value)
                for g in range(NCH):
                    for i in range(CT):
                        mm = T.matmul(bank[g][:, i * CH:i * CH + CH], Tb[:, CT * g + i, :], eye2, start=True, stop=True)
                    pe_s.on(mm)

            @block.scalar
            def _(act):
                for g in range(NCH):
                    act.wait_ge(pe_s.sem, pe0 + NCH + g + 1)
                    act_s.on(S.activation(Xs[:, group(g), :], four(bank[g]), ACT.Copy))

        s_lm = Signal(nc, ctx, "pair_level_blocks")
        s_w = Signal(nc, ctx, "pair_product")
        s_wc = Signal(nc, ctx, "pair_product_copied")
        s_xw = Signal(nc, ctx, "pair_corrections")
        s_x = Signal(nc, ctx, "pair_updated")
        s_tb = Signal(nc, ctx, "pair_diagonal")
        todo = [(n, g) for n in range(1, 6) for g in range(NCH)]
        keep_t = lambda i: i < len(todo) - NCH
        copies = [sum(3 if keep_t(k) else 1 for k in range(i + 1)) for i in range(len(todo))]
        updates = [sum(2 if keep_t(k) else 1 for k in range(i + 1)) for i in range(len(todo))]
        with nc.Block() as block:
            @block.vector
            def _(dve):
                def mask(i):
                    n, g = todo[i]
                    if i >= 2:
                        dve.wait_ge(s_w.sem, i - 1)
                    for half in HALF:
                        s_lm.on(V.tensor_tensor(LMb[half, i % 2, :, half], L[half, group(g), :],
                                                bc(lower[n][half, half], CT), ALU.mult))

                def update(i):
                    n, g = todo[i]
                    dve.wait_ge(s_xw.sem, i + 1)
                    s_x.on(V.tensor_tensor(Xs[:, group(g), :], Xs[:, group(g), :], four(bank[2 + i % 2]), ALU.subtract))
                    if keep_t(i):
                        s_x.on(V.tensor_tensor(Ts[:, group(g), :], Ts[:, group(g), :], four(bank[4 + i % 2]), ALU.subtract))
                for i in range(len(todo) + 2):
                    if i < len(todo):
                        mask(i)
                    if i >= 2:
                        update(i - 2)

            @block.gpsimd
            def _(pool):
                for i in range(len(todo) - NCH):
                    pool.wait_ge(s_x.sem, updates[i])
                    for half in HALF:
                        s_tb.on(G.tensor_copy(Tb[half, group(todo[i][1]), half], Ts[half, group(todo[i][1]), :]))

            @block.tensor
            def _(pe):
                def block_product(i):
                    n, g = todo[i]
                    pe.wait_ge(s_lm.sem, 2 * i + 2)
                    if i >= NCH:
                        pe.wait_ge(s_x.sem, updates[i - NCH])
                    if i >= 2:
                        pe.wait_ge(s_wc.sem, copies[i - 2])
                    for q in range(CT):
                        mm = T.matmul(bank[i % 2][:, q * CH:q * CH + CH], LMb[:, i % 2, q, :], Xs[:, CT * g + q, :],
                                      start=True, stop=True)
                    s_w.on(mm)

                def corrections(i):
                    n, g = todo[i]
                    pe.wait_ge(s_wc.sem, copies[i])
                    if i >= NCH:
                        pe.wait_ge(s_tb.sem, 2 * (i - NCH + 1))
                    if i >= 2:
                        pe.wait_ge(s_x.sem, updates[i - 2])
                    for q in range(CT):
                        mm = T.matmul(bank[2 + i % 2][:, q * CH:q * CH + CH], Tb[:, CT * g + q, :], WWs[:, i % 2, q, :],
                                      start=True, stop=True)
                    if keep_t(i):
                        for q in range(CT):
                            mm = T.matmul(bank[4 + i % 2][:, q * CH:q * CH + CH], WWb[:, i % 2, q, :], Ts[:, CT * g + q, :],
                                          start=True, stop=True)
                    s_xw.on(mm)
                for i in range(len(todo) + 1):
                    if i < len(todo):
                        block_product(i)
                    if i >= 1:
                        corrections(i - 1)

            @block.scalar
            def _(act):
                for i in range(len(todo)):
                    act.wait_ge(s_w.sem, i + 1)
                    if i >= 2:
                        act.wait_ge(s_xw.sem, i - 1)
                    s_wc.on(S.activation(WWs[:, i % 2], four(bank[i % 2]), ACT.Copy))
                    if keep_t(i):
                        for half in HALF:
                            s_wc.on(S.activation(WWb[half, i % 2, :, half], four(bank[i % 2])[half], ACT.Copy))

        def triangular_inverse(L, X, Tm, LM, WW, width, per, groups, levels):
            s_lm = Signal(nc, ctx, "level_block" + str(width))
            s_w = Signal(nc, ctx, "block_times_inverse" + str(width))
            s_wc = Signal(nc, ctx, "block_times_inverse_copied" + str(width))
            s_xw = Signal(nc, ctx, "correction" + str(width))
            s_x = Signal(nc, ctx, "inverse_updated" + str(width))
            shaped = lambda b: b[0:width, :].rearrange("p (a b) -> p a b", b=width)
            todo = [(n, g) for n in levels for g in range(groups)]
            keep_t = lambda i: i < len(todo) - groups
            updates = [sum(2 if keep_t(k) else 1 for k in range(i + 1)) for i in range(len(todo))]
            with nc.Block() as block:
                @block.vector
                def _(dve):
                    def mask(i):
                        n, g = todo[i]
                        if i >= 2:
                            dve.wait_ge(s_w.sem, i - 1)
                        s_lm.on(V.tensor_tensor(LM[0:width, i % 2], L[0:width, per * g:per * g + per, :],
                                                bc(lower[n][0:width, 0:width], per), ALU.mult))

                    def update(i):
                        n, g = todo[i]
                        s = slice(per * g, per * g + per)
                        dve.wait_ge(s_xw.sem, i + 1)
                        s_x.on(V.tensor_tensor(X[:, s, :], X[:, s, :], shaped(bank[2 + i % 2]), ALU.subtract))
                        if keep_t(i):
                            s_x.on(V.tensor_tensor(Tm[:, s, :], Tm[:, s, :], shaped(bank[4 + i % 2]), ALU.subtract))
                    for i in range(len(todo) + 2):
                        if i < len(todo):
                            mask(i)
                        if i >= 2:
                            update(i - 2)

                @block.tensor
                def _(pe):
                    def block_product(i):
                        n, g = todo[i]
                        pe.wait_ge(s_lm.sem, i + 1)
                        if i >= groups:
                            pe.wait_ge(s_x.sem, updates[i - groups])
                        if i >= 2:
                            pe.wait_ge(s_wc.sem, i - 1)
                        for q in range(per):
                            mm = T.matmul(bank[i % 2][0:width, q * width:q * width + width], LM[0:width, i % 2, q, :],
                                          X[:, per * g + q, :], start=True, stop=True)
                        s_w.on(mm)

                    def corrections(i):
                        n, g = todo[i]
                        pe.wait_ge(s_wc.sem, i + 1)
                        if i >= 2:
                            pe.wait_ge(s_x.sem, updates[i - 2])
                        for q in range(per):
                            mm = T.matmul(bank[2 + i % 2][0:width, q * width:q * width + width], Tm[:, per * g + q, :],
                                     WW[0:width, i % 2, q, :], start=True, stop=True)
                        if keep_t(i):
                            for q in range(per):
                                mm = T.matmul(bank[4 + i % 2][0:width, q * width:q * width + width], WW[0:width, i % 2, q, :],
                                              Tm[:, per * g + q, :], start=True, stop=True)
                        s_xw.on(mm)
                    for i in range(len(todo) + 1):
                        if i < len(todo):
                            block_product(i)
                        if i >= 1:
                            corrections(i - 1)

                @block.scalar
                def _(act):
                    for i in range(len(todo)):
                        act.wait_ge(s_w.sem, i + 1)
                        if i >= 2:
                            act.wait_ge(s_xw.sem, i - 1)
                        s_wc.on(S.activation(WW[0:width, i % 2], shaped(bank[i % 2]), ACT.Copy))

        s_odd = Signal(nc, ctx, "odd_inverses")
        with nc.Block() as block:
            dve0, pe0 = dve_s.value, pe_s.value

            @block.tensor
            def _(pe):
                for ch in range(NCH):
                    if ch >= 4:
                        pe.wait_ge(dve_s.sem, dve0 + 2 + ch - 3)
                    for j in range(CT):
                        t = T.transpose(bank[ch % 4][:, j * P:j * P + P], vS[:, j, CH * ch:CH * ch + P], ident)
                    pe_s.on(t)
                for i in range(0, NP, 8):
                    n = min(8, NP - i)
                    s_odd.on(T.matmul(bank[4 + i // 8][0:64, 0:n * CH], ident[:, HALF[1]],
                                      Xs[:, i:i + n, :].rearrange("p a b -> p (a b)"), start=True, stop=True))

            @block.scalar
            def _(act):
                for i in range(0, NP, 8):
                    n = min(8, NP - i)
                    act.wait_ge(s_odd.sem, i // 8 + 1)
                    act_s.on(S.activation(XO[0:64, i:i + n, :].rearrange("p a b -> p (a b)"), bank[4 + i // 8][0:64, 0:n * CH], ACT.Copy))

            @block.vector
            def _(dve):
                dve_s.on(V.memset(UV[0:64, :, :], 0.0))
                dve_s.on(V.memset(SBD, 0.0))
                for ch in range(NCH):
                    dve.wait_ge(pe_s.sem, pe0 + ch + 1)
                    dve_s.on(V.tensor_copy(UV[64:128, ch, :], bank[ch % 4][64:128, :]))

        s_r = Signal(nc, ctx, "rhs_ready")
        s_rc = Signal(nc, ctx, "rhs_copied")
        s_u = Signal(nc, ctx, "u_ready")
        s_uc = Signal(nc, ctx, "u_copied")
        s_ry = Signal(nc, ctx, "chunk_out")
        s_ryc = Signal(nc, ctx, "chunk_out_copied")
        s_st = Signal(nc, ctx, "state_change")
        s_state = Signal(nc, ctx, "state_ready")
        with nc.Block() as block:
            @block.tensor
            def _(pe):
                for ch in range(NCH):
                    if ch:
                        pe.wait_ge(s_state.sem, 4 * ch)
                    for j in range(CT):
                        T.matmul(bank[0][0:64, j * P:j * P + P], Q2[:, j, ch, 0, :], SBD[:, j, :], start=True, stop=False,
                                 skip_group_check=True)
                        for h in (2 * j, 2 * j + 1):
                            mm = T.matmul(bank[0][0:64, h * DH:h * DH + DH], O[:, m_of(ch, h), 0:CH],
                                          UV[:, ch, h * DH:h * DH + DH], start=False, stop=True, skip_group_check=True)
                    s_r.on(mm)
                    pe.wait_ge(s_rc.sem, ch + 1)
                    for h in range(HEADS):
                        mm = T.matmul(bank[1][0:64, h * DH:h * DH + DH], inverse(ch, h), R[0:64, h * DH:h * DH + DH],
                                      start=True, stop=True)
                    s_u.on(mm)
                    pe.wait_ge(s_uc.sem, ch + 1)
                    if ch < NCH - 1:
                        for h in range(HEADS):
                            lo = DH * (h % 2)
                            mm = T.matmul(bank[4][lo:lo + DH, (h // 2) * P + lo:(h // 2) * P + lo + DH],
                                          K2tok[:, ch * CT + h // 2, lo:lo + DH], UV[:, ch, h * DH:h * DH + DH],
                                          start=True, stop=True)
                        s_st.on(mm)
                    if ch >= 2:
                        pe.wait_ge(s_ryc.sem, ch - 1)
                    for j in range(CT):
                        T.matmul(bank[2 + ch % 2][:, j * CH:j * CH + CH], SBD[:, j, :], Q2[:, j, ch, 1, :], start=True,
                                 stop=False, skip_group_check=True)
                        for h in (2 * j, 2 * j + 1):
                            lo = DH * (h % 2)
                            mm = T.matmul(bank[2 + ch % 2][lo:lo + DH, j * CH:j * CH + CH], UV[:, ch, h * DH:h * DH + DH],
                                          O[:, m_of(ch, h), CH:P], start=False, stop=True, skip_group_check=True)
                    s_ry.on(mm)

            @block.scalar
            def _(act):
                for ch in range(NCH):
                    act.wait_ge(s_r.sem, ch + 1)
                    if ch:
                        act.wait_ge(s_u.sem, ch)
                    s_rc.on(S.activation(R[0:64], bank[0][0:64, :], ACT.Copy))
                    act.wait_ge(s_u.sem, ch + 1)
                    s_uc.on(S.activation(UV[0:64, ch, :], bank[1][0:64, :], ACT.Copy, scale=-1.0))

            @block.vector
            def _(dve):
                for ch in range(NCH):
                    if ch < NCH - 1:
                        dve.wait_ge(s_st.sem, ch + 1)
                        dve.wait_ge(s_ry.sem, ch + 1)
                        for lo in (0, DH):
                            s = SBD[lo:lo + DH, :, lo:lo + DH]
                            s_state.on(V.tensor_tensor(s, s, bank[4][lo:lo + DH, :].rearrange("p (a b) -> p a b", b=P)[:, :, lo:lo + DH], ALU.add))
                        dve.wait_ge(s_state.sem, 4 * ch + 2)
                        for lo in (0, DH):
                            s = SBD[lo:lo + DH, :, lo:lo + DH]
                            s_state.on(V.tensor_tensor(s, s, decay_end[lo:lo + DH, :, ch:ch + 1].broadcast_to([DH, CT, DH]), ALU.mult))
                    dve.wait_ge(s_ry.sem, ch + 1)
                    n = min(CH, T1 - ch * CH)
                    s_ryc.on(V.tensor_copy(y_rw[:, :, ch * CH:ch * CH + n],
                                           bank[2 + ch % 2][:, 0:CT * CH].rearrange("p (a b) -> p a b", b=CH)[:, :, 0:n]))

        mg = Memory(mixer, at_K2, MIX)
        dev, sq, gnr = mg.take(CT, T1), mg.take(CT, T1), mg.take(CT, T1)
        with nc.Block() as block:
            pe0 = pe_s.value

            @block.tensor
            def _(pe):
                for j in range(CT):
                    pe_s.on(T.matmul(bank[j][:, 0:T1], blk64, y_rw[:, j, :], start=True, stop=True))
                for j in range(CT):
                    pe_s.on(T.matmul(bank[4 + j][:, 0:T1], blk64, rk[:, j, :], start=True, stop=True))

            @block.vector
            def _(dve):
                for j in range(CT):
                    dve.wait_ge(pe_s.sem, pe0 + j + 1)
                    n = dve_s.on(V.scalar_tensor_tensor(out=dev[:, j, :], in0=bank[j][:, 0:T1], scalar=-1.0 / DH,
                                                        in1=y_rw[:, j, :], op0=ALU.mult, op1=ALU.add))
                dve.wait_ge(dve_s.sem, n)
                dve_s.on(V.tensor_tensor(sq, dev, dev, ALU.mult))
                for j in range(CT):
                    dve.wait_ge(pe_s.sem, pe0 + 4 + j + 1)
                    dve_s.on(V.tensor_tensor(rk[:, j, :], bank[4 + j][:, 0:T1], vS[:, j, CH:CH + T1], ALU.mult))

            @block.tensor
            def _(pe):
                pe.wait_ge(dve_s.sem, dve_s.value - 4)
                for j in range(CT):
                    pe_s.on(T.matmul(bank[j][:, 0:T1], blk64, sq[:, j, :], start=True, stop=True))
                pe.wait_ge(dve_s.sem, dve_s.value)
                for j in range(CT):
                    T.matmul(bank[4 + j][:, 0:T1], g_up0[:, j * P:j * P + P], g_in[:, 0, :], start=True, stop=False)
                    pe_s.on(T.matmul(bank[4 + j][:, 0:T1], g_up1[0:32, j * P:j * P + P], g_in[0:32, 1, :], start=False, stop=True))

            @block.scalar
            def _(act):
                for j in range(CT):
                    act.wait_ge(pe_s.sem, pe0 + 8 + j + 1)
                    act_s.on(S.activation(gnr[:, j, :], bank[j][:, 0:T1], ACT.Sqrt, bias=eps_gn, scale=1.0 / DH))

            @block.vector
            def _(dve):
                dve.wait_ge(act_s.sem, act_s.value)
                dve.wait_ge(dve_s.sem, dve_s.on(V.reciprocal(gnr, gnr)))
                dve.wait_ge(dve_s.sem, dve_s.on(V.tensor_tensor(dev, dev, gnr, ALU.mult)))
                for j in range(CT):
                    n = dve_s.on(V.tensor_scalar(dev[:, j, :], dev[:, j, :], param("ln_x_w", j), param("ln_x_b", j), ALU.mult, ALU.add))
                dve.wait_ge(dve_s.sem, n)
                dve.wait_ge(dve_s.sem, dve_s.on(V.tensor_tensor(dev, dev, rk, ALU.add)))
                for j in range(CT):
                    dve.wait_ge(pe_s.sem, pe0 + 12 + j + 1)
                    dve_s.on(V.tensor_tensor(y_rw[:, j, :], dev[:, j, :], bank[4 + j][:, 0:T1], ALU.mult))
        mixer_stack.close()
        over_qkv = Memory(first_kept, after_mixer, FIRST)
        gates = over_qkv.take(2 * KD, T1)
        part = over_qkv.take(KD, T1)
        merged = over_qkv.take(KD, T1)
        s_mix = Signal(nc, ctx, "branch_b_gated")
        merge_stack = ExitStack()
        parts = split_memory(merge_stack, "merge_", 2 * KD, T1)
        gates0, parts0 = act_s.value, dve_s.value

        def merge(engine, m, psum):
            if m < 2 * KD:
                return S.activation(gates[:, m, :], psum, ACT.Sigmoid)
            j = m % KD
            if m < 3 * KD:
                engine.wait_ge(act_s.sem, gates0 + j + 1)
                return V.tensor_tensor(part[:, j, :], psum, gates[:, j, :], ALU.mult)
            engine.wait_ge(act_s.sem, gates0 + KD + j + 1)
            engine.wait_ge(s_mix.sem, s_mix.on(V.tensor_tensor(merged[:, j, :], psum, gates[:, KD + j, :], ALU.mult)))
            engine.wait_ge(dve_s.sem, parts0 + j + 1)
            return V.tensor_tensor(merged[:, j, :], merged[:, j, :], part[:, j, :], ALU.add)
        project([xnT, y_sb, y_rw], T1,
                [(7 + m // 4, (m % 4) * P, P, 0) for m in range(2 * KD)]
                + [(SB_OUT + i, m * P, P, 1 + i) for i in range(2) for m in range(KD)],
                merge, 7, 6, parts, owner=lambda m: "act" if m < 2 * KD else "dve")

        def add_to_stream(engine, m, psum):
            return V.tensor_tensor(hT[:, m, :], hT[:, m, :], psum, ALU.add)
        project([merged], T1, [(W_OUT + m // 4, (m % 4) * P, P, 0) for m in range(KD)], add_to_stream, W_OUT, 2, parts,
                owner=lambda m: "dve")
        merge_stack.close()

        arena.close()
        arena = ExitStack()
        take = lambda name, shape, dt: arena.enter_context(nc.sbuf_tensor(name, shape, dt))
        MODC = 512
        fmem = Memory(take("ffn_memory", [P, 4 * T1 + 2 * MODC], F32), 0, 4 * T1 + 2 * MODC)
        fsig = fmem.take(2, T1)
        fprod = fmem.take(2, T1)
        ada = fmem.take(2, MODC)
        ffn_hi, ffn_lo = take("ffn_hidden_hi", [P, FT, T1], F32R), take("ffn_hidden_lo", [P, FT, T1], F32R)
        fx_hi, fx_lo = take("ffn_x_hi", [P, KD, T1], F32R), take("ffn_x_lo", [P, KD, T1], F32R)
        norm_stack = ExitStack()
        nmem = norm_stack.enter_context(nc.sbuf_tensor("ffn_norm", [P, 2, KD, T1], F32))
        hnT, fsq = nmem[:, 0], nmem[:, 1]
        rms_norm(hT, hnT, lambda j: param("norm_ffn", j), None, T1, fsq, fsig[:, 0, :])
        with nc.Block() as block:
            @block.scalar
            def _(act):
                act_s.on(S.activation(fx_hi[:, :, :], hnT, ACT.Copy))
                c0 = ROWS0["c_2"][0]
                act_s.on(S.activation(csil[:, :, 0], vec0[:, c0:c0 + KD], ACT.Sigmoid))

            @block.vector
            def _(dve):
                dve.wait_ge(act_s.sem, act_s.value - 1)
                dve_s.on(V.tensor_tensor(fx_lo[:, :, :], hnT, fx_hi[:, :, :].bitcast(F32), ALU.subtract))
                dve.wait_ge(act_s.sem, act_s.value)
                dve_s.on(V.tensor_tensor(csil[:, :, 0], csil[:, :, 0], vec0[:, ROWS0["c_2"][0]:ROWS0["c_2"][0] + KD], ALU.mult))
        norm_stack.close()
        f_hi = [take(f"ffn_weights_hi{i}", [P, PIECE], F32R) for i in range(CUT)]
        f_lo = [take(f"ffn_weights_lo{i}", [P, PIECE], F32R) for i in range(CUT)]
        n_in, n_out = FT, FT // 2
        s_cut = Signal(nc, ctx, "piece_hi_ready")
        s_rest = Signal(nc, ctx, "piece_lo_ready")
        s_used = Signal(nc, ctx, "piece_used")
        s_sig = Signal(nc, ctx, "gate_sigmoid")
        s_hid = Signal(nc, ctx, "hidden_ready")
        s_fhi = Signal(nc, ctx, "ffn_hidden_hi")
        s_flo = Signal(nc, ctx, "ffn_hidden_lo")
        s_ada = Signal(nc, ctx, "modulation_steps")
        ada_ready = [Signal(nc, ctx, f"modulation_slot{i}") for i in range(2)]
        ada_w = take("modulation_weights", [P, 2, 2, MODC], F32)
        s_ada_sum = Signal(nc, ctx, "modulation_block_summed")
        N_ADA = 48

        sum_bank = []

        def steps_by(m):
            return 4 * (m + 1)

        def piece(r):
            if r < n_in:
                n = FFN_IN + r // 2
                return n, slot(n).rearrange("p k (u c) -> p k u c", u=2)[:, :, :, (r % 2) * P:(r % 2) * P + P]
            r -= n_in
            n = FFN_OUT + r // 2
            return n, slot(n)[:, (r % 2) * 2:(r % 2) * 2 + 2, :]

        def as_piece(ap, r):
            return (ap[:, :].rearrange("p (k u c) -> p k u c", k=KD, u=2) if r < n_in
                    else ap[:, :].rearrange("p (k c) -> p k c", k=2))

        for r in range(n_in + n_out):
            slot_freed[piece(r)[0]] = s_rest, r + 1
        with nc.Block() as block:
            @block.sync
            def _(sp):
                load_slots(sp, W_IN2 + RING)

            @block.gpsimd
            def _(pool):
                w = a["w_ada_2"][0]
                for n in range(N_ADA):
                    if n >= 2:
                        pool.wait_ge(s_ada.sem, 2 * (n - 1))
                    cb, kg = n // 4, n % 4
                    src = w[2 * kg * P:(2 * kg + 2) * P, cb * MODC:(cb + 1) * MODC].rearrange("(k p) c -> p k c", p=P)
                    ada_ready[n % 2].on(pool.dma_start(ada_w[:, n % 2], src), 16)

            @block.tensor
            def _(pe):
                summed = [0]

                def sum_partitions(steps, b):
                    while 8 * (summed[0] + 1) <= steps:
                        cb = summed[0]
                        pe.wait_ge(s_ada.sem, 8 * (cb + 1))
                        for m in range(MODC // P):
                            at = 320 + cb * MODC // P + m
                            mm = T.matmul(bank[b][:, at:at + 1], ada[:, cb % 2, m * P:m * P + P],
                                          one_col, start=True, stop=True)
                        s_ada_sum.on(mm)
                        sum_bank.append(b)
                        summed[0] += 1
                for m in range(n_in):
                    pe.wait_ge(s_rest.sem, m + 1)
                    if m >= 4:
                        pe.wait_ge(s_hid.sem, 2 * (m - 3))
                    sum_partitions(steps_by(m - 3), 2 * (m % 4))
                    hi, lo = as_piece(f_hi[m % CUT], m), as_piece(f_lo[m % CUT], m)
                    for up in range(2):
                        for k in range(KD):
                            for w, x in ((hi, fx_hi), (hi, fx_lo), (lo, fx_hi)):
                                mm = T.matmul(bank[2 * (m % 4) + up][:, 0:T1], w[:, k, up, :], x[:, k, :],
                                              start=(k == 0 and w is hi and x is fx_hi), stop=(k == KD - 1 and w is lo))
                    s_used.on(mm)
                pe.wait_ge(s_hid.sem, 2 * n_in)
                sum_partitions(steps_by(n_in - 1), 7)
                for r in range(n_in, n_in + n_out):
                    pe.wait_ge(s_rest.sem, r + 1)
                    hi, lo = as_piece(f_hi[r % CUT], r), as_piece(f_lo[r % CUT], r)
                    for i in range(2):
                        k = 2 * (r - n_in) + i
                        pe.wait_ge(s_flo.sem, k + 1)
                        for m in range(KD):
                            for w, x in ((hi, ffn_hi), (hi, ffn_lo), (lo, ffn_hi)):
                                mm = T.matmul(bank[m][:, 0:T1], w[:, i, m * P:m * P + P], x[:, k, :],
                                              start=(k == 0 and w is hi and x is ffn_hi), stop=(k == FT - 1 and w is lo))
                    s_used.on(mm)
                sum_partitions(2 * N_ADA, 7)

            @block.scalar
            def _(act):
                def cut(r):
                    n, src = piece(r)
                    await_slot(act, n)
                    if r >= CUT:
                        act.wait_ge(s_used.sem, r - CUT + 1)
                    s_cut.on(S.activation(as_piece(f_hi[r % CUT], r), src, ACT.Copy))
                for r in range(CUT):
                    cut(r)
                for m in range(n_in):
                    act.wait_ge(s_used.sem, m + 1)
                    if m >= 2:
                        act.wait_ge(s_hid.sem, 2 * (m - 1))
                    s_sig.on(S.activation(fsig[:, m % 2, :], bank[2 * (m % 4)][:, 0:T1], ACT.Sigmoid))
                    cut(m + CUT)
                    act.wait_ge(s_hid.sem, 2 * m + 2)
                    s_fhi.on(S.activation(ffn_hi[:, m, :], fprod[:, m % 2, :], ACT.Copy))
                for r in range(n_in + CUT, n_in + n_out):
                    cut(r)

            @block.vector
            def _(dve):
                ada_at = [0]

                def rest_of(r):
                    n, src = piece(r)
                    dve.wait_ge(s_cut.sem, r + 1)
                    s_rest.on(V.tensor_tensor(as_piece(f_lo[r % CUT], r), src, as_piece(f_hi[r % CUT], r).bitcast(F32), ALU.subtract))

                def modulation(upto):
                    while ada_at[0] < min(upto, 2 * N_ADA):
                        step = ada_at[0]
                        n, half = step // 2, step % 2
                        cb, k = n // 4, 2 * (n % 4) + half
                        if half == 0:
                            dve.wait_ge(ada_ready[n % 2].sem, 16 * (n // 2 + 1))
                        if k == 0 and cb >= 2:
                            dve.wait_ge(s_ada_sum.sem, cb - 1)
                        if step:
                            dve.wait_ge(s_ada.sem, step)
                        dst, src = ada[:, cb % 2, :], ada_w[:, n % 2, half, :]
                        if k == 0:
                            s_ada.on(V.tensor_scalar(dst, src, csil[:, 0, :], None, ALU.mult))
                        else:
                            s_ada.on(V.scalar_tensor_tensor(out=dst, in0=src, scalar=csil[:, k, :], in1=dst, op0=ALU.mult, op1=ALU.add))
                        ada_at[0] += 1
                for r in range(CUT):
                    rest_of(r)
                for m in range(n_in):
                    b = 2 * (m % 4)
                    dve.wait_ge(s_sig.sem, m + 1)
                    if m >= 2:
                        dve.wait_ge(s_flo.sem, m - 1)
                    s_hid.on(V.tensor_tensor(fprod[:, m % 2, :], bank[b][:, 0:T1], fsig[:, m % 2, :], ALU.mult))
                    dve.wait_ge(s_hid.sem, 2 * m + 1)
                    s_hid.on(V.tensor_tensor(fprod[:, m % 2, :], fprod[:, m % 2, :], bank[b + 1][:, 0:T1], ALU.mult))
                    rest_of(m + CUT)
                    dve.wait_ge(s_fhi.sem, m + 1)
                    s_flo.on(V.tensor_tensor(ffn_lo[:, m, :], fprod[:, m % 2, :], ffn_hi[:, m, :].bitcast(F32), ALU.subtract))
                    modulation(steps_by(m))
                for r in range(n_in + CUT, n_in + n_out):
                    rest_of(r)
                    modulation(steps_by(n_in - 1) + 2 * (r - n_in - CUT + 1))
                modulation(2 * N_ADA)
                dve.wait_ge(s_ada_sum.sem, 12)
                for m in range(KD):
                    dve_s.on(V.tensor_tensor(hT[:, m, :], hT[:, m, :], bank[m][:, 0:T1], ALU.add))
                c0 = ROWS1["b_ada_2"][0]
                for cb in range(6 * D // MODC):
                    lo, n = cb * MODC // P, MODC // P
                    dve_s.on(V.tensor_tensor(mod[:, lo:lo + n], bank[sum_bank[cb]][:, 320 + lo:320 + lo + n],
                                             vec1[:, c0 + lo:c0 + lo + n], ALU.add))

        arena.close()
        arena = ExitStack()
        LOW = KD * T2 + 12 * (3 + T2) + 5 * GH * T2
        SECOND = LOW + KD * T2
        second_kept = arena.enter_context(nc.sbuf_tensor("mixer2_kept", [P, SECOND], F32))
        view = Memory(second_kept, 0, SECOND).view
        xT = Memory(kept, CONSTS, CONSTS + KD * T1).take(KD, T2)
        x_new = view(2 * KD * T2, KD, T2)
        rms_norm(hT[:, :, N_META:T1], x_new, lambda j: param("norm_final", j), None, T2, view(0, KD, T2), view(KD * T2, T2))
        with nc.Block() as block:
            @block.scalar
            def _(act):
                act_s.on(S.activation(xT, x_new, ACT.Copy))

            @block.vector
            def _(dve):
                for gain_, name, sc in ((gain1, "norm1_w_2", 1), (gain2, "norm2_w_2", 4)):
                    c0 = ROWS0[name][0]
                    dve_s.on(V.scalar_tensor_tensor(out=gain_, in0=mod[:, sc * KD:sc * KD + KD], scalar=1.0,
                                                    in1=vec0[:, c0:c0 + KD], op0=ALU.add, op1=ALU.mult))
                r0 = ROWS0["hg_lb_2"][0]
                a0_, a1_ = vec0[:, r0:r0 + GH], vec0[:, r0 + GH:r0 + 2 * GH]
                n = dve_s.on(V.tensor_tensor(lb, a0_, a1_, ALU.max))
                dve.wait_ge(dve_s.sem, n)
                dve_s.on(V.tensor_tensor(e_hg[:, 0:GH], a0_, lb, ALU.subtract))
                dve_s.on(V.tensor_tensor(e_hg[:, GH:2 * GH], a1_, lb, ALU.subtract))

            @block.scalar
            def _(act):
                act.wait_ge(dve_s.sem, dve_s.value)
                act_s.on(S.activation(e_hg, e_hg, ACT.Exp))

            @block.vector
            def _(dve):
                dve.wait_ge(act_s.sem, act_s.value)
                dve.wait_ge(dve_s.sem, dve_s.on(V.tensor_tensor(lb1, e_hg[:, 0:GH], e_hg[:, GH:2 * GH], ALU.add)))
                dve.wait_ge(dve_s.sem, dve_s.on(V.reciprocal(lb1, lb1)))
                dve_s.on(V.tensor_tensor(lb, e_hg[:, 0:GH], lb1, ALU.mult))
                dve.wait_ge(dve_s.sem, dve_s.value)
                dve_s.on(V.tensor_scalar(lb1, lb, -1.0, 1.0, ALU.mult, ALU.add))
        low = Memory(second_kept, 0, LOW)
        hm = low.take(KD, T2)
        raw2 = low.take(12, 3 + T2)
        proj_b = low.take(5, GH, T2)
        gate_a, f_b, i_b, q_b, gate_b = (proj_b[:, i] for i in range(5))
        o_all = view(LOW, KD, T2)
        ba = small[:, 0:64].rearrange("p (k c) -> p k c", c=8)
        alog, dtb = small[0:GH, 64:65], small[0:GH, 65:66]
        rms_norm(xT, hm, lambda j: gain1[:, j:j + 1], lambda j: mod[:, j:j + 1], T2, view(KD * T2, KD, T2), view(2 * KD * T2, T2))
        with nc.Block() as block:
            @block.gpsimd
            def _(pool):
                pool_s.on(G.memset(raw2[:, :, 0:3], 0.0))

        def put_in2(engine, m, psum):
            dst = raw2[:, m, 3:3 + T2] if m < 12 else proj_b[:, (m - 12) // 4, m % 4, :]
            if engine is nc.scalar:
                return S.activation(dst, psum, ACT.Copy)
            return V.tensor_copy(dst, psum)
        with ExitStack() as stack:
            project([hm], T2, [(W_IN2 + m // 4, (m % 4) * P, P, 0) for m in range(32)], put_in2, W_IN2, 8,
                    split_memory(stack, "in2_", KD, T2))
        MIX2 = total - SECOND - 16
        mixer_stack = ExitStack()
        m2 = Memory(mixer_stack.enter_context(nc.sbuf_tensor("mixer2_memory", [P, MIX2], F32)), 0, MIX2)
        qkv = m2.take(12, T2)
        gcB = m2.take(GH, T2)
        beB = m2.take(GH, T2)
        Dm = m2.take(2 * GH, P)
        GG = m2.take(2 * GH, 2 * P)
        L2 = m2.take(2 * GH, P)
        Tm2 = m2.take(2 * GH, P)
        LM2 = m2.take(2, 4, P)
        WW2 = m2.take(2, 4, P)
        rows_b, rows_g = m2.take(T2), m2.take(T2)
        cols = m2.take(4, GH)
        tail_f = m2.take(GH)
        ealog = m2.take(1)

        with nc.Block() as block:
            @block.tensor
            def _(pe):
                for i in range(2):
                    for k in range(KD):
                        mm = T.matmul(bank[i][0:GH, 0:T2], ba[:, k, GH * i:GH * i + GH], hm[:, k, :],
                                      start=(k == 0), stop=(k == KD - 1))
                    pe_s.on(mm)

            @block.scalar
            def _(act):
                act.wait_ge(pe_s.sem, pe_s.value - 1)
                act_s.on(S.activation(rows_b[0:GH, :], bank[0][0:GH, 0:T2], ACT.Sigmoid))
                act.wait_ge(pe_s.sem, pe_s.value)
                act_s.on(S.activation(ealog[0:GH, :], alog, ACT.Exp))
                marks["abs"] = act_s.on(S.activation(rows_g[0:GH, :], bank[1][0:GH, 0:T2], ACT.Abs, bias=dtb))
                act.wait_ge(act_s.sem, act_s.value)
                act.wait_ge(act_s.sem, act_s.on(S.activation(rows_g[0:GH, :], rows_g[0:GH, :], ACT.Exp, scale=-1.0)))
                act_s.on(S.activation(rows_g[0:GH, :], rows_g[0:GH, :], ACT.Ln, bias=one_col[0:GH, :]))

            @block.vector
            def _(dve):
                for j in (3, 2, 1, 0):
                    for m in range(12):
                        w = param("conv_w_2", 12 * j + m)
                        if j == 3:
                            dve_s.on(V.tensor_scalar(qkv[:, m, :], raw2[:, m, 3:3 + T2], w, None, ALU.mult))
                        else:
                            dve.wait_ge(dve_s.sem, dve_s.value - 11)
                            dve_s.on(V.scalar_tensor_tensor(out=qkv[:, m, :], in0=raw2[:, m, j:j + T2], scalar=w,
                                                            in1=qkv[:, m, :], op0=ALU.mult, op1=ALU.add))
                marks["conv"] = dve_s.value

            @block.scalar
            def _(act):
                act.wait_ge(dve_s.sem, dve_s.value)
                marks["log_term"] = act_s.value
                marks["sig"] = act_s.on(S.activation(raw2[:, :, 0:T2], qkv, ACT.Sigmoid))

            @block.vector
            def _(dve):
                dve.wait_ge(act_s.sem, marks["log_term"])
                t = gcB[0:GH, 0, :]
                dve.wait_ge(dve_s.sem, dve_s.on(V.tensor_scalar(t, bank[1][0:GH, 0:T2], dtb, 0.0, ALU.add, ALU.max)))
                dve.wait_ge(dve_s.sem, dve_s.on(V.tensor_tensor(rows_g[0:GH, :], rows_g[0:GH, :], t, ALU.add)))
                dve.wait_ge(dve_s.sem, dve_s.on(V.tensor_scalar(t, rows_g[0:GH, :], ealog[0:GH, :], -1.0, ALU.mult, ALU.mult)))
                marks["rows"] = dve_s.on(V.tensor_tensor_scan(rows_g[0:GH, :], reset128[0:GH, :], t, 0.0, ALU.mult, ALU.add))
                dve.wait_ge(act_s.sem, marks["sig"])
                dve.wait_ge(dve_s.sem, dve_s.on(V.tensor_tensor(qkv, qkv, raw2[:, :, 0:T2], ALU.mult)))
                dve_s.on(V.tensor_tensor(raw2[:, 0:8, 0:T2], qkv[:, 0:8, :], qkv[:, 0:8, :], ALU.mult))

            @block.tensor
            def _(pe):
                pe.wait_ge(dve_s.sem, dve_s.value)
                for m in range(8):
                    mm = T.matmul(bank[2 + m // 2][:, (m % 2) * T2:(m % 2) * T2 + T2], ones, raw2[:, m, 0:T2], start=True, stop=True)
                    if m % 2:
                        pe_s.on(mm)
                for i, rows in enumerate((rows_g, rows_b)):
                    for h in range(GH):
                        b = (6, 7, 0, 1)[2 * i + h // 2]
                        mm = T.matmul(bank[b][:, (h % 2) * T2:(h % 2) * T2 + T2], row_sel[0:GH, h, :], rows[0:GH, :],
                                      start=True, stop=True)
                    pe_s.on(mm)

            @block.scalar
            def _(act):
                for b in range(4):
                    act.wait_ge(pe_s.sem, pe_s.value - 5 + b)
                    act_s.on(S.activation(raw2[:, 2 * b:2 * b + 2, 0:T2], bank[2 + b][:, :].rearrange("p (a b) -> p a b", b=T2),
                                          ACT.Sqrt, bias=eps_rms))

            @block.vector
            def _(dve):
                dve.wait_ge(pe_s.sem, pe_s.value)
                for i, dst in enumerate((gcB, beB)):
                    for q in range(2):
                        dve_s.on(V.tensor_copy(dst[:, 2 * q:2 * q + 2, :], bank[(6, 7, 0, 1)[2 * i + q]][:, :].rearrange("p (a b) -> p a b", b=T2)))
                dve.wait_ge(act_s.sem, act_s.value)
                dve.wait_ge(dve_s.sem, dve_s.on(V.reciprocal(raw2[:, 0:8, 0:T2], raw2[:, 0:8, 0:T2])))
                dve_s.on(V.scalar_tensor_tensor(out=qkv[:, 0:4, :], in0=qkv[:, 0:4, :], scalar=P ** -0.5,
                                                in1=raw2[:, 0:4, 0:T2], op0=ALU.mult, op1=ALU.mult))
                dve_s.on(V.tensor_tensor(qkv[:, 4:8, :], qkv[:, 4:8, :], raw2[:, 4:8, 0:T2], ALU.mult))

            @block.tensor
            def _(pe):
                pe.wait_ge(act_s.sem, act_s.value)
                for i, rows in enumerate((rows_g, rows_b)):
                    for c in range(2):
                        t = T.transpose(bank[2][:, (2 * i + c) * GH:(2 * i + c) * GH + GH], rows[0:GH, c * P:c * P + P],
                                        ident[0:GH, 0:GH])
                pe_s.on(t)

            @block.vector
            def _(dve):
                dve.wait_ge(pe_s.sem, pe_s.value)
                dve_s.on(V.tensor_copy(cols, bank[2][:, 0:4 * GH].rearrange("p (a b) -> p a b", b=GH)))

        lowa = Memory(second_kept, 0, KD * T2 + 12 * (3 + T2))
        kg, qg, ktok, vtok, eg = (lowa.take(2 * GH, P) for _ in range(5))
        q2, k2, v2 = qkv[:, 0:4, :], qkv[:, 4:8, :], qkv[:, 8:12, :]
        mats = lambda ap: ap.rearrange("p h (c t) -> p (h c) t", c=2)
        pair = lambda b: b[:, :].rearrange("p (a b) -> p a b", b=P)
        X2 = GG[:, :, 0:P]
        AT = GG[:, :, P:2 * P]
        with nc.Block() as block:
            pe0, act0, dve0 = pe_s.value, act_s.value, dve_s.value

            @block.tensor
            def _(pe):
                for h in range(GH):
                    for c in range(2):
                        s = slice(c * P, c * P + P)
                        T.matmul(bank[h][:, c * 2 * P:c * 2 * P + P], k2[:, h, s], k2[:, h, s], start=True, stop=True)
                        mm = T.matmul(bank[h][:, c * 2 * P + P:c * 2 * P + 2 * P], k2[:, h, s], q2[:, h, s], start=True, stop=True)
                    pe_s.on(mm)
                for h in range(GH):
                    for c in range(2):
                        t = T.transpose(bank[4 + h // 2][:, (h % 2) * 2 * P + c * P:(h % 2) * 2 * P + c * P + P], v2[:, h, c * P:c * P + P], ident)
                pe_s.on(t)
                for h in range(GH):
                    t = T.transpose(bank[6][:, h * P:h * P + P], k2[:, h, 0:P], ident)
                pe_s.on(t)

            @block.vector
            def _(dve):
                for h in range(GH):
                    for c in range(2):
                        dve_s.on(V.tensor_scalar(Dm[:, 2 * h + c, :], gcB[:, h, c * P:c * P + P], cols[:, c, h:h + 1], 0.0,
                                                 ALU.subtract, ALU.min))
                for h in range(GH):
                    dve_s.on(V.tensor_tensor(tail_f[:, h:h + 1], gcB[:, h, P - 1:P], cols[:, 0, h:h + 1], ALU.subtract))

            @block.scalar
            def _(act):
                act.wait_ge(dve_s.sem, dve_s.value)
                act_s.on(S.activation(Dm, Dm, ACT.Exp))
                act_s.on(S.activation(eg, mats(gcB), ACT.Exp))
                act_s.on(S.activation(tail_f, tail_f, ACT.Exp))
                act.wait_ge(pe_s.sem, pe0 + 5)
                for q in range(2):
                    act_s.on(S.activation(vtok[:, 4 * q:4 * q + 4, :], pair(bank[4 + q]), ACT.Copy))
                act.wait_ge(pe_s.sem, pe0 + 6)
                act.wait_ge(act_s.sem, act_s.value - 2)
                for h in range(GH):
                    act_s.on(S.activation(ktok[:, h, :], bank[6][:, h * P:h * P + P], ACT.Copy, scale=tail_f[:, h:h + 1]))

            @block.vector
            def _(dve):
                dve.wait_ge(act_s.sem, act0 + 1)
                n = dve_s.on(V.tensor_tensor(mats(beB), mats(beB), Dm, ALU.mult))
                dve.wait_ge(dve_s.sem, n)
                for h in range(GH):
                    dve.wait_ge(pe_s.sem, pe0 + h + 1)
                    b3 = bank[h][:, :].rearrange("p (c i t) -> p c i t", c=2, i=2)
                    s = slice(2 * h, 2 * h + 2)
                    dve_s.on(V.tensor_tensor(X2[:, s, :], b3[:, :, 0, :], mats(beB)[:, s, :], ALU.mult))
                    dve_s.on(V.tensor_tensor(AT[:, s, :], b3[:, :, 1, :], Dm[:, s, :], ALU.mult))
                dve.wait_ge(dve_s.sem, dve_s.value)
                dve_s.on(V.tensor_tensor(X2, X2, bc(upper_strict, 2 * GH), ALU.mult))
                marks["n2"] = dve_s.value
                dve_s.on(V.tensor_tensor(AT, AT, bc(upper_incl, 2 * GH), ALU.mult))
                dve.wait_ge(act_s.sem, act0 + 2)
                dve_s.on(V.tensor_tensor(kg, mats(k2), eg, ALU.mult))
                dve_s.on(V.tensor_tensor(qg, mats(q2), eg, ALU.mult))

            @block.tensor
            def _(pe):
                pe.wait_ge(dve_s.sem, marks["n2"])
                for q in range(2):
                    for i in range(4):
                        t = T.transpose(bank[q][:, i * P:i * P + P], X2[:, 4 * q + i, :], ident)
                    pe_s.on(t)

            @block.vector
            def _(dve):
                eye = bc(ident, 4)
                for q in range(2):
                    s = slice(4 * q, 4 * q + 4)
                    dve.wait_ge(pe_s.sem, pe_s.value - 1 + q)
                    dve_s.on(V.tensor_copy(L2[:, s, :], pair(bank[q])))
                    dve.wait_ge(dve_s.sem, dve_s.on(V.tensor_tensor(X2[:, s, :], X2[:, s, :], bc(upper[0], 4), ALU.mult)))
                    dve_s.on(V.tensor_tensor(X2[:, s, :], eye, X2[:, s, :], ALU.subtract))
                    dve.wait_ge(dve_s.sem, dve_s.on(V.tensor_tensor(Tm2[:, s, :], L2[:, s, :], bc(lower[0], 4), ALU.mult)))
                    dve_s.on(V.tensor_tensor(Tm2[:, s, :], eye, Tm2[:, s, :], ALU.subtract))

        triangular_inverse(L2, X2, Tm2, LM2, WW2, P, 4, 2, range(1, 7))

        vn = L2
        RR = Tm2[:, 0:4, :]
        S2 = Tm2[:, 4:8, :]
        oA = LM2[:, :, :, :].rearrange("p a b c -> p (a b) c")
        with nc.Block() as block:
            @block.vector
            def _(dve):
                for h in range(GH):
                    dve_s.on(V.tensor_scalar(RR[:, h, :], vtok[:, 2 * h, :], cols[:, 2, h:h + 1], None, ALU.mult))

            @block.tensor
            def _(pe):
                pe.wait_ge(dve_s.sem, dve_s.value)
                for h in range(GH):
                    mm = T.matmul(bank[0][:, h * P:h * P + P], X2[:, 2 * h, :], RR[:, h, :], start=True, stop=True)
                pe_s.on(mm)

            @block.scalar
            def _(act):
                act.wait_ge(pe_s.sem, pe_s.value)
                act_s.on(S.activation(vn[:, 0:4, :], pair(bank[0]), ACT.Copy))

            @block.tensor
            def _(pe):
                pe.wait_ge(act_s.sem, act_s.value)
                for h in range(GH):
                    mm = T.matmul(bank[1][:, h * P:h * P + P], ktok[:, h, :], vn[:, h, :], start=True, stop=True)
                pe_s.on(mm)
                for h in range(GH):
                    mm = T.matmul(bank[2][:, h * P:h * P + P], vn[:, h, :], AT[:, 2 * h, :], start=True, stop=True)
                pe_s.on(mm)

            @block.scalar
            def _(act):
                act.wait_ge(pe_s.sem, pe_s.value - 1)
                act_s.on(S.activation(S2, pair(bank[1]), ACT.Copy))

            @block.tensor
            def _(pe):
                pe.wait_ge(act_s.sem, act_s.value)
                for h in range(GH):
                    mm = T.matmul(bank[3][:, h * P:h * P + P], kg[:, 2 * h + 1, :], S2[:, h, :], start=True, stop=True)
                pe_s.on(mm)

            @block.vector
            def _(dve):
                dve.wait_ge(pe_s.sem, pe_s.value)
                vt = vtok.rearrange("p (h c) t -> p h c t", c=2)
                dve.wait_ge(dve_s.sem, dve_s.on(V.tensor_tensor(RR, vt[:, :, 1, :], pair(bank[3]), ALU.subtract)))
                for h in range(GH):
                    dve_s.on(V.tensor_scalar(RR[:, h, :], RR[:, h, :], cols[:, 3, h:h + 1], None, ALU.mult))

            @block.tensor
            def _(pe):
                pe.wait_ge(dve_s.sem, dve_s.value)
                for h in range(GH):
                    mm = T.matmul(bank[4][:, h * P:h * P + P], X2[:, 2 * h + 1, :], RR[:, h, :], start=True, stop=True)
                pe_s.on(mm)

            @block.scalar
            def _(act):
                act.wait_ge(pe_s.sem, pe_s.value)
                act_s.on(S.activation(vn[:, 4:8, :], pair(bank[4]), ACT.Copy))

            @block.tensor
            def _(pe):
                pe.wait_ge(act_s.sem, act_s.value)
                for h in range(GH):
                    T.matmul(bank[5][:, h * P:h * P + P], S2[:, h, :], qg[:, 2 * h + 1, :], start=True, stop=False)
                    mm = T.matmul(bank[5][:, h * P:h * P + P], vn[:, 4 + h, :], AT[:, 2 * h + 1, :], start=False, stop=True)
                pe_s.on(mm)

            @block.vector
            def _(dve):
                dve.wait_ge(pe_s.sem, pe_s.value)
                ov = oA.rearrange("p (h c) t -> p h c t", c=2)
                dve_s.on(V.tensor_copy(ov[:, :, 0, :], pair(bank[2])))
                dve_s.on(V.tensor_copy(ov[:, :, 1, :], pair(bank[5])))

        oAh = oA.rearrange("p (h c) t -> p h (c t)", c=2)
        two = lambda b: b[:, :].rearrange("p (a b) -> p a b", b=T2)

        def gated_norm(o, sq, norm, gate, gain, dst, per_head):
            with nc.Block() as block:
                @block.vector
                def _(dve):
                    dve_s.on(V.tensor_tensor(sq, o, o, ALU.mult))

                @block.tensor
                def _(pe):
                    pe.wait_ge(dve_s.sem, dve_s.value)
                    for h in range(GH):
                        if per_head:
                            mm = T.matmul(bank[h // 2][:, (h % 2) * T2:(h % 2) * T2 + T2], ones, sq[:, h, :], start=True, stop=True)
                        else:
                            mm = T.matmul(bank[0][:, 0:T2], ones, sq[:, h, :], start=(h == 0), stop=(h == GH - 1))
                    pe_s.on(mm)

                @block.scalar
                def _(act):
                    act_s.on(S.activation(dst, gate, ACT.Sigmoid))
                    act.wait_ge(pe_s.sem, pe_s.value)
                    if per_head:
                        for q in range(2):
                            act_s.on(S.activation(norm[:, 2 * q:2 * q + 2, :], two(bank[q]), ACT.Sqrt, bias=eps_rms, scale=1.0 / P))
                    else:
                        act_s.on(S.activation(norm[:, 0, :], bank[0][:, 0:T2], ACT.Sqrt, bias=eps_rms, scale=1.0 / C))

                @block.vector
                def _(dve):
                    n = GH if per_head else 1
                    dve.wait_ge(act_s.sem, act_s.value)
                    dve.wait_ge(dve_s.sem, dve_s.on(V.reciprocal(norm[:, 0:n, :], norm[:, 0:n, :])))
                    for h in range(GH):
                        dve_s.on(V.scalar_tensor_tensor(out=sq[:, h, :], in0=o[:, h, :], scalar=gain(h), in1=norm[:, h if per_head else 0, :],
                                                        op0=ALU.mult, op1=ALU.mult))
                    dve.wait_ge(dve_s.sem, dve_s.on(V.tensor_tensor(dst, dst, gate, ALU.mult)))
                    dve_s.on(V.tensor_tensor(dst, dst, sq, ALU.mult))

        gated_norm(oAh, WW2.rearrange("p a b c -> p (a b c)").rearrange("p (h t) -> p h t", h=GH), gcB, gate_a,
                   lambda h: param("gdn_norm_w_2"), o_all[:, 0:GH, :], True)

        mh = Memory(m2.tensor, 0, MIX2)
        logf, kB = mh.take(GH, T2), mh.take(GH, T2)
        bcum, sgm = mh.take(GH, T2), mh.take(GH, T2)
        E = [mh.take(GH * T2) for _ in range(2)]
        Qb = [mh.take(GH * T2) for _ in range(2)]
        Kb = [mh.take(GH * T2) for _ in range(2)]
        acc = mh.take(2 * GH, P)
        masked = mh.take(2 * GH, P)
        low2 = Memory(second_kept, 0, KD * T2 + 12 * (3 + T2))
        cross = low2.take(GH, P)
        itok = low2.take(2 * GH, P)
        oB = low2.take(GH, T2)
        wsq = low2.take(GH, T2)
        flat = lambda ap: ap.rearrange("p h t -> p (h t)")
        with nc.Block() as block:
            @block.scalar
            def _(act):
                act_s.on(S.activation(sgm, f_b, ACT.Sigmoid))
                act_s.on(S.activation(kB, f_b, ACT.Sigmoid, scale=-1.0))
                act_s.on(S.activation(acc, mats(q_b), ACT.Sigmoid))

            @block.gpsimd
            def _(pool):
                for ap in Qb + Kb:
                    pool.wait_ge(pool_s.sem, pool_s.on(G.memset(ap, 0.0)))

            @block.vector
            def _(dve):
                dve.wait_ge(act_s.sem, act_s.value)
                for h in range(GH):
                    dve_s.on(V.tensor_scalar(sgm[:, h, :], sgm[:, h, :], lb1[:, h:h + 1], lb[:, h:h + 1], ALU.mult, ALU.add))
                marks["f"] = dve_s.value
                for h in range(GH):
                    dve_s.on(V.tensor_scalar(kB[:, h, :], kB[:, h, :], lb1[:, h:h + 1], None, ALU.mult))
                dve_s.on(V.tensor_tensor(mats(q_b), mats(q_b), acc, ALU.mult))

            @block.scalar
            def _(act):
                act.wait_ge(dve_s.sem, marks["f"])
                act_s.on(S.activation(logf, sgm, ACT.Ln))

            @block.vector
            def _(dve):
                dve.wait_ge(act_s.sem, act_s.value)
                for h in range(GH):
                    dve_s.on(V.tensor_tensor_scan(bcum[:, h, :], reset128, logf[:, h, :], 0.0, ALU.mult, ALU.add))

            @block.tensor
            def _(pe):
                for h in range(GH):
                    for c in range(2):
                        t = T.transpose(bank[6 + h // 2][:, (h % 2) * 2 * P + c * P:(h % 2) * 2 * P + c * P + P], i_b[:, h, c * P:c * P + P], ident)
                pe_s.on(t)

            @block.scalar
            def _(act):
                act.wait_ge(pe_s.sem, pe_s.value)
                for q in range(2):
                    act_s.on(S.activation(itok[:, 4 * q:4 * q + 4, :], pair(bank[6 + q]), ACT.Copy))

        s_e = Signal(nc, ctx, "level_exponents")
        s_ee = Signal(nc, ctx, "level_decays")
        s_qk = Signal(nc, ctx, "level_operands")
        s_a = Signal(nc, ctx, "level_products")
        s_m = Signal(nc, ctx, "level_masked")
        s_acc = Signal(nc, ctx, "level_added")
        with nc.Block() as block:
            @block.vector
            def _(dve):
                def exponents(n):
                    b = 1 << n
                    v = flat(bcum).rearrange("p (k i t) -> p k i t", i=2, t=b)
                    e = E[n % 2].rearrange("p (k i t) -> p k i t", i=2, t=b)
                    ref = v[:, :, 0, b - 1:b].broadcast_to([P, GH * T2 // (2 * b), b])
                    if n >= 2:
                        dve.wait_ge(s_qk.sem, 2 * (n - 1))
                    s_e.on(V.tensor_tensor(e[:, :, 1, :], v[:, :, 1, :], ref, ALU.subtract))
                    s_e.on(V.tensor_tensor(e[:, :, 0, :], ref, v[:, :, 0, :], ALU.subtract))

                def operands(n):
                    b = 1 << n
                    sh_ = lambda ap: ap.rearrange("p (k i t) -> p k i t", i=2, t=b)
                    dve.wait_ge(s_ee.sem, n + 1)
                    if n >= 2:
                        dve.wait_ge(s_a.sem, n)
                    s_qk.on(V.tensor_tensor(sh_(Qb[n % 2])[:, :, 1, :], sh_(flat(q_b))[:, :, 1, :], sh_(E[n % 2])[:, :, 1, :], ALU.mult))
                    s_qk.on(V.tensor_tensor(sh_(Kb[n % 2])[:, :, 0, :], sh_(flat(kB))[:, :, 0, :], sh_(E[n % 2])[:, :, 0, :], ALU.mult))

                def mask(i):
                    u = ident if i == 0 else upper[i - 1]
                    dve.wait_ge(s_a.sem, i + 1)
                    b0 = (i % 2) * 2
                    dst = acc if i == 0 else masked
                    if i >= 2:
                        dve.wait_ge(s_acc.sem, i - 1)
                    s_m.on(V.tensor_tensor(dst[:, 0:4, :], pair(bank[b0]), bc(u, 4), ALU.mult))
                    s_m.on(V.tensor_tensor(dst[:, 4:8, :], pair(bank[b0 + 1]), bc(u, 4), ALU.mult))

                exponents(0)
                for n in range(7):
                    if n + 1 < 7:
                        exponents(n + 1)
                    operands(n)
                    mask(n)
                mask(7)
                dve.wait_ge(s_qk.sem, 14)
                last = bcum[:, :, P - 1:P].broadcast_to([P, GH, P])
                ex = E[0][:, 0:GH * P].rearrange("p (h t) -> p h t", h=GH)
                s_e.on(V.tensor_tensor(ex, last, bcum[:, :, 0:P], ALU.subtract))
                dve.wait_ge(s_ee.sem, 9)
                dve.wait_ge(s_a.sem, 8)
                s_qk.on(V.tensor_tensor(Kb[0][:, 0:GH * P].rearrange("p (h t) -> p h t", h=GH), kB[:, :, 0:P], ex, ALU.mult))
                s_qk.on(V.tensor_tensor(Qb[0][:, 0:GH * P].rearrange("p (h t) -> p h t", h=GH), q_b[:, :, P:T2],
                                        E[0][:, GH * P:2 * GH * P].rearrange("p (h t) -> p h t", h=GH), ALU.mult))
                dve.wait_ge(s_a.sem, 9)
                s_m.on(V.tensor_copy(cross, pair(bank[4])))

            @block.scalar
            def _(act):
                for n in range(7):
                    act.wait_ge(s_e.sem, 2 * n + 2)
                    s_ee.on(S.activation(E[n % 2], E[n % 2], ACT.Exp))
                act.wait_ge(s_qk.sem, 14)
                s_ee.on(S.activation(E[0][:, GH * P:2 * GH * P].rearrange("p (h t) -> p h t", h=GH), bcum[:, :, P:T2], ACT.Exp))
                act.wait_ge(s_e.sem, 15)
                s_ee.on(S.activation(E[0][:, 0:GH * P], E[0][:, 0:GH * P], ACT.Exp))

            @block.gpsimd
            def _(pool):
                for i in range(1, 8):
                    pool.wait_ge(s_m.sem, 2 * i + 2)
                    if i >= 2:
                        pool.wait_ge(s_acc.sem, i - 1)
                    s_acc.on(G.tensor_tensor(acc, acc, masked, ALU.add))

            @block.tensor
            def _(pe):
                for i in range(8):
                    if i:
                        pe.wait_ge(s_qk.sem, 2 * i)
                    if i >= 2:
                        pe.wait_ge(s_m.sem, 2 * (i - 1))
                    for m in range(2 * GH):
                        k_, q_ = ((flat(kB), flat(q_b)) if i == 0 else (Kb[(i - 1) % 2], Qb[(i - 1) % 2]))
                        mm = T.matmul(bank[(i % 2) * 2 + m // 4][:, (m % 4) * P:(m % 4) * P + P], k_[:, m * P:m * P + P],
                                      q_[:, m * P:m * P + P], start=True, stop=True)
                    s_a.on(mm)
                pe.wait_ge(s_qk.sem, 16)
                for h in range(GH):
                    mm = T.matmul(bank[4][:, h * P:h * P + P], Kb[0][:, h * P:h * P + P], Qb[0][:, h * P:h * P + P],
                                  start=True, stop=True)
                s_a.on(mm)
                pe.wait_ge(s_acc.sem, 7)
                pe.wait_ge(s_m.sem, 17)
                for h in range(GH):
                    o = (h % 2) * T2
                    T.matmul(bank[6 + h // 2][:, o:o + P], itok[:, 2 * h, :], acc[:, 2 * h, :], start=True, stop=True)
                    T.matmul(bank[6 + h // 2][:, o + P:o + T2], itok[:, 2 * h, :], cross[:, h, :], start=True, stop=False)
                    mm = T.matmul(bank[6 + h // 2][:, o + P:o + T2], itok[:, 2 * h + 1, :], acc[:, 2 * h + 1, :], start=False, stop=True)
                s_a.on(mm)

            @block.scalar
            def _(act):
                act.wait_ge(s_a.sem, 10)
                for q in range(2):
                    act_s.on(S.activation(oB[:, 2 * q:2 * q + 2, :], two(bank[6 + q]), ACT.Copy))
        gated_norm(oB, wsq, E[0].rearrange("p (h t) -> p h t", h=GH), gate_b, lambda h: param("hg_norm_w_2", h),
                   o_all[:, GH:2 * GH, :], False)

        def mixer_out(engine, m, psum):
            return V.scalar_tensor_tensor(out=xT[:, m, :], in0=psum, scalar=mod[:, 2 * KD + m:2 * KD + m + 1], in1=xT[:, m, :],
                                          op0=ALU.mult, op1=ALU.add)
        mixer_stack.close()
        with ExitStack() as stack:
            project([o_all], T2, [(W_OUT2 + m // 4, (m % 4) * P, P, 0) for m in range(KD)], mixer_out, W_OUT2, 2,
                    split_memory(stack, "out2_", KD, T2), owner=lambda m: "dve")
        arena.close()
        ring_stack.close()
        raw_w = ctx.enter_context(nc.sbuf_tensor("raw_weights", [P, RAW, PIECE], F32))
        w_hi = [ctx.enter_context(nc.sbuf_tensor(f"weights_hi{t}", [P, PIECE], F32R)) for t in range(3)]
        w_lo = [ctx.enter_context(nc.sbuf_tensor(f"weights_lo{t}", [P, PIECE], F32R)) for t in range(3)]
        x_hi = ctx.enter_context(nc.sbuf_tensor("x_hi", [P, KD, T2], F32R))
        x_lo = ctx.enter_context(nc.sbuf_tensor("x_lo", [P, KD, T2], F32R))
        hid_hi = ctx.enter_context(nc.sbuf_tensor("hidden_hi", [P, 2, T2], F32R))
        hid_lo = ctx.enter_context(nc.sbuf_tensor("hidden_lo", [P, 2, T2], F32R))
        rest = ctx.enter_context(nc.sbuf_tensor("moe_memory", [P, 10752], F32))
        raw_ready = [Signal(nc, ctx, f"piece_ready{i}") for i in range(RAW)]
        row_ready = [Signal(nc, ctx, f"router_row_ready{i}") for i in range(GROWS)]
        s_gates = Signal(nc, ctx, "gates_stored")
        mm_ = Memory(rest, 0, 10752)
        hB = mm_.take(KD, T2)
        wr = mm_.take(KD, NE)
        scores, sel, rep, tmp64 = (mm_.take(2, NE) for _ in range(4))
        top8 = mm_.take(2, 8, 8)
        gsum, rank = mm_.take(2, 8), mm_.take(2, 8)
        cmp, eqm = mm_.take(2, 8, 8), mm_.take(2, 8, 8)
        total_w = mm_.take(2)
        gatesT = mm_.take(T2)
        gb = mm_.take(GROWS, T2)
        esig = mm_.take(2, 2 * T2)
        eprod = mm_.take(2 * T2)
        hid = mm_.take(2 * T2)
        rs2 = mm_.take(T2)
        zero = mm_.take(512)
        y_tok = mm_.take(2, D)
        sq2 = y_tok.rearrange("p c (j t) -> p (c j) t", t=T2)
        routed = (a["w_gate_2"][0], a["w_up_2"][0], a["w_down_2"][0])
        shared = (a["ws_gate_2"][0], a["ws_up_2"][0], a["ws_down_2"][0])

        def piece_view(ap, t):
            return ap.rearrange("p (k c) -> p k c", c=(FE, FE, D)[t])

        def load_piece(sp, r, t, source):
            sp.dma_start(piece_view(raw_w[:, r, :], t), source.rearrange("(k p) c -> p k c", p=P)).then_inc(raw_ready[r].sem, 16)

        def load_row(sp, q, row):
            sp.dma_start(gb[:, q, :], row.partition_broadcast(P)).then_inc(row_ready[q].sem, 16)

        with nc.Block() as block:
            @block.sync
            def _(sp):
                small_in.on(sp.dma_start(wr, a["w_router_2"][0].rearrange("(k p) e -> p k e", p=P)), 16)
                for t in range(3):
                    load_piece(sp, t, t, shared[t])
                for t in range(3):
                    load_piece(sp, 3 + t, t, routed[t][0])
        rms_norm(xT, hB, lambda j: gain2[:, j:j + 1], lambda j: mod[:, 3 * KD + j:3 * KD + j + 1], T2, sq2, rs2)
        lt8 = small[:, 192:256].rearrange("p (g j) -> p g j", j=8)
        with nc.Block() as block:
            @block.gpsimd
            def _(pool):
                pool.wait_ge(pool_s.sem, pool_s.on(G.memset(lt8, 1.0)))
                pool_s.on(G.affine_select(out=lt8, in_=lt8, compare_op=ALU.is_gt, fill=0.0, base=0,
                                          pattern=[[1, 8], [-1, 8]], channel_multiplier=0))

            @block.tensor
            def _(pe):
                pe.wait_ge(small_in.sem, small_in.value)
                for c in range(2):
                    for k in range(KD):
                        mm = T.matmul(bank[4][:, c * NE:c * NE + NE], hB[:, k, c * P:c * P + P], wr[:, k, :],
                                      start=(k == 0), stop=(k == KD - 1))
                pe_s.on(mm)

            @block.scalar
            def _(act):
                act.wait_ge(pe_s.sem, pe_s.value)
                act_s.on(S.activation(scores, bank[4][:, 0:2 * NE].rearrange("p (a b) -> p a b", b=NE), ACT.Sigmoid))

            @block.vector
            def _(dve):
                def step(instruction):
                    dve.wait_ge(dve_s.sem, dve_s.on(instruction))
                dve.wait_ge(act_s.sem, act_s.value)
                step(V.tensor_tensor(sel, scores, bc(small[:, 128:192], 2), ALU.add))
                for c in range(2):
                    for g in range(8):
                        last = V.max(top8[:, c, g, :], sel[:, c, 8 * g:8 * g + 8])
                        dve_s.on(last)
                dve.wait_ge(dve_s.sem, dve_s.value)
                step(V.tensor_tensor(gsum, top8[:, :, :, 0], top8[:, :, :, 1], ALU.add))
                for c in range(2):
                    mine = gsum[:, c, :].unsqueeze(2).broadcast_to([P, 8, 8])
                    other = gsum[:, c, :].unsqueeze(1).broadcast_to([P, 8, 8])
                    dve_s.on(V.tensor_tensor(cmp[:, c], other, mine, ALU.is_gt))
                    dve_s.on(V.tensor_tensor(eqm[:, c], other, mine, ALU.is_equal))
                dve.wait_ge(dve_s.sem, dve_s.value)
                dve.wait_ge(pool_s.sem, pool_s.value)
                for c in range(2):
                    dve_s.on(V.tensor_tensor(eqm[:, c], eqm[:, c], lt8, ALU.mult))
                dve.wait_ge(dve_s.sem, dve_s.value)
                step(V.tensor_tensor(cmp, cmp, eqm, ALU.add))
                step(V.tensor_reduce(rank, cmp, AX.X, ALU.add))
                step(V.tensor_scalar(rank, rank, 4.0, None, ALU.is_lt))
                for c in range(2):
                    grp = rank[:, c, :].unsqueeze(2).broadcast_to([P, 8, 8])
                    g8 = lambda ap: ap[:, c, :].rearrange("p (g e) -> p g e", e=8)
                    step(V.tensor_tensor(g8(sel), g8(sel), grp, ALU.mult))
                    step(V.tensor_scalar(g8(tmp64), grp, 1.0, -NEG, ALU.subtract, ALU.mult))
                    step(V.tensor_tensor(g8(sel), g8(sel), g8(tmp64), ALU.add))
                    step(V.max(top8[:, c, 0, :], sel[:, c, :]))
                    step(V.match_replace(out=rep[:, c, :], in_to_replace=top8[:, c, 0, :], in_values=sel[:, c, :], imm_value=-3e38))
                step(V.tensor_tensor(rep, rep, sel, ALU.not_equal))
                step(V.tensor_tensor(scores, scores, rep, ALU.mult))
                step(V.tensor_reduce(total_w, scores, AX.X, ALU.add))
                step(V.reciprocal(total_w, total_w))
                for c in range(2):
                    step(V.tensor_scalar(scores[:, c, :], scores[:, c, :], total_w[:, c:c + 1], 2.5, ALU.mult, ALU.mult))

            @block.tensor
            def _(pe):
                pe.wait_ge(dve_s.sem, dve_s.value)
                for c in range(2):
                    t = T.transpose(bank[5][0:NE, c * P:c * P + P], scores[:, c, :], ident)
                pe_s.on(t)

            @block.gpsimd
            def _(pool):
                G.memset(gb[:, 0, :], 1.0).then_inc(row_ready[0].sem, 16)

            @block.scalar
            def _(act):
                act_s.on(S.activation(x_hi[:, :, :], hB, ACT.Copy))

            @block.vector
            def _(dve):
                dve.wait_ge(act_s.sem, act_s.value)
                dve_s.on(V.tensor_tensor(x_lo[:, :, :], hB, x_hi[:, :, :].bitcast(F32), ALU.subtract))
                dve.wait_ge(pe_s.sem, pe_s.value)
                dve_s.on(V.tensor_copy(gatesT[0:NE, :], bank[5][0:NE, 0:T2]))
                dve_s.on(V.memset(zero, 0.0))

            @block.sync
            def _(sp):
                sp.wait_ge(dve_s.sem, dve_s.value - 1)
                s_gates.on(sp.dma_start(gates_dram, gatesT[0:NE, :]), 16)
                sp.wait_ge(s_gates.sem, 16)
                for n in range(1, GROWS):
                    load_row(sp, n, gates_dram[n - 1])

        s_hi = [Signal(nc, ctx, f"hi_ready{t}") for t in range(3)]
        s_lo = [Signal(nc, ctx, f"lo_ready{t}") for t in range(3)]
        s_gate = Signal(nc, ctx, "expert_gate")
        s_up = Signal(nc, ctx, "expert_up")
        s_down = Signal(nc, ctx, "expert_down")
        s_esig = Signal(nc, ctx, "expert_sigmoid")
        s_mul = Signal(nc, ctx, "expert_first_product")
        s_read = Signal(nc, ctx, "expert_banks_read")
        s_ehid = Signal(nc, ctx, "expert_hidden")
        s_hhi = Signal(nc, ctx, "hidden_hi_ready")
        s_hlo = Signal(nc, ctx, "hidden_lo_ready")
        LAST = NE
        with nc.Block() as block:
            @block.sync
            def _(sp):
                def load(n, q, row=True):
                    for t in range(3):
                        sp.wait_ge(s_lo[t].sem, n - 1)
                        load_piece(sp, (3 * q + t) % RAW, t, routed[t][n - 1])
                    if row:
                        sp.wait_ge(s_ehid.sem, n - 1)
                        load_row(sp, (q + 2) % GROWS, gates_dram[n + 1])
                with sp.Fori(0, 15) as i:
                    for q in range(2, 6):
                        load(i * 4 + q, q)
                load(62, 62)
                load(63, 63, False)
                load(64, 64, False)

            @block.tensor
            def _(pe):
                def halves(t):
                    return piece_view(w_hi[t][:, :], t), piece_view(w_lo[t][:, :], t)

                def product(t, par, n):
                    pe.wait_ge(s_lo[t].sem, n + 1)
                    if t == 0:
                        pe.wait_ge(s_read.sem, n + 1)
                    hi, lo = halves(t)
                    for f in range(2):
                        out_ = bank[4 + 2 * par + t][:, f * T2:f * T2 + T2]
                        cut = slice(f * P, f * P + P)
                        for d in range(KD):
                            T.matmul(out_, hi[:, d, cut], x_hi[:, d, :], start=(d == 0), stop=False)
                            T.matmul(out_, hi[:, d, cut], x_lo[:, d, :], start=False, stop=False)
                            mm = T.matmul(out_, lo[:, d, cut], x_hi[:, d, :], start=False, stop=(d == KD - 1))
                    mm.then_inc((s_gate, s_up)[t].sem, 1)

                def down(n):
                    pe.wait_ge(s_lo[2].sem, n + 1)
                    pe.wait_ge(s_hlo.sem, n + 1)
                    hi, lo = halves(2)
                    for d in range(KD):
                        out_ = bank[d // 2][:, (d % 2) * T2:(d % 2) * T2 + T2]
                        cut = slice(d * P, d * P + P)
                        for f in range(2):
                            for w, h in ((hi, hid_hi), (hi, hid_lo), (lo, hid_hi)):
                                mm = T.matmul(out_, w[:, f, cut], h[:, f, :], start=False, stop=False, skip_group_check=True)
                    mm.then_inc(s_down.sem, 1)

                for b in range(4):
                    mm = T.matmul(bank[b][:, :], ident, zero, start=True, stop=False, skip_group_check=True)
                mm.then_inc(s_down.sem, 1)
                product(0, 0, 0)
                product(1, 0, 0)
                with pe.Fori(0, NE // 4) as i:
                    for q in range(4):
                        product(0, (q + 1) % 2, i * 4 + (q + 1))
                        product(1, (q + 1) % 2, i * 4 + (q + 1))
                        down(i * 4 + q)
                down(LAST)

            @block.scalar
            def _(act):
                def cut(t, q, n, arrived):
                    r = (3 * q + t) % RAW
                    act.wait_ge(raw_ready[r].sem, arrived)
                    S.activation(w_hi[t][:, :], raw_w[:, r, :], ACT.Copy).then_inc(s_hi[t].sem, 1)

                def sigmoid(par, n):
                    act.wait_ge(s_gate.sem, n + 1)
                    act.wait_ge(s_read.sem, n + 1)
                    S.activation(esig[:, par, :], bank[4 + 2 * par][:, :], ACT.Sigmoid).then_inc(s_esig.sem, 1)

                def hidden_hi(n):
                    act.wait_ge(s_ehid.sem, n + 1)
                    act.wait_ge(s_down.sem, n + 1)
                    S.activation(hid_hi[:, :, :].rearrange("p f t -> p (f t)"), hid, ACT.Copy).then_inc(s_hhi.sem, 1)

                def expert(q, n, arrived, next_arrived):
                    sigmoid(q % 2, n)
                    cut(0, q + 1, n + 1, next_arrived)
                    act.wait_ge(s_up.sem, n + 1)
                    cut(1, q + 1, n + 1, next_arrived)
                    hidden_hi(n)
                    cut(2, q, n, arrived)
                cut(0, 0, 0, 16)
                cut(1, 0, 0, 16)
                with act.Fori(0, NE // 4) as i:
                    for q in range(4):
                        expert(q, i * 4 + q, i * 32 + 16 * (q // 2 + 1), i * 32 + 16 * ((q + 1) // 2 + 1))
                sigmoid(0, LAST)
                hidden_hi(LAST)
                cut(2, 0, LAST, 16 * (LAST // 2 + 1))

            @block.vector
            def _(dve):
                def rest_of(t, q, n):
                    dve.wait_ge(s_hi[t].sem, n + 1)
                    V.tensor_tensor(w_lo[t][:, :], raw_w[:, (3 * q + t) % RAW, :], w_hi[t][:, :].bitcast(F32),
                                    ALU.subtract).then_inc(s_lo[t].sem, 1)

                def hidden(par, n, q, row):
                    dve.wait_ge(s_esig.sem, n + 1)
                    V.tensor_tensor(eprod, bank[4 + 2 * par][:, :], esig[:, par, :], ALU.mult).then_inc(s_mul.sem, 1)
                    dve.wait_ge(s_mul.sem, n + 1)
                    dve.wait_ge(s_up.sem, n + 1)
                    V.tensor_tensor(eprod, eprod, bank[5 + 2 * par][:, :], ALU.mult).then_inc(s_read.sem, 1)
                    dve.wait_ge(s_read.sem, n + 3)
                    dve.wait_ge(row_ready[q % GROWS].sem, row)
                    V.tensor_tensor(hid.rearrange("p (f t) -> p f t", f=2), eprod.rearrange("p (f t) -> p f t", f=2),
                                    gb[:, q % GROWS, :].unsqueeze(1).broadcast_to([P, 2, T2]), ALU.mult).then_inc(s_ehid.sem, 1)

                def hidden_lo(n):
                    dve.wait_ge(s_hhi.sem, n + 1)
                    V.tensor_tensor(hid_lo[:, :, :].rearrange("p f t -> p (f t)"), hid,
                                    hid_hi[:, :, :].rearrange("p f t -> p (f t)").bitcast(F32), ALU.subtract).then_inc(s_hlo.sem, 1)
                V.memset(eprod[:, 0:1], 0.0).then_inc(s_read.sem, 2)
                dve.wait_ge(s_read.sem, 2)
                rest_of(0, 0, 0)
                rest_of(1, 0, 0)
                with dve.Fori(0, NE // 4) as i:
                    for q in range(4):
                        n = i * 4 + q
                        rest_of(0, q + 1, n + 1)
                        hidden(q % 2, n, q, i * 16 + 16)
                        rest_of(1, q + 1, n + 1)
                        hidden_lo(n)
                        rest_of(2, q, n)
                hidden(0, LAST, 0, 16 * (LAST // 4 + 1))
                hidden_lo(LAST)
                rest_of(2, 0, LAST)

        with nc.Block() as block:
            @block.vector
            def _(dve):
                for m in range(KD):
                    dve_s.on(V.scalar_tensor_tensor(out=xT[:, m, :], in0=bank[m // 2][:, (m % 2) * T2:(m % 2) * T2 + T2],
                                                    scalar=mod[:, 5 * KD + m:5 * KD + m + 1], in1=xT[:, m, :],
                                                    op0=ALU.mult, op1=ALU.add))
        rms_norm(xT, hB, lambda j: param("final_norm_w_2", j), None, T2, sq2, rs2)
        with nc.Block() as block:
            pe0 = pe_s.value

            @block.tensor
            def _(pe):
                for c in range(2):
                    for half in range(2):
                        for j in range(4):
                            t = T.transpose(bank[2 * c + half][:, j * P:j * P + P], hB[:, 4 * half + j, c * P:c * P + P], ident)
                        pe_s.on(t)

            @block.vector
            def _(dve):
                for i in range(0, 4, 2):
                    dve.wait_ge(pe_s.sem, pe0 + i + 1)
                    dve_s.on(V.tensor_copy(y_tok[:, i // 2, 0:512], bank[i][:, :]))

            @block.scalar
            def _(act):
                for i in range(1, 4, 2):
                    act.wait_ge(pe_s.sem, pe0 + i + 1)
                    act_s.on(S.activation(y_tok[:, i // 2, 512:D], bank[i][:, :], ACT.Copy))

            @block.sync
            def _(sp):
                for c in range(2):
                    sp.wait_ge(dve_s.sem, dve_s.value - 1 + c)
                    sp.wait_ge(act_s.sem, act_s.value - 1 + c)
                    stored.on(sp.dma_start(out[0, c * P:c * P + P, :], y_tok[:, c, :]), 16)
                sp.wait_ge(stored.sem, stored.value)


INPUTS = ["x", "meta_tokens", "norm_mix", "norm_ffn", "norm_final", "w_in", "mu_rw", "w0", "w_up", "a0", "a_up",
          "g_up", "k_k", "k_a", "r_k", "ln_x_w", "ln_x_b", "w_sb_out", "w_rw_out", "w_out", "w_ffn_in",
          "w_ffn_out", "c_2", "w_ada_2", "b_ada_2", "norm1_w_2", "w_in_2", "conv_w_2", "gdn_a_log_2",
          "gdn_dt_bias_2", "gdn_norm_w_2", "hg_lb_2", "hg_norm_w_2", "w_out_2", "norm2_w_2", "w_router_2",
          "router_bias_2", "w_gate_2", "w_up_2", "w_down_2", "ws_gate_2", "ws_up_2", "ws_down_2",
          "final_norm_w_2"]


def kernel(**inputs):
    import concourse.bacc as bacc
    from concourse.bass_utils import run_bass_kernel_spmd

    nc = bacc.Bacc("TRN2", target_bir_lowering=False, num_devices=1)
    arrays, aps = {}, {}
    for name in INPUTS:
        array = np.ascontiguousarray(inputs[name])
        arrays[f"in_{name}"] = array
        aps[name] = nc.dram_tensor(f"in_{name}", array.shape, mybir.dt.from_np(array.dtype), kind="ExternalInput").ap()
    out = nc.dram_tensor("out", (1, SEQ, D), F32, kind="ExternalOutput").ap()
    build(nc, aps, out)
    result = run_bass_kernel_spmd(nc, [arrays], core_ids=[0])
    return result.results[0]["out"]
```
